# Optimizing a Trainium2 kernel written in Bass

```python
import jax, jax.numpy as jnp
from jax import lax
import numpy as np
import jax
import jax.numpy as jnp

D_MODEL = 1024
BATCH = 1
SEQ = 256
DEPTH = 1

LRU_WIDTH = 1024
LRU_BLOCKS = 16
LRU_BLOCK_W = LRU_WIDTH // LRU_BLOCKS
CONV_WIDTH = 4
LRU_C = 8.0
HEAD_DIM = 64
N_Q_HEADS = 16
N_KV_HEADS = 4
Q_PER_KV = N_Q_HEADS // N_KV_HEADS
ATTN_WIDTH = N_Q_HEADS * HEAD_DIM
KV_WIDTH = N_KV_HEADS * HEAD_DIM
WINDOW = 128
BLOCK = 128
ROPE_THETA = 10000.0
D_FF = 2816
MACARON_SCALE = 0.5
NORM_EPS = 1e-6
MASK_VALUE = -1e30
IN_WIDTH = 2 * LRU_WIDTH + ATTN_WIDTH + 2 * KV_WIDTH + 2 * D_MODEL
IN_SPLITS = (
    LRU_WIDTH,
    2 * LRU_WIDTH,
    2 * LRU_WIDTH + ATTN_WIDTH,
    2 * LRU_WIDTH + ATTN_WIDTH + KV_WIDTH,
    2 * LRU_WIDTH + ATTN_WIDTH + 2 * KV_WIDTH,
    2 * LRU_WIDTH + ATTN_WIDTH + 2 * KV_WIDTH + D_MODEL,
)


def rms_norm(x, g):
    xf = x.astype(jnp.float32)
    y = xf * lax.rsqrt(jnp.mean(xf * xf, axis=-1, keepdims=True) + NORM_EPS)
    return (y * g.astype(jnp.float32)).astype(x.dtype)

def swiglu(x, w_gu, w_down):
    g, u = jnp.split(x @ w_gu, 2, axis=-1)
    return (jax.nn.silu(g) * u) @ w_down

def rope_tables(seq_len):
    half = HEAD_DIM // 2
    inv_freq = ROPE_THETA ** (-jnp.arange(half, dtype=jnp.float32) / half)
    ang = jnp.arange(seq_len, dtype=jnp.float32)[:, None] * inv_freq[None, :]
    return jnp.cos(ang), jnp.sin(ang)

def apply_rope(x, cos, sin):
    half = HEAD_DIM // 2
    xf = x.astype(jnp.float32)
    x1, x2 = xf[..., :half], xf[..., half:]
    c = cos[None, :, None, :]
    s = sin[None, :, None, :]
    return jnp.concatenate([x1 * c - x2 * s, x2 * c + x1 * s], axis=-1).astype(x.dtype)

def causal_depthwise_conv(x, w, b):
    s = x.shape[1]
    xp = jnp.pad(x, ((0, 0), (CONV_WIDTH - 1, 0), (0, 0)))
    y = xp[:, 0:s] * w[0]
    for k in range(1, CONV_WIDTH):
        y = y + xp[:, k:k + s] * w[k]
    return y + b

def block_diag_linear(x, w, b):
    bsz, s, _ = x.shape
    xb = x.reshape(bsz, s, LRU_BLOCKS, LRU_BLOCK_W)
    y = jnp.einsum('bsnc,ncd->bsnd', xb, w).reshape(bsz, s, LRU_WIDTH)
    return y + b

def rg_lru(x, w_a, b_a, w_x, b_x, lam):
    xf = x.astype(jnp.float32)
    r = jax.nn.sigmoid(block_diag_linear(x, w_a, b_a).astype(jnp.float32))
    i = jax.nn.sigmoid(block_diag_linear(x, w_x, b_x).astype(jnp.float32))
    log_a = -LRU_C * r * jax.nn.softplus(-lam.astype(jnp.float32))
    a = jnp.exp(log_a)
    mult = jnp.sqrt(jnp.maximum(-jnp.expm1(2.0 * log_a), 0.0))
    bterm = mult * (i * xf)

    def combine(left, right):
        a1, b1 = left
        a2, b2 = right
        return a1 * a2, a2 * b1 + b2

    _, h = lax.associative_scan(combine, (a, bterm), axis=1)
    return h.astype(x.dtype)

def band_blocks(t):
    bsz, s, h, d = t.shape
    tb = t.reshape(bsz, s // BLOCK, BLOCK, h, d)
    prev = jnp.pad(tb, ((0, 0), (1, 0), (0, 0), (0, 0), (0, 0)))[:, :-1]
    return jnp.concatenate([prev, tb], axis=2)

def sliding_window_attention_with_sinks(q, k, v, sinks):
    bsz, s = q.shape[0], q.shape[1]
    nb = s // BLOCK
    qb = q.reshape(bsz, nb, BLOCK, N_KV_HEADS, Q_PER_KV, HEAD_DIM)
    kb = band_blocks(k)
    vb = band_blocks(v)
    scores = jnp.einsum('bnqhgd,bnshd->bhgnqs', qb, kb).astype(jnp.float32) * (HEAD_DIM ** -0.5)
    qi = jnp.arange(BLOCK)[:, None]
    si = jnp.arange(2 * BLOCK)[None, :]
    diff = BLOCK + qi - si
    key_pos = (jnp.arange(nb)[:, None, None] - 1) * BLOCK + si[None]
    mask = ((diff >= 0) & (diff < WINDOW))[None] & (key_pos >= 0)
    scores = jnp.where(mask, scores, MASK_VALUE)
    sink = sinks.astype(jnp.float32).reshape(1, N_KV_HEADS, Q_PER_KV, 1, 1, 1)
    sink = jnp.broadcast_to(sink, scores.shape[:-1] + (1,))
    probs = jax.nn.softmax(jnp.concatenate([scores, sink], axis=-1), axis=-1)[..., :-1]
    out = jnp.einsum('bhgnqs,bnshd->bnqhgd', probs.astype(v.dtype), vb)
    return out.reshape(bsz, s, ATTN_WIDTH)

def hybrid_mixer(u, cos, sin, w_in, conv_w, conv_b, lru_w_a, lru_b_a, lru_w_x, lru_b_x,
                 lru_lambda, attn_sinks, w_proj_lru, w_proj_attn, w_out):
    bsz, s, _ = u.shape
    z = u @ w_in
    gate_br, x_br, q, k, v, g_lru, g_attn = jnp.split(z, IN_SPLITS, axis=-1)
    xc = causal_depthwise_conv(x_br, conv_w, conv_b)
    y_lru = rg_lru(xc, lru_w_a, lru_b_a, lru_w_x, lru_b_x, lru_lambda) * jax.nn.gelu(gate_br)
    q = apply_rope(q.reshape(bsz, s, N_Q_HEADS, HEAD_DIM), cos, sin)
    k = apply_rope(k.reshape(bsz, s, N_KV_HEADS, HEAD_DIM), cos, sin)
    v = v.reshape(bsz, s, N_KV_HEADS, HEAD_DIM)
    y_attn = sliding_window_attention_with_sinks(q, k, v, attn_sinks)
    merged = jax.nn.sigmoid(g_lru) * (y_lru @ w_proj_lru) + jax.nn.sigmoid(g_attn) * (y_attn @ w_proj_attn)
    return merged @ w_out

def first_inputs(seed: int = 0) -> dict:
    key = jax.random.key(seed)
    ks = jax.random.split(key, 24)

    def nrm(k, shape, scale):
        return jax.random.normal(k, shape, jnp.float32) * scale

    def gain(k, shape):
        return 1.0 + 0.05 * jax.random.normal(k, shape, jnp.float32)

    u = jax.random.uniform(ks[13], (DEPTH, LRU_WIDTH), jnp.float32, minval=0.9, maxval=0.999)
    a0 = u ** (1.0 / LRU_C)
    lam = jnp.log(a0) - jnp.log1p(-a0)
    return {
        "x": nrm(ks[0], (BATCH, SEQ, D_MODEL), 1.0),
        "ffn1_pre_g": gain(ks[1], (DEPTH, D_MODEL)),
        "ffn1_w_gu": nrm(ks[2], (DEPTH, D_MODEL, 2 * D_FF), D_MODEL ** -0.5),
        "ffn1_w_down": nrm(ks[3], (DEPTH, D_FF, D_MODEL), D_FF ** -0.5),
        "ffn1_post_g": gain(ks[4], (DEPTH, D_MODEL)),
        "mix_pre_g": gain(ks[5], (DEPTH, D_MODEL)),
        "w_in": nrm(ks[6], (DEPTH, D_MODEL, IN_WIDTH), D_MODEL ** -0.5),
        "conv_w": nrm(ks[7], (DEPTH, CONV_WIDTH, LRU_WIDTH), CONV_WIDTH ** -0.5),
        "conv_b": nrm(ks[8], (DEPTH, LRU_WIDTH), 0.01),
        "lru_w_a": nrm(ks[9], (DEPTH, LRU_BLOCKS, LRU_BLOCK_W, LRU_BLOCK_W), LRU_BLOCK_W ** -0.5),
        "lru_b_a": nrm(ks[10], (DEPTH, LRU_WIDTH), 0.01),
        "lru_w_x": nrm(ks[11], (DEPTH, LRU_BLOCKS, LRU_BLOCK_W, LRU_BLOCK_W), LRU_BLOCK_W ** -0.5),
        "lru_b_x": nrm(ks[12], (DEPTH, LRU_WIDTH), 0.01),
        "lru_lambda": lam,
        "attn_sinks": nrm(ks[14], (DEPTH, N_Q_HEADS), 0.5),
        "w_proj_lru": nrm(ks[15], (DEPTH, LRU_WIDTH, D_MODEL), LRU_WIDTH ** -0.5),
        "w_proj_attn": nrm(ks[16], (DEPTH, ATTN_WIDTH, D_MODEL), ATTN_WIDTH ** -0.5),
        "w_out": nrm(ks[17], (DEPTH, D_MODEL, D_MODEL), D_MODEL ** -0.5),
        "mix_post_g": gain(ks[18], (DEPTH, D_MODEL)),
        "ffn2_pre_g": gain(ks[19], (DEPTH, D_MODEL)),
        "ffn2_w_gu": nrm(ks[20], (DEPTH, D_MODEL, 2 * D_FF), D_MODEL ** -0.5),
        "ffn2_w_down": nrm(ks[21], (DEPTH, D_FF, D_MODEL), D_FF ** -0.5),
        "ffn2_post_g": gain(ks[22], (DEPTH, D_MODEL)),
    }

def first_block(x, ffn1_pre_g, ffn1_w_gu, ffn1_w_down, ffn1_post_g,
              mix_pre_g, w_in, conv_w, conv_b, lru_w_a, lru_b_a, lru_w_x, lru_b_x,
              lru_lambda, attn_sinks, w_proj_lru, w_proj_attn, w_out, mix_post_g,
              ffn2_pre_g, ffn2_w_gu, ffn2_w_down, ffn2_post_g):
    cos, sin = rope_tables(x.shape[1])
    h = x
    for l in range(DEPTH):
        f = swiglu(rms_norm(h, ffn1_pre_g[l]), ffn1_w_gu[l], ffn1_w_down[l])
        h = h + MACARON_SCALE * rms_norm(f, ffn1_post_g[l])
        m = hybrid_mixer(rms_norm(h, mix_pre_g[l]), cos, sin, w_in[l], conv_w[l], conv_b[l],
                         lru_w_a[l], lru_b_a[l], lru_w_x[l], lru_b_x[l], lru_lambda[l],
                         attn_sinks[l], w_proj_lru[l], w_proj_attn[l], w_out[l])
        h = h + rms_norm(m, mix_post_g[l])
        f = swiglu(rms_norm(h, ffn2_pre_g[l]), ffn2_w_gu[l], ffn2_w_down[l])
        h = h + MACARON_SCALE * rms_norm(f, ffn2_post_g[l])
    return h


DEPTH_2 = 2

CONV_WIDTH_2 = 512
CONV_GROUPS = 8
CONV_K = 3
MLA_HEADS = 8
MLA_Q_LORA = 256
MLA_KV_LORA = 128
MLA_NOPE = 64
MLA_ROPE = 32
MLA_V = 64
MLA_QK = MLA_NOPE + MLA_ROPE
DIL_PATTERNS = ((128, 1), (512, 4), (2048, 16))
DIL_GROUPS = len(DIL_PATTERNS)
DIL_HEADS = 8
DIL_HEAD_DIM = 64
DIL_WIDTH = DIL_HEADS * DIL_HEAD_DIM
N_BRANCH = 3
Q_BLOCK = 128
EPS = 1e-6

SPLIT_SIZES = ((CONV_WIDTH_2,) * 4
               + (MLA_Q_LORA, MLA_KV_LORA, MLA_ROPE, MLA_HEADS * MLA_V)
               + (DIL_GROUPS * DIL_WIDTH,) * 3 + (DIL_WIDTH,)
               + (N_BRANCH * D_MODEL,))
SPLIT_POINTS = tuple(int(v) for v in np.cumsum(SPLIT_SIZES)[:-1])
N_IN = int(sum(SPLIT_SIZES))


def rmsnorm(x, g):
    xf = x.astype(jnp.float32)
    y = xf * lax.rsqrt(jnp.mean(xf * xf, axis=-1, keepdims=True) + EPS)
    return (y * g.astype(jnp.float32)).astype(x.dtype)

def rope_tables_2(S):
    inv = ROPE_THETA ** (-jnp.arange(0, MLA_ROPE, 2, dtype=jnp.float32) / MLA_ROPE)
    ang = jnp.arange(S, dtype=jnp.float32)[:, None] * inv[None, :]
    return jnp.cos(ang), jnp.sin(ang)

def apply_rope_2(t, cos, sin):
    tf = t.astype(jnp.float32)
    t1, t2 = jnp.split(tf, 2, axis=-1)
    c = cos[None, :, None, :]
    s = sin[None, :, None, :]
    return jnp.concatenate([t1 * c - t2 * s, t2 * c + t1 * s], axis=-1).astype(t.dtype)

def alibi_slopes():
    n = DIL_GROUPS * DIL_HEADS
    m = 2.0 ** (-8.0 * jnp.arange(1, n + 1, dtype=jnp.float32) / n)
    return m.reshape(DIL_GROUPS, DIL_HEADS)

def causal_block_attention(q, k, v, scale):
    B, H, S, Dk = q.shape
    Dv = v.shape[-1]
    nqb = S // Q_BLOCK
    qb = q.reshape(B, H, nqb, Q_BLOCK, Dk).transpose(2, 0, 1, 3, 4)
    kf = k.astype(jnp.float32)
    vf = v.astype(jnp.float32)
    kpos = jnp.arange(S)

    def one_block(args):
        qblk, i = args
        s = jnp.einsum('bhqc,bhkc->bhqk', qblk.astype(jnp.float32), kf) * scale
        qpos = i * Q_BLOCK + jnp.arange(Q_BLOCK)
        s = jnp.where(kpos[None, :] <= qpos[:, None], s, -jnp.inf)
        p = jax.nn.softmax(s, axis=-1)
        return jnp.einsum('bhqk,bhkc->bhqc', p, vf)

    o = lax.map(one_block, (qb, jnp.arange(nqb)))
    return o.transpose(1, 2, 0, 3, 4).reshape(B, H, S, Dv)

def dilated_group_attention(q, k, v, slopes, dilation, n_back):
    B, S, H, hd = q.shape
    L = S // dilation
    nb = -(-L // Q_BLOCK)
    Lp = nb * Q_BLOCK

    def to_sub(t):
        return t.reshape(B, L, dilation, H, hd).transpose(0, 2, 3, 1, 4)

    qs = jnp.pad(to_sub(q).astype(jnp.float32), ((0, 0), (0, 0), (0, 0), (0, Lp - L), (0, 0)))
    qs = qs.reshape(B, dilation, H, nb, Q_BLOCK, hd)

    def windows(t):
        tp = jnp.pad(to_sub(t).astype(jnp.float32), ((0, 0), (0, 0), (0, 0), (Q_BLOCK, Lp - L), (0, 0)))
        tb = tp.reshape(B, dilation, H, nb + 1, Q_BLOCK, hd)
        return jnp.concatenate([tb[:, :, :, :-1], tb[:, :, :, 1:]], axis=4)

    kw = windows(k)
    vw = windows(v)
    qq = jnp.arange(Q_BLOCK)[:, None]
    kk = jnp.arange(2 * Q_BLOCK)[None, :]
    j = Q_BLOCK + qq - kk
    key_idx = (jnp.arange(nb)[:, None, None] - 1) * Q_BLOCK + kk[None]
    valid = (j >= 0) & (j <= n_back) & (key_idx >= 0)
    dist = (dilation * j).astype(jnp.float32)
    bias = -slopes.reshape(1, 1, H, 1, 1, 1) * dist
    scale = DIL_HEAD_DIM ** -0.5
    s = jnp.einsum('bdhnqc,bdhnkc->bdhnqk', qs, kw) * scale + bias
    s = jnp.where(valid, s, -jnp.inf)
    lse = jax.nn.logsumexp(s, axis=-1)
    p = jnp.exp(s - lse[..., None])
    o = jnp.einsum('bdhnqk,bdhnkc->bdhnqc', p, vw)
    o = o.reshape(B, dilation, H, Lp, hd)[:, :, :, :L]
    lse = lse.reshape(B, dilation, H, Lp)[:, :, :, :L]
    o = o.transpose(0, 3, 1, 2, 4).reshape(B, S, H, hd)
    lse = lse.transpose(0, 3, 1, 2).reshape(B, S, H)
    return o, lse

def hybrid_layer(x, norm_g, w_in, b_gate, conv_w, conv_b, q_a_norm_g, w_uq, kv_a_norm_g, w_ukv,
                 mla_q_norm_g, mla_k_norm_g, dil_q_norm_g, dil_k_norm_g,
                 w_out_a, w_out_b, w_out_c, w_o, cos, sin, slopes):
    B, S, _ = x.shape
    h = rmsnorm(x, norm_g)
    proj = h @ w_in
    (a_b, a_c, a_x, a_z, c_q, c_kv, k_pe, b_z, dq, dk, dv, c_z, gate_pre) = jnp.split(proj, SPLIT_POINTS, axis=-1)

    u = a_c * a_x
    up = jnp.pad(u, ((0, 0), (CONV_K - 1, 0), (0, 0)))
    conv = conv_b
    for tap in range(CONV_K):
        conv = conv + up[:, tap:tap + S] * conv_w[tap]
    y_a = a_b * conv * jax.nn.silu(a_z)

    q = (rmsnorm(c_q, q_a_norm_g) @ w_uq).reshape(B, S, MLA_HEADS, MLA_QK)
    kv = (rmsnorm(c_kv, kv_a_norm_g) @ w_ukv).reshape(B, S, MLA_HEADS, MLA_NOPE + MLA_V)
    k_nope, v = jnp.split(kv, [MLA_NOPE], axis=-1)
    k = jnp.concatenate([k_nope, jnp.broadcast_to(k_pe[:, :, None, :], (B, S, MLA_HEADS, MLA_ROPE))], axis=-1)
    q = rmsnorm(q, mla_q_norm_g)
    k = rmsnorm(k, mla_k_norm_g)
    q = jnp.concatenate([q[..., :MLA_NOPE], apply_rope_2(q[..., MLA_NOPE:], cos, sin)], axis=-1)
    k = jnp.concatenate([k[..., :MLA_NOPE], apply_rope_2(k[..., MLA_NOPE:], cos, sin)], axis=-1)
    o_b = causal_block_attention(q.transpose(0, 2, 1, 3), k.transpose(0, 2, 1, 3), v.transpose(0, 2, 1, 3),
                                 MLA_QK ** -0.5)
    o_b = o_b.transpose(0, 2, 1, 3).reshape(B, S, MLA_HEADS * MLA_V).astype(x.dtype)
    y_b = o_b * jax.nn.silu(b_z)

    dq = rmsnorm(dq.reshape(B, S, DIL_GROUPS, DIL_HEADS, DIL_HEAD_DIM), dil_q_norm_g[:, None, :])
    dk = rmsnorm(dk.reshape(B, S, DIL_GROUPS, DIL_HEADS, DIL_HEAD_DIM), dil_k_norm_g[:, None, :])
    dv = dv.reshape(B, S, DIL_GROUPS, DIL_HEADS, DIL_HEAD_DIM)
    outs = []
    lses = []
    for gi, (window, dilation) in enumerate(DIL_PATTERNS):
        o_g, lse_g = dilated_group_attention(dq[:, :, gi], dk[:, :, gi], dv[:, :, gi], slopes[gi],
                                             dilation, window // dilation)
        outs.append(o_g)
        lses.append(lse_g)
    alpha = jax.nn.softmax(jnp.stack(lses, axis=0), axis=0)
    o_c = jnp.sum(alpha[..., None] * jnp.stack(outs, axis=0), axis=0)
    o_c = o_c.reshape(B, S, DIL_WIDTH).astype(x.dtype)
    y_c = o_c * jax.nn.silu(c_z)

    g_a, g_b, g_c = jnp.split(jax.nn.sigmoid(gate_pre + b_gate), N_BRANCH, axis=-1)
    merged = g_a * (y_a @ w_out_a) + g_b * (y_b @ w_out_b) + g_c * (y_c @ w_out_c)
    return x + merged @ w_o

def second_inputs(seed: int = 0) -> dict:
    key = jax.random.key(seed)
    ks = jax.random.split(key, 18)
    f32 = jnp.float32

    def nrm(k, shape, scale):
        return jax.random.normal(k, shape, f32) * scale

    def gain(k, shape):
        return 1.0 + 0.02 * jax.random.normal(k, shape, f32)

    Ld = DEPTH_2
    return {
        'x': jax.random.normal(ks[0], (BATCH, SEQ, D_MODEL), f32),
        'norm_g': gain(ks[1], (Ld, D_MODEL)),
        'w_in': nrm(ks[2], (Ld, D_MODEL, N_IN), D_MODEL ** -0.5),
        'b_gate': nrm(ks[3], (Ld, N_BRANCH * D_MODEL), 0.1),
        'conv_w': nrm(ks[4], (Ld, CONV_K, CONV_WIDTH_2), CONV_K ** -0.5),
        'conv_b': nrm(ks[5], (Ld, CONV_WIDTH_2), 0.02),
        'q_a_norm_g': gain(ks[6], (Ld, MLA_Q_LORA)),
        'w_uq': nrm(ks[7], (Ld, MLA_Q_LORA, MLA_HEADS * MLA_QK), MLA_Q_LORA ** -0.5),
        'kv_a_norm_g': gain(ks[8], (Ld, MLA_KV_LORA)),
        'w_ukv': nrm(ks[9], (Ld, MLA_KV_LORA, MLA_HEADS * (MLA_NOPE + MLA_V)), MLA_KV_LORA ** -0.5),
        'mla_q_norm_g': gain(ks[10], (Ld, MLA_QK)),
        'mla_k_norm_g': gain(ks[11], (Ld, MLA_QK)),
        'dil_q_norm_g': gain(ks[12], (Ld, DIL_GROUPS, DIL_HEAD_DIM)),
        'dil_k_norm_g': gain(ks[13], (Ld, DIL_GROUPS, DIL_HEAD_DIM)),
        'w_out_a': nrm(ks[14], (Ld, CONV_WIDTH_2, D_MODEL), CONV_WIDTH_2 ** -0.5),
        'w_out_b': nrm(ks[15], (Ld, MLA_HEADS * MLA_V, D_MODEL), (MLA_HEADS * MLA_V) ** -0.5),
        'w_out_c': nrm(ks[16], (Ld, DIL_WIDTH, D_MODEL), DIL_WIDTH ** -0.5),
        'w_o': nrm(ks[17], (Ld, D_MODEL, D_MODEL), D_MODEL ** -0.5),
    }

def second_block(x, norm_g, w_in, b_gate, conv_w, conv_b, q_a_norm_g, w_uq, kv_a_norm_g, w_ukv,
              mla_q_norm_g, mla_k_norm_g, dil_q_norm_g, dil_k_norm_g, w_out_a, w_out_b, w_out_c, w_o):
    cos, sin = rope_tables_2(x.shape[1])
    slopes = alibi_slopes()
    for l in range(DEPTH_2):
        x = hybrid_layer(x, norm_g[l], w_in[l], b_gate[l], conv_w[l], conv_b[l], q_a_norm_g[l], w_uq[l],
                         kv_a_norm_g[l], w_ukv[l], mla_q_norm_g[l], mla_k_norm_g[l], dil_q_norm_g[l],
                         dil_k_norm_g[l], w_out_a[l], w_out_b[l], w_out_c[l], w_o[l], cos, sin, slopes)
    return x


def setup_inputs(seed=0):
    out = dict(first_inputs(seed))
    for name, value in second_inputs(seed + 1).items():
        if name != "x":
            out[name + "_2"] = value
    return out


def reference(
    x, ffn1_pre_g, ffn1_w_gu, ffn1_w_down, ffn1_post_g, mix_pre_g, w_in, conv_w, conv_b,
    lru_w_a, lru_b_a, lru_w_x, lru_b_x, lru_lambda, attn_sinks, w_proj_lru, w_proj_attn, w_out,
    mix_post_g, ffn2_pre_g, ffn2_w_gu, ffn2_w_down, ffn2_post_g, norm_g_2, w_in_2, b_gate_2,
    conv_w_2, conv_b_2, q_a_norm_g_2, w_uq_2, kv_a_norm_g_2, w_ukv_2, mla_q_norm_g_2,
    mla_k_norm_g_2, dil_q_norm_g_2, dil_k_norm_g_2, w_out_a_2, w_out_b_2, w_out_c_2, w_o_2,
):
    x = first_block(
        x, ffn1_pre_g, ffn1_w_gu, ffn1_w_down, ffn1_post_g, mix_pre_g, w_in, conv_w, conv_b,
        lru_w_a, lru_b_a, lru_w_x, lru_b_x, lru_lambda, attn_sinks, w_proj_lru, w_proj_attn,
        w_out, mix_post_g, ffn2_pre_g, ffn2_w_gu, ffn2_w_down, ffn2_post_g,
    )
    return second_block(
        x, norm_g_2, w_in_2, b_gate_2, conv_w_2, conv_b_2, q_a_norm_g_2, w_uq_2, kv_a_norm_g_2,
        w_ukv_2, mla_q_norm_g_2, mla_k_norm_g_2, dil_q_norm_g_2, dil_k_norm_g_2, w_out_a_2,
        w_out_b_2, w_out_c_2, w_o_2,
    )


_drawn_inputs = setup_inputs


def setup_inputs(seed=0):
    import zlib

    import numpy as np

    out = dict(_drawn_inputs(seed))
    spreads = {}
    factors = {'lru_b_a': 8.0,
     'lru_b_x': 8.0,
     'attn_sinks': 2.697,
     'ffn2_post_g': 3.133,
     'norm_g_2': 4.304,
     'b_gate_2': 4.319,
     'conv_b_2': 25.754,
     'q_a_norm_g_2': 8.0,
     'kv_a_norm_g_2': 8.0,
     'mla_q_norm_g_2': 8.0,
     'mla_k_norm_g_2': 8.0,
     'dil_q_norm_g_2': 30.447,
     'dil_k_norm_g_2': 30.14}
    for name, (base, spread) in spreads.items():
        noise = np.random.default_rng([zlib.crc32(name.encode()), seed]).standard_normal(out[name].shape)
        drawn = base * np.exp(spread * noise) if base else spread * noise
        out[name] = jnp.asarray(drawn.astype(out[name].dtype))
    for name, factor in factors.items():
        out[name] = (out[name] * factor).astype(out[name].dtype)
    return out
```

```python
import math
from contextlib import ExitStack

import concourse.bass as bass
import numpy as np
from concourse import mybir

F32 = mybir.dt.float32
F32R = mybir.dt.float32r
ALU = mybir.AluOpType
ACT = mybir.ActivationFunctionType
AX = mybir.AxisListType

P = 128
SEQ = 256
TOK = SEQ // P
D = 1024
KD = D // P
D_FF = 2816
FF_STEP = 256
FF_STEPS = D_FF // FF_STEP
LAYERS = 2
TILE = 1024
RING = 3
BIG = 1e33
NEG = -1e30

HEAD = 64
HALF = HEAD // 2
Q_HEADS = 16
KV_HEADS = 4
LRU_C = 8.0
CONV1 = 4
MLA_HEADS = 8
NOPE = 64
ROPE2 = 32
QK = NOPE + ROPE2
DIL_HEADS = 8
DIL_GROUPS = 3
DILATIONS = (1, 4, 16)
DIL_BACK = 128
CONV2 = 3
W2 = 512
K2 = W2 // P
EPS = 1e-6
GELU_C = math.sqrt(2.0 / math.pi)

FFN_TILES = 6 * FF_STEPS
MIX_CHUNKS = 17
MIX_TILES = 4 * MIX_CHUNKS
FFN1_AT = 0
MIX_AT = FFN1_AT + FFN_TILES
FFN2_AT = MIX_AT + MIX_TILES
LAYER_AT = FFN2_AT + FFN_TILES
LAYER_CHUNKS = 22
LAYER_TILES = 4 * LAYER_CHUNKS + 3 + 12 + 8
LOOK = 2
ALL_TILES = LAYER_AT + LAYERS * LAYER_TILES + LOOK
assert LAYER_TILES % RING == 0

C_IDENT = 0
C_MASK1 = C_IDENT + P
C_MASK2 = C_MASK1 + SEQ
C_DIL = C_MASK2 + SEQ
C_ROPE1 = C_DIL + DIL_GROUPS * SEQ
C_ROPE2 = C_ROPE1 + 2 * TOK * HALF
N_CONST = C_ROPE2 + 2 * TOK * (ROPE2 // 2)
B_FFN1, B_MIX, B_FFN2, B_CONVW = 0, 8, 16, 24
B_CONVB, B_BA, B_BX, B_LAM, B_SINK = 56, 64, 72, 80, 88
N_B1 = B_SINK + Q_HEADS
L_NORM, L_CONVW, L_CONVB, L_QA, L_KVA, L_DQ, L_DK, L_GQ = 0, 8, 20, 24, 26, 27, 30, 33
L_GK = L_GQ + QK
N_LP = L_GK + QK
GATE_CHUNKS = 6


class At:

    def __init__(self, base, var=None, per=0):
        self.base, self.var, self.per = base, var, per

    def __add__(self, n):
        return At(self.base + n, self.var, self.per)

    def __mul__(self, n):
        return At(self.base * n, self.var, self.per * n)

    @property
    def slot(self):
        assert self.per % RING == 0
        return self.base % RING

    @property
    def value(self):
        return self.base if self.var is None else self.var * self.per + self.base

    @property
    def loaded(self):
        rounds = 16 * (self.base // RING + 1)
        return rounds if self.var is None else self.var * (16 * self.per // RING) + rounds

    @property
    def first(self):
        return self.var is None and self.base < RING


class Steps:

    def __init__(self, eng, sem):
        self.eng, self.sem, self.n = eng, sem, 0

    def mark(self, ins):
        ins.then_inc(self.sem, 1)
        self.n += 1

    def sync(self):
        self.eng.wait_ge(self.sem, self.n)

    def link(self, ins):
        self.mark(ins)
        self.sync()

    def restart(self):
        self.sync()
        self.eng.sem_clear(self.sem)
        self.n = 0


def slope(g, h):
    return 2.0 ** (-8.0 * (g * DIL_HEADS + h + 1) / (DIL_GROUPS * DIL_HEADS))


def units_two_tiles(heads):
    return [(0, list(range(h, h + 8))) for h in range(0, heads, 8)] + [
        (1, list(range(h, h + 4))) for h in range(0, heads, 4)]


def even_odd(heads):
    return heads[0::2] + heads[1::2]


DIL_UNITS = [(0, [h, h + 2]) for h in (0, 1, 4, 5)] + [(1, [h]) for h in range(DIL_HEADS)]
UNITS1 = [(qt, even_odd(heads)) for qt, heads in units_two_tiles(Q_HEADS)]
UNITS_MLA = units_two_tiles(MLA_HEADS)
UNITS_LAYER = len(UNITS_MLA) + len(DIL_UNITS)


def block_program(nc, x, weights, consts, params1, gains, lru_w, layer_params, gate_bias, selectors, out):
    ctx = ExitStack()
    with ctx:
        def sb(name, shape, dt=F32):
            return ctx.enter_context(nc.sbuf_tensor(name, shape, dt))

        def sem(name):
            return ctx.enter_context(nc.semaphore(name))

        raw = sb("raw", [P, RING, TILE])
        w_hi = sb("w_hi", [P, RING, TILE], F32R)
        w_lo = sb("w_lo", [P, RING, TILE], F32R)
        x_hi = sb("x_hi", [P, KD, SEQ], F32R)
        x_lo = sb("x_lo", [P, KD, SEQ], F32R)
        y1_hi = sb("y1_hi", [P, KD, SEQ], F32R)
        y1_lo = sb("y1_lo", [P, KD, SEQ], F32R)
        y2_hi = sb("y2_hi", [P, KD, SEQ], F32R)
        y2_lo = sb("y2_lo", [P, KD, SEQ], F32R)
        res = sb("res", [P, TOK, D])
        norm = sb("norm", [P, TOK, D])
        cst = sb("cst", [P, N_CONST])
        squares = sb("squares", [P, 80])
        rstd = sb("rstd", [P, 80])
        mean = sb("mean", [P, 32])
        power = sb("power", [P, 32])
        scores_max = sb("scores_max", [P, Q_HEADS])
        scores_sum = sb("scores_sum", [P, TOK * Q_HEADS])
        sum_recip = sb("sum_recip", [P, TOK * Q_HEADS])
        probs = sb("probs", [P, 1024])
        probs_t = sb("probs_t", [P, 1024])
        ident = cst[:, C_IDENT:C_IDENT + P]
        mask_window = cst[:, C_MASK1:C_MASK1 + SEQ]
        mask_causal = cst[:, C_MASK2:C_MASK2 + SEQ]
        dil_dist = cst[:, C_DIL:C_DIL + DIL_GROUPS * SEQ].rearrange("p (g s) -> p g s", g=DIL_GROUPS)
        rope1 = cst[:, C_ROPE1:C_ROPE1 + 2 * TOK * HALF].rearrange("p (c t i) -> p c t i", c=2, t=TOK)
        rope2 = cst[:, C_ROPE2:N_CONST].rearrange("p (c t i) -> p c t i", c=2, t=TOK)

        ARENA = 21760
        arena = sb("arena", [P, ARENA])
        sel_r = sb("sel_r", [GATE_CHUNKS, GATE_CHUNKS * P], F32R)
        bias_hi = sb("bias_hi", [GATE_CHUNKS, 512], F32R)
        bias_lo = sb("bias_lo", [GATE_CHUNKS, 512], F32R)

        def view(at, *shape):
            n = int(np.prod(shape))
            assert at + n <= ARENA, (at, shape)
            flat = arena[:, at:at + n]
            if len(shape) == 1:
                return flat
            names = "abcd"[:len(shape)]
            return flat.rearrange(f"p ({' '.join(names)}) -> p {' '.join(names)}",
                                  **{n_: s for n_, s in zip(names[:-1], shape[:-1])})

        XB_W = SEQ + CONV1 - 1
        gain_row = view(0, D)
        lru_blocks = view(0, 2, KD, P)
        par = view(2048, N_B1)
        half_bias = view(2152, 2 * KD)
        c4 = view(2168, KD)
        soft = view(2176, 6, KD)
        sink_exp = view(2224, TOK * Q_HEADS)
        kv_tok = view(2304, TOK, 512)
        q_t = view(3328, KD, SEQ)
        k_t = view(5376, KV_HEADS // 2, SEQ)
        gate_t = view(5888, 2, TOK, D)
        xb = view(9984, KD, XB_W)
        xc = view(12064, KD, SEQ)
        lru_a = view(14112, KD, SEQ)
        lru_i = view(16160, KD, SEQ)
        lru_e = view(18208, KD, SEQ)
        q_tok = view(14112, TOK, D)
        lru_tl = view(9984, KD, SEQ)
        heads1 = view(9984, TOK, D)
        gelu = norm[:, :, :].rearrange("p t (f s) -> p (t f) s", s=SEQ)
        merged1 = view(18208, TOK, D)
        merge_tmp1 = view(14112, TOK, 512)
        ff_t = view(9984, TOK, FF_STEP)
        ff_a = view(9984 + 512, TOK, FF_STEP)
        sel_stage = view(9984, GATE_CHUNKS * P)[0:GATE_CHUNKS, :]
        lp = view(0, N_LP)
        bias_stage = view(10496, 512)[0:GATE_CHUNKS, :]
        dil_v = view(256, DIL_GROUPS, TOK, 512)
        dil_q = view(3328, 4 * DIL_GROUPS, SEQ)
        dil_k = view(6400, 4 * DIL_GROUPS, SEQ)
        mla_v = view(9472, TOK, 512)
        y_tok = view(10496, TOK, 512)
        ga_t = view(11520, 3, TOK, D)
        qk = view(11520, TOK, 2 * MLA_HEADS, QK)
        qk_sq = view(14592, TOK, 2 * MLA_HEADS, QK)
        mla_t = view(17664, 2 * MLA_HEADS, SEQ)
        conv_in = view(17664 + 1024, 4, SEQ + CONV2 - 1)
        a_c = view(17664, 4, SEQ)
        a_y = view(17664 + 2056, 4, SEQ)
        a_z = view(17664, 4, SEQ)
        merged2 = view(17664, TOK, D)
        merge_tmp2 = view(17664 + 2048, TOK, 512)

        psum = ctx.enter_context(nc.psum_tensor("psum", [P, 8, 512], F32))

        def pair(fill):
            return psum[:, 2 * (fill % 2):2 * (fill % 2) + 2, :]

        def wide(b, n):
            return psum[:, b:8, :].rearrange("p b n -> p (b n)")[:, 0:n]

        raw_loaded = [sem(f"raw_loaded{i}") for i in range(RING)]
        hi_ready = sem("hi_ready")
        lo_ready = sem("lo_ready")
        weights_used = sem("weights_used")
        x_loaded = sem("x_loaded")
        small_loaded = sem("small_loaded")
        gain_loaded = sem("gain_loaded")
        layer_loaded = sem("layer_loaded")
        x_ready = sem("x_ready")
        x_stored = sem("x_stored")
        power_set = sem("power_set")
        mean_ready = sem("mean_ready")
        root_started = sem("root_started")
        act_step = sem("act_step")
        dve_step = sem("dve_step")
        squares_ready = sem("squares_ready")
        rstd_ready = sem("rstd_ready")
        normed = sem("normed")
        norm_turned = sem("norm_turned")
        norm_hi = sem("norm_hi")
        norm_lo = sem("norm_lo")
        post_squares = sem("post_squares")
        post_rstd = sem("post_rstd")
        swish_tanh = sem("swish_tanh")
        hidden_ready = sem("hidden_ready")
        hidden_turned = sem("hidden_turned")
        hidden_hi = sem("hidden_hi")
        hidden_lo = sem("hidden_lo")
        act_freed = sem("act_freed")
        dve_freed = sem("dve_freed")
        scores_ready = sem("scores_ready")
        max_ready = sem("max_ready")
        exp_done = sem("exp_done")
        probs_turned = sem("probs_turned")
        probs_act = sem("probs_act")
        probs_dve = sem("probs_dve")
        values_ready = sem("values_ready")
        values_read = sem("values_read")
        fold_ready = sem("fold_ready")
        abs_exp = sem("abs_exp")
        rope_ready = sem("rope_ready")
        qk_turned = sem("qk_turned")
        q_copied = sem("q_copied")
        k_copied = sem("k_copied")
        conv_done = sem("conv_done")
        lru_loaded = sem("lru_loaded")
        bias_rest = sem("bias_rest")
        q_copied_b = sem("q_copied_b")
        sink_done = sem("sink_done")
        half_swish = sem("half_swish")
        ri_ready = sem("ri_ready")
        tl_ready = sem("tl_ready")
        decay_ready = sem("decay_ready")
        gelu_arg = sem("gelu_arg")
        gelu_tanh = sem("gelu_tanh")
        sqrt_arg = sem("sqrt_arg")
        sqrt_done = sem("sqrt_done")
        lru_ready = sem("lru_ready")
        lru_hi = sem("lru_hi")
        lru_lo = sem("lru_lo")
        heads_ready = sem("heads_ready")
        heads_turned = sem("heads_turned")
        heads_hi = sem("heads_hi")
        heads_lo = sem("heads_lo")
        merged_ready = sem("merged_ready")
        merged_turned = sem("merged_turned")
        merged_hi = sem("merged_hi")
        merged_lo = sem("merged_lo")
        bias_split = sem("bias_split")
        lora_squares = sem("lora_squares")
        lora_rstd = sem("lora_rstd")
        lora_ready = sem("lora_ready")
        lora_turned = sem("lora_turned")
        lora_hi = sem("lora_hi")
        lora_lo = sem("lora_lo")
        dil_squares = sem("dil_squares")
        dil_sums = sem("dil_sums")
        dil_rstd = sem("dil_rstd")
        dil_normed = sem("dil_normed")
        dil_turned = sem("dil_turned")
        dil_copied = sem("dil_copied")
        up_copied = sem("up_copied")
        mla_squares = sem("mla_squares")
        mla_sums = sem("mla_sums")
        mla_rstd = sem("mla_rstd")
        mla_ready = sem("mla_ready")
        mla_turned = sem("mla_turned")
        mla_copied = sem("mla_copied")
        silu_tanh = sem("silu_tanh")
        ya_ready = sem("ya_ready")
        ya_hi = sem("ya_hi")
        ya_lo = sem("ya_lo")

        FILLS1 = "AAAAA" + "AA" + "AA" + "A" + "AA" + "AAA" + "VVVV"
        (F_KV, F_Q0, F_Q1, F_XB0, F_XB1, F_GATE0, F_GATE1, F_R0, F_I0, F_GL0, F_R1, F_I1, F_GL1, F_GA0,
         F_GA1, F_PL0, F_PL1, F_PA0, F_PA1) = range(19)
        FILLS2 = "AAA" + "AA" + "AAAAAAA" + "VV" + "AVVV" + "AAAAAA" + "VVVVVV"
        FREED = {"A": act_freed, "V": dve_freed}

        def freed(fill, layer=None):
            fills = FILLS1 if layer is None else FILLS2
            who = fills[fill]
            n = fills[:fill + 1].count(who)
            if layer is None:
                return FREED[who], n
            return FREED[who], At(FILLS1.count(who) + n, layer, FILLS2.count(who)).value

        def fill_of(chunk):
            return chunk if chunk < 3 else chunk + 2

        def chunk_at(base, chunk):
            return base + (4 * chunk if chunk < 3 else 4 * chunk + 3)

        block = ctx.enter_context(nc.Block())

        @block.sync
        def _(sp):
            sp.dma_start(res[:, :, :], x.rearrange("(t p) d -> p t d", p=P)).then_inc(x_loaded, 16)
            for t in range(RING):
                sp.dma_start(raw[:, t, :], weights[t, :, :]).then_inc(raw_loaded[t], 16)
            rounds = ALL_TILES // RING
            with sp.Fori(1, rounds) as r:
                for s in range(RING):
                    sp.wait_ge(lo_ready, At(s - RING + 1, r, RING).value)
                    sp.dma_start(raw[:, s, :], weights[bass.ds(r * RING + s, 1), :, :].rearrange("a p n -> (a p) n")
                                 ).then_inc(raw_loaded[s], 16)
            for t in range(rounds * RING, ALL_TILES):
                sp.wait_ge(lo_ready, t - RING + 1)
                sp.dma_start(raw[:, t % RING, :], weights[t, :, :]).then_inc(raw_loaded[t % RING], 16)
            sp.wait_ge(x_ready, 2 * (3 + LAYERS))
            sp.dma_start(out.rearrange("(t p) d -> p t d", p=P), res[:, :, :]).then_inc(x_stored, 16)
            sp.wait_ge(x_stored, 16)

        @block.gpsimd
        def _(pool):
            pool.memset(power[:, :], -0.5).then_inc(power_set, 1)
            pool.wait_ge(power_set, 1)

            jobs = At(0)

            def inverse_root(at, n, width, done):
                nonlocal jobs
                jobs = jobs + 1
                pool.sem_inc(root_started, 1)
                pool.tensor_scalar(mean[:, 0:n], squares[:, at:at + n], 1.0 / width, EPS,
                                   ALU.mult, ALU.add).then_inc(mean_ready, 1)
                pool.wait_ge(mean_ready, jobs.value)
                pool.tensor_tensor(rstd[:, at:at + n], mean[:, 0:n], power[:, 0:n], ALU.pow).then_inc(done, 1)

            def pre_norm(n):
                for tok in range(TOK):
                    pool.wait_ge(squares_ready, (n + (1 + tok)).value)
                    inverse_root(tok, 1, D, rstd_ready)
                    pool.wait_ge(rstd_ready, (n + (1 + tok)).value)

            for n in range(3):
                pre_norm(At(TOK * n))
                for tok in range(TOK):
                    pool.wait_ge(post_squares, TOK * n + tok + 1)
                    inverse_root(2 + tok, 1, D, post_rstd)
                    pool.wait_ge(post_rstd, TOK * n + tok + 1)
            roots1, roots_layer = jobs.base, 2 + 2 + 6 + 1
            with pool.Fori(0, LAYERS) as l:
                jobs = At(roots1, l, roots_layer)
                pre_norm(At(3 * TOK, l, TOK))

                def dil(j):
                    pool.wait_ge(dil_sums, At(j + 1, l, 6).value)
                    inverse_root(8 + 16 * (j % 2), 16, HEAD, dil_rstd)
                    pool.wait_ge(dil_rstd, At(j + 1, l, 6).value)

                pool.wait_ge(lora_squares, At(1, l, 1).value)
                inverse_root(4, 2, 256, lora_rstd)
                pool.wait_ge(lora_rstd, At(1, l, 2).value)
                inverse_root(6, 2, 128, lora_rstd)
                pool.wait_ge(lora_rstd, At(2, l, 2).value)
                for j in range(3):
                    dil(j)
                pool.wait_ge(mla_sums, At(1, l, 1).value)
                inverse_root(40, 32, QK, mla_rstd)
                pool.wait_ge(mla_rstd, At(1, l, 1).value)
                for j in range(3, 6):
                    dil(j)
                assert jobs.base == roots1 + roots_layer

        @block.scalar
        def _(act):
            step = Steps(act, act_step)

            def split_hi(t):
                if not t.first:
                    act.wait_ge(weights_used, (t + (1 - RING)).value)
                act.wait_ge(raw_loaded[t.slot], t.loaded)
                act.activation(w_hi[:, t.slot, :], raw[:, t.slot, :], ACT.Copy).then_inc(hi_ready, 1)

            def pre_norm(n, gain, ready=None):
                for tok in range(TOK):
                    act.activation(norm[:, tok, :], res[:, tok, :], ACT.Square,
                                   accum_out=squares[:, tok:tok + 1]).then_inc(squares_ready, 1)
                act.wait_ge(norm_turned, (n + TOK).value)
                for k in range(KD):
                    act.activation(x_hi[:, k, :], wide(4, 2048)[:, k * SEQ:(k + 1) * SEQ], ACT.Copy,
                                   scale=gain[:, k:k + 1]).then_inc(norm_hi, 1)

            def post_norm(n, last):
                act.wait_ge(weights_used, last)
                for tok in range(TOK):
                    act.activation(norm[:, tok, :], wide(4 + 2 * tok, D), ACT.Square,
                                   accum_out=squares[:, 2 + tok:3 + tok]).then_inc(post_squares, 1)

            def load_gain(n):
                act.dma_start(gain_row, gains[n, :, :]).then_inc(gain_loaded, 16)

            def swish(at, i):
                act.wait_ge(weights_used, at.value)
                for tok in range(TOK):
                    act.activation(ff_t[:, tok, :], psum[:, tok, 0:FF_STEP], ACT.Tanh, scale=0.5
                                   ).then_inc(swish_tanh, 1)

            def hidden_copy(n):
                act.wait_ge(hidden_turned, n.value)
                act.activation(y1_hi[:, 0:2, :].rearrange("p a s -> p (a s)"), psum[:, 2, :], ACT.Copy
                               ).then_inc(hidden_hi, 1)

            def ffn(f, base):
                for j in range(LOOK, 4):
                    split_hi(At(base + j))
                swish(At(base + 4), 0)
                split_hi(At(base + 4))
                split_hi(At(base + 5))
                with act.Fori(1, FF_STEPS) as i:
                    t = At(base - 2, i, 6)
                    hidden_copy(At(f * FF_STEPS, i, 1))
                    for j in range(4):
                        split_hi(t + (j + LOOK))
                    swish(t + 4, i)
                    split_hi(t + (4 + LOOK))
                    split_hi(t + (5 + LOOK))
                hidden_copy(At((f + 1) * FF_STEPS))
                split_hi(At(base + FFN_TILES))
                split_hi(At(base + FFN_TILES + 1))
                post_norm(f, base + FFN_TILES)

            def exps(u, rows):
                act.wait_ge(max_ready, u.value)
                for n, (lo, hi, col) in enumerate(rows):
                    ins = act.activation(probs[:, lo:hi], probs[:, lo:hi], ACT.Exp,
                                         bias=scores_max[:, n:n + 1], accum_out=scores_sum[:, col:col + 1])
                ins.then_inc(exp_done, 1)

            def probs_copy(u):
                act.wait_ge(probs_turned, u.value)
                act.activation(probs_t[:, 0:512], psum[:, 4, :], ACT.Copy).then_inc(probs_act, 1)

            def chunk_done(at):
                act.wait_ge(weights_used, at.value)

            for dst, src in ((cst[:, :], consts), (par, params1),
                             (sel_stage, selectors)):
                act.dma_start(dst, src).then_inc(small_loaded, 16)
            load_gain(0)
            act.wait_ge(x_loaded, 16)
            act.wait_ge(small_loaded, 48)
            step.link(act.activation(sel_r[:, :], sel_stage, ACT.Copy))
            step.link(act.activation(soft[:, 0, :], par[:, B_LAM:B_LAM + KD], ACT.Abs))
            act.activation(soft[:, 1, :], soft[:, 0, :], ACT.Exp, scale=-1.0).then_inc(abs_exp, 1)
            split_hi(At(0))
            split_hi(At(1))

            pre_norm(At(0), par[:, B_FFN1:B_FFN1 + KD])
            ffn(0, FFN1_AT)

            act.wait_ge(x_ready, 2)
            act.dma_start(lru_blocks.rearrange("p a f d -> p (a f d)"), lru_w).then_inc(lru_loaded, 16)
            pre_norm(At(TOK), par[:, B_MIX:B_MIX + KD])
            rows1 = [[(j * P * (qt + 1), (j + 1) * P * (qt + 1), qt * Q_HEADS + h)
                      for j, h in enumerate(heads)] for qt, heads in UNITS1]

            def sink_part(u):
                qt, heads = UNITS1[u]
                cols = slice(qt * Q_HEADS + min(heads), qt * Q_HEADS + min(heads) + len(heads))
                act.activation(sink_exp[:, cols], sum_recip[:, cols], ACT.Exp).then_inc(sink_done, 1)

            def tanh_part(half, which):
                act.wait_ge(ri_ready, 2 * half + which + 1)
                fill = (F_R0, F_I0, F_R1, F_I1)[2 * half + which]
                dst = lru_i if which else lru_a
                for j in range(4):
                    f = 4 * half + j
                    ins = act.activation(dst[:, f, :], pair(fill)[:, j // 2, (j % 2) * SEQ:(j % 2 + 1) * SEQ],
                                         ACT.Tanh, scale=0.5, bias=half_bias[:, which * KD + f:which * KD + f + 1])
                ins.then_inc(act_freed, 1)

            for c in range(MIX_CHUNKS):
                t = At(MIX_AT + 4 * c)
                u = c - 6
                if c == 5:
                    act.wait_ge(qk_turned, 1)
                    act.activation(q_t[:, 0:4, :].rearrange("p a s -> p (a s)"), wide(4, 1024), ACT.Copy,
                                   scale=HEAD ** -0.5).then_inc(q_copied, 1)
                if 0 <= u - 1 < len(UNITS1):
                    probs_copy(At(u))
                split_hi(t + LOOK)
                if 1 <= c <= 11:
                    chunk_done(t)
                if c == 1:
                    act.activation(kv_tok, pair(F_KV), ACT.Copy).then_inc(act_freed, 1)
                if c in (2, 3):
                    h = c - 2
                    act.activation(q_tok[:, :, h * 512:(h + 1) * 512], pair(F_Q0 + h), ACT.Copy).then_inc(act_freed, 1)
                if c in (4, 5):
                    h = c - 4
                    act.activation(xb[:, 4 * h:4 * h + 4, CONV1 - 1:XB_W],
                                   pair(F_XB0 + h).rearrange("p b (f s) -> p (b f) s", s=SEQ), ACT.Copy
                                   ).then_inc(act_freed, 1)
                if c in (6, 7):
                    h = c - 6
                    act.activation(gelu[:, 4 * h:4 * h + 4, :],
                                   pair(F_GATE0 + h).rearrange("p b (f s) -> p (b f) s", s=SEQ), ACT.Copy
                                   ).then_inc(act_freed, 1)
                if c == 7:
                    tanh_part(0, 0)
                    tanh_part(0, 1)
                if 8 <= c <= 11:
                    j = c - 8
                    act.activation(gate_t[:, j // 2, :, (j % 2) * 512:(j % 2 + 1) * 512],
                                   pair((F_GL0, F_GL1, F_GA0, F_GA1)[j]), ACT.Tanh, scale=0.5).then_inc(act_freed, 1)
                if c == 5:
                    act.wait_ge(qk_turned, 2)
                    act.activation(k_t.rearrange("p a s -> p (a s)"), psum[:, 4, :], ACT.Copy).then_inc(k_copied, 1)
                if c == 8:
                    tanh_part(1, 0)
                    tanh_part(1, 1)
                split_hi(t + (1 + LOOK))
                if 0 <= u < len(UNITS1):
                    exps(At(u + 1), rows1[u])
                    sink_part(u)
                split_hi(t + (2 + LOOK))
                if c == 8:
                    act.wait_ge(gelu_arg, 1)
                    act.activation(lru_e.rearrange("p f s -> p (f s)"), lru_e.rearrange("p f s -> p (f s)"),
                                   ACT.Tanh).then_inc(gelu_tanh, 1)
                    for f in range(KD):
                        ins = act.activation(lru_tl[:, f, :], lru_a[:, f, :], ACT.Tanh, scale=c4[:, f:f + 1],
                                             bias=c4[:, f:f + 1])
                    ins.then_inc(tl_ready, 1)
                    act.wait_ge(tl_ready, 1)
                    for f in range(KD):
                        ins = act.activation(lru_a[:, f, :], lru_a[:, f, :], ACT.Exp, scale=c4[:, f:f + 1],
                                             bias=c4[:, f:f + 1])
                    ins.then_inc(decay_ready, 1)
                split_hi(t + (3 + LOOK))
                if c == 9:
                    load_gain(1)
                    act.wait_ge(sqrt_arg, 1)
                    flat = lru_e.rearrange("p f s -> p (f s)")
                    act.activation(flat, flat, ACT.Sqrt, scale=0.25).then_inc(sqrt_done, 1)
                if c == 10:
                    act.wait_ge(lru_ready, 1)
                    act.activation(y1_hi[:, :, :], gelu, ACT.Copy, scale=0.5).then_inc(lru_hi, 1)
                if c == 12:
                    act.wait_ge(heads_turned, 1)
                    act.activation(y2_hi[:, :, :].rearrange("p f s -> p (f s)"), wide(4, 2048), ACT.Copy
                                   ).then_inc(heads_hi, 1)
                if c == 14:
                    act.wait_ge(merged_turned, 1)
                    act.activation(x_hi[:, :, :].rearrange("p f s -> p (f s)"), wide(4, 2048), ACT.Copy, scale=0.5
                                   ).then_inc(merged_hi, 1)
            post_norm(1, MIX_AT + MIX_TILES)

            act.wait_ge(x_ready, 4)
            load_gain(2)
            pre_norm(At(2 * TOK), par[:, B_FFN2:B_FFN2 + KD])
            ffn(1, FFN2_AT)

            act.wait_ge(x_ready, 6)
            step.restart()
            with act.Fori(0, LAYERS) as l:
                base = At(LAYER_AT, l, LAYER_TILES)
                act.wait_ge(x_ready, At(6, l, 2).value)
                act.dma_start(lp, layer_params[bass.ds(l, 1), :, :].rearrange("a p n -> (a p) n")
                              ).then_inc(layer_loaded, 16)
                act.dma_start(bias_stage,
                              gate_bias[bass.ds(l, 1), :, :].rearrange("a p n -> (a p) n")
                              ).then_inc(layer_loaded, 16)
                act.wait_ge(layer_loaded, At(32, l, 32).value)
                pre_norm(At(3 * TOK, l, TOK), lp[:, L_NORM:L_NORM + KD])
                act.activation(bias_hi[:, :], bias_stage, ACT.Copy).then_inc(bias_split, 1)
                rows_mla = [[(j * P * (qt + 1), (j + 1) * P * (qt + 1), qt * MLA_HEADS + h)
                             for j, h in enumerate(heads)] for qt, heads in UNITS_MLA]
                rows_dil = [[(j * 3 * P * (qt + 1), (j + 1) * 3 * P * (qt + 1), qt * DIL_HEADS + h)
                             for j, h in enumerate(heads)] for qt, heads in DIL_UNITS]
                rows2 = rows_mla + rows_dil
                UB = len(UNITS1)

                def dil_chunk(j):
                    z = norm[:, (j + 1) % 2, :].rearrange("p (t n) -> p t n", t=TOK)
                    if j:
                        act.wait_ge(dil_sums, At(j, l, 6).value)
                    act.activation(probs[:, :].rearrange("p (t n) -> p t n", t=TOK), pair(fill_of(1 + j)), ACT.Square
                                   ).then_inc(dil_squares, 1)
                    if j >= 2:
                        act.wait_ge(dil_turned, At(j - 1, l, 6).value)
                    if j == 1:
                        act.wait_ge(lora_turned, At(1, l, 1).value)
                    act.activation(z, pair(fill_of(1 + j)), ACT.Copy).then_inc(act_freed, 1)

                def dil_copy(j):
                    act.wait_ge(dil_turned, At(j + 1, l, 6).value)
                    dst, g = (dil_q, j) if j < 3 else (dil_k, j - 3)
                    gain = lp[:, (L_DQ, L_DK)[j // 3] + g:(L_DQ, L_DK)[j // 3] + g + 1]
                    act.activation(dst[:, 4 * g:4 * g + 4, :].rearrange("p f s -> p (f s)"), wide(4, 1024), ACT.Copy,
                                   scale=gain).then_inc(dil_copied, 1)

                for c in range(LAYER_CHUNKS + 2):
                    t = chunk_at(base, c)
                    u = c - 9
                    if 1 <= u:
                        probs_copy(At(UB + u, l, UNITS_LAYER))
                    if 4 <= c <= 8:
                        dil_copy(c - 3)
                    split_hi(t + LOOK)
                    if c == 3:
                        chunk_done(t)
                        up = psum[:, 4:8, :].rearrange("p b (h n) -> p (b h) n", n=P)
                        act.activation(qk[:, :, MLA_HEADS:, 0:NOPE],
                                       up[:, :, 0:NOPE].rearrange("p (t h) n -> p t h n", t=TOK), ACT.Copy
                                       ).then_inc(up_copied, 1)
                        act.activation(mla_v.rearrange("p t (h n) -> p (t h) n", n=HEAD), up[:, :, NOPE:P],
                                       ACT.Copy).then_inc(up_copied, 1)
                    if c and c != 3 and c < LAYER_CHUNKS + 1:
                        chunk_done(t)
                    if c == 1:
                        z = norm[:, 0, :].rearrange("p (t n) -> p t n", t=TOK)
                        for n, (lo, hi) in enumerate(((0, 256), (256, 384))):
                            for tok in range(TOK):
                                ins = act.activation(z[:, tok, lo:hi], pair(0)[:, tok, lo:hi], ACT.Square,
                                                     accum_out=squares[:, 4 + 2 * n + tok:5 + 2 * n + tok])
                                step.mark(ins)
                        step.sync()
                        act.activation(z[:, :, 0:416], pair(0)[:, :, 0:416], ACT.Copy).then_inc(act_freed, 1)
                        act.sem_inc(lora_squares, 1)
                    if c == 2:
                        dil_chunk(0)
                    if 4 <= c <= 7:
                        dil_chunk(c - 2)
                    if 8 <= c <= 10:
                        act.activation(dil_v[:, c - 8, :, :], pair(fill_of(c - 1)), ACT.Copy).then_inc(act_freed, 1)
                    if c in (11, 12):
                        z = norm[:, c - 11, :].rearrange("p (t n) -> p t n", t=TOK)
                        act.activation(z, pair(fill_of(c - 1)), ACT.Tanh, scale=0.5).then_inc(silu_tanh, 1)
                    if c == 13:
                        act.wait_ge(values_ready, At(UB + 3, l, UNITS_LAYER).value)
                        act.activation(a_c, pair(fill_of(c - 1)).rearrange("p b (f s) -> p (b f) s", s=SEQ), ACT.Copy
                                       ).then_inc(act_freed, 1)
                    if c == 16:
                        act.activation(a_z, pair(fill_of(c - 1)).rearrange("p b (f s) -> p (b f) s", s=SEQ), ACT.Tanh,
                                       scale=0.5).then_inc(silu_tanh, 1)
                    if 17 <= c <= 22:
                        i = c - 17
                        act.activation(ga_t[:, i // 2, :, (i % 2) * 512:(i % 2 + 1) * 512], pair(fill_of(c - 1)),
                                       ACT.Tanh, scale=0.5).then_inc(act_freed, 1)
                    if c == 8:
                        for r in range(2):
                            act.wait_ge(mla_turned, At(r + 1, l, 4).value)
                            act.activation(mla_t[0:QK, 4 * r:4 * r + 4, :].rearrange("p h s -> p (h s)"),
                                           wide((6, 4)[r % 2], 1024)[0:QK, :], ACT.Copy).then_inc(mla_copied, 1)
                    split_hi(t + (1 + LOOK))
                    if c == 2:
                        act.wait_ge(lora_turned, At(1, l, 1).value)
                        for k in range(3):
                            gain = lp[:, L_QA + k:L_QA + k + 1]
                            act.activation(y2_hi[:, 4 + k, :], wide(4, 1024)[:, k * SEQ:(k + 1) * SEQ], ACT.Copy,
                                           scale=gain).then_inc(lora_hi, 1)
                    if c == 4:
                        act.activation(qk_sq, qk, ACT.Square).then_inc(mla_squares, 1)
                    if c == 8:
                        for r in range(2, 4):
                            act.wait_ge(mla_turned, At(r + 1, l, 4).value)
                            act.activation(mla_t[0:QK, 4 * r:4 * r + 4, :].rearrange("p h s -> p (h s)"),
                                           wide((6, 4)[r % 2], 1024)[0:QK, :], ACT.Copy).then_inc(mla_copied, 1)
                    if 0 <= u:
                        exps(At(UB + u + 1, l, UNITS_LAYER), rows2[u])
                    split_hi(t + (2 + LOOK))
                    split_hi(t + (3 + LOOK))
                    if c == 2:
                        dil_copy(0)
                        chunk_done(t + 4)
                        dil_chunk(1)
                        split_hi(t + (4 + LOOK))
                        split_hi(t + (5 + LOOK))
                        chunk_done(t + 6)
                        for tok in range(TOK):
                            act.activation(qk[:, tok, 0:MLA_HEADS, :].rearrange("p h n -> p (h n)"),
                                           wide(2 * ((3 + tok) % 2), MLA_HEADS * QK), ACT.Copy).then_inc(act_freed, 1)
                        split_hi(t + (6 + LOOK))
                    if c == 14:
                        act.wait_ge(heads_turned, At(2, l, 2).value)
                        act.activation(y1_hi[:, 4:8, :].rearrange("p f s -> p (f s)"), wide(4, 1024), ACT.Copy,
                                       scale=0.5).then_inc(heads_hi, 1)
                    if c == 17:
                        act.wait_ge(ya_ready, At(1, l, 1).value)
                        act.activation(y1_hi[:, 0:4, :], a_z, ACT.Copy, scale=0.5).then_inc(ya_hi, 1)
                t = chunk_at(base, LAYER_CHUNKS + 2)
                probs_copy(At(UB + UNITS_LAYER, l, UNITS_LAYER))
                act.wait_ge(heads_turned, At(3, l, 2).value)
                act.activation(y2_hi[:, 0:4, :].rearrange("p f s -> p (f s)"), wide(4, 1024), ACT.Copy,
                               scale=0.5).then_inc(heads_hi, 1)
                for j in range(4):
                    split_hi(t + (j + LOOK))
                act.wait_ge(merged_turned, At(2, l, 1).value)
                act.activation(x_hi[:, :, :].rearrange("p f s -> p (f s)"), wide(4, 2048), ACT.Copy, scale=0.5
                               ).then_inc(merged_hi, 1)
                for j in range(4, 12):
                    split_hi(t + (j + LOOK))
                step.restart()

        @block.vector
        def _(dve):
            step = Steps(dve, dve_step)

            def split_lo(t):
                dve.wait_ge(hi_ready, (t + 1).value)
                dve.tensor_tensor(w_lo[:, t.slot, :], raw[:, t.slot, :], w_hi[:, t.slot, :].bitcast(F32),
                                  ALU.subtract).then_inc(lo_ready, 1)

            def rest(out_, in_, scale, hi):
                return dve.scalar_tensor_tensor(out_, in_, scale, hi.bitcast(F32), ALU.mult, ALU.subtract)

            def pre_norm(n, gain):
                for tok in range(TOK):
                    dve.wait_ge(rstd_ready, (n * TOK + (1 + tok)).value)
                    dve.tensor_scalar(norm[:, tok, :], res[:, tok, :], rstd[:, tok:tok + 1], None, ALU.mult
                                      ).then_inc(normed, 1)
                for k in range(KD):
                    dve.wait_ge(norm_hi, (n * KD + 2 * (1 + k // 2)).value)
                    rest(x_lo[:, k, :], wide(4, 2048)[:, k * SEQ:(k + 1) * SEQ], gain[:, k:k + 1], x_hi[:, k, :]
                         ).then_inc(norm_lo, 1)

            def post_norm(n, scale):
                dve.wait_ge(gain_loaded, 16 * (n + 1))
                for tok in range(TOK):
                    dve.wait_ge(post_rstd, TOK * n + tok + 1)
                    step.link(dve.scalar_tensor_tensor(norm[:, tok, :], wide(4 + 2 * tok, D), rstd[:, 2 + tok:3 + tok],
                                                       gain_row, ALU.mult, ALU.mult))
                    dve.scalar_tensor_tensor(res[:, tok, :], norm[:, tok, :], scale, res[:, tok, :],
                                             ALU.mult, ALU.add).then_inc(x_ready, 1)

            def swiglu(n):
                for tok in range(TOK):
                    dve.wait_ge(swish_tanh, (n * TOK + (1 + tok)).value)
                    dve.scalar_tensor_tensor(ff_a[:, tok, :], ff_t[:, tok, :], 1.0, psum[:, tok, 0:FF_STEP],
                                             ALU.add, ALU.mult).then_inc(half_swish, 1)
                for tok in range(TOK):
                    dve.wait_ge(half_swish, (n * TOK + (1 + tok)).value)
                    dve.scalar_tensor_tensor(ff_a[:, tok, :], ff_a[:, tok, :], 0.5,
                                             psum[:, tok, FF_STEP:2 * FF_STEP], ALU.mult, ALU.mult
                                             ).then_inc(hidden_ready, 1)

            def hidden_rest(n):
                dve.wait_ge(hidden_hi, n.value)
                dve.tensor_tensor(y1_lo[:, 0:2, :].rearrange("p a s -> p (a s)"), psum[:, 2, :],
                                  y1_hi[:, 0:2, :].rearrange("p a s -> p (a s)").bitcast(F32),
                                  ALU.subtract).then_inc(hidden_lo, 1)

            def ffn(f, base):
                for j in range(LOOK, 4):
                    split_lo(At(base + j))
                swiglu(At(f * FF_STEPS))
                split_lo(At(base + 4))
                split_lo(At(base + 5))
                with dve.Fori(1, FF_STEPS) as i:
                    t = At(base - 2, i, 6)
                    hidden_rest(At(f * FF_STEPS, i, 1))
                    for j in range(4):
                        split_lo(t + (j + LOOK))
                    swiglu(At(f * FF_STEPS, i, 1))
                    split_lo(t + (4 + LOOK))
                    split_lo(t + (5 + LOOK))
                hidden_rest(At((f + 1) * FF_STEPS))
                split_lo(At(base + FFN_TILES))
                split_lo(At(base + FFN_TILES + 1))
                post_norm(2 * f, 0.5)

            def rows(n, width):
                return probs[:, 0:n * width].rearrange("p (h s) -> p h s", h=n)

            def mask_scores(u, qt, n, mask):
                width = P * (qt + 1)
                dve.wait_ge(scores_ready, u.value)
                step.link(dve.tensor_tensor(rows(n, width), wide(4, n * width).rearrange("p (h s) -> p h s", h=n),
                                            mask[:, SEQ - width:].unsqueeze(1).broadcast_to([P, n, width]), ALU.add))

            def negated_max(n, width):
                return dve.tensor_reduce(scores_max[:, 0:n], rows(n, width), AX.X, ALU.max, negate=True)

            def probs_copy(u, blocks):
                dve.wait_ge(probs_turned, u.value)
                n = (blocks - 4) * P
                dve.tensor_copy(probs_t[:, 512:512 + n], psum[:, 5, 0:n]).then_inc(probs_dve, 1)

            def recip_sums(lo, hi):
                step.link(dve.reciprocal(sum_recip[:, lo:hi], scores_sum[:, lo:hi]))

            def divide_rows(out_, in_, heads, lo):
                return dve.tensor_tensor(out_.rearrange("p (h n) -> p h n", h=heads),
                                         in_.rearrange("p (h n) -> p h n", h=heads),
                                         sum_recip[:, lo:lo + heads].unsqueeze(2).broadcast_to([P, heads, HEAD]),
                                         ALU.mult)

            def rotate(first, second, cos, sin, temps):
                shape = list(first.shape)
                tmp = [t_.rearrange("p (a b) -> p a b", b=shape[-1]) if len(shape) == 3 else
                       t_.rearrange("p (a b c) -> p a b c", a=shape[1], b=shape[2]) for t_ in temps]
                for dst, a, b in ((0, first, cos), (1, second, sin), (2, second, cos), (3, first, sin)):
                    step.mark(dve.tensor_tensor(tmp[dst], a, b, ALU.mult))
                step.sync()
                step.mark(dve.tensor_tensor(first, tmp[0], tmp[1], ALU.subtract))
                step.mark(dve.tensor_tensor(second, tmp[2], tmp[3], ALU.add))
                step.sync()

            dve.wait_ge(small_loaded, 48)
            dve.tensor_scalar(half_bias, par[:, B_BA:B_BA + 2 * KD], 0.5, None, ALU.mult).then_inc(fold_ready, 1)
            dve.wait_ge(abs_exp, 1)
            e, two_e, t_, t2, poly = (soft[:, j, :] for j in range(1, 6))
            step.link(dve.tensor_scalar(two_e, e, 2.0, None, ALU.add))
            step.link(dve.reciprocal(two_e, two_e))
            step.link(dve.tensor_tensor(t_, e, two_e, ALU.mult))
            step.link(dve.tensor_tensor(t2, t_, t_, ALU.mult))
            step.link(dve.tensor_scalar(poly, t2, 1.0 / 17.0, 1.0 / 15.0, ALU.mult, ALU.add))
            for odd in range(13, 0, -2):
                step.link(dve.tensor_tensor(poly, poly, t2, ALU.mult))
                step.link(dve.tensor_scalar(poly, poly, 1.0 / odd, None, ALU.add))
            step.link(dve.tensor_tensor(poly, poly, t_, ALU.mult))
            step.link(dve.tensor_scalar(t_, par[:, B_LAM:B_LAM + KD], -1.0, 0.0, ALU.mult, ALU.max))
            step.link(dve.scalar_tensor_tensor(t_, poly, 2.0, t_, ALU.mult, ALU.add))
            dve.tensor_scalar(c4, t_, -0.5 * LRU_C, None, ALU.mult).then_inc(fold_ready, 1)
            split_lo(At(0))
            split_lo(At(1))

            pre_norm(At(0), par[:, B_FFN1:B_FFN1 + KD])
            ffn(0, FFN1_AT)

            pre_norm(At(1), par[:, B_MIX:B_MIX + KD])
            temps = [probs[:, 0:512], probs[:, 512:], probs_t[:, 0:512], probs_t[:, 512:]]

            def rotate_q(tok):
                q = q_tok[:, tok, :].rearrange("p (h n) -> p h n", h=Q_HEADS)
                c_, s_ = (rope1[:, j, tok, :].unsqueeze(1).broadcast_to([P, Q_HEADS, HALF]) for j in range(2))
                rotate(q[:, :, 0:HALF], q[:, :, HALF:], c_, s_, temps)

            def conv1(half):
                dve.wait_ge(*freed(F_XB0 + half))
                fs = range(4 * half, 4 * half + 4)
                w = par[:, B_CONVW:B_CONVW + CONV1 * KD]
                for f in fs:
                    step.mark(dve.tensor_scalar(xc[:, f, :], xb[:, f, 0:SEQ], w[:, f:f + 1],
                                                par[:, B_CONVB + f:B_CONVB + f + 1], ALU.mult, ALU.add))
                for tap in range(1, CONV1):
                    step.sync()
                    for f in fs:
                        ins = dve.scalar_tensor_tensor(xc[:, f, :], xb[:, f, tap:tap + SEQ],
                                                       w[:, tap * KD + f:tap * KD + f + 1], xc[:, f, :],
                                                       ALU.mult, ALU.add)
                        if tap < CONV1 - 1:
                            step.mark(ins)
                ins.then_inc(conv_done, 1)

            def recip_part(qt):
                part = slice(qt * Q_HEADS, (qt + 1) * Q_HEADS)
                dve.wait_ge(sink_done, (2, 6)[qt])
                step.link(dve.tensor_tensor(scores_sum[:, part], scores_sum[:, part], sink_exp[:, part], ALU.add))
                recip_sums(qt * Q_HEADS, (qt + 1) * Q_HEADS)

            def flat(v):
                return v.rearrange("p f s -> p (f s)")

            def gated(dst, gate, fill):
                return dve.scalar_tensor_tensor(dst, gate, 1.0, pair(fill), ALU.add, ALU.mult)

            for c in range(MIX_CHUNKS):
                t = At(MIX_AT + 4 * c)
                u = c - 6
                if 0 <= u - 1 < len(UNITS1):
                    probs_copy(At(u), 8)
                if c == 5:
                    dve.wait_ge(qk_turned, 1)
                    dve.tensor_scalar(flat(q_t[:, 4:8, :]), wide(6, 1024), HEAD ** -0.5, None, ALU.mult
                                      ).then_inc(q_copied_b, 1)
                split_lo(t + LOOK)
                if 0 <= u < len(UNITS1):
                    qt, heads = UNITS1[u]
                    n = len(heads)
                    mask_scores(At(u + 1), qt, n, mask_window)
                    step.link(negated_max(n, P * (qt + 1)))
                    h0, col = B_SINK + min(heads), qt * Q_HEADS + min(heads)
                    sink = par[:, h0:h0 + n].rearrange("p (a b) -> p b a", b=2)
                    top = scores_max[:, 0:n].rearrange("p (b a) -> p b a", b=2)
                    over = sum_recip[:, col:col + n].rearrange("p (a b) -> p b a", b=2)
                    step.link(dve.scalar_tensor_tensor(top, sink, -1.0, top, ALU.mult, ALU.min))
                    dve.tensor_tensor(over, sink, top, ALU.add).then_inc(max_ready, 1)
                if c == 3:
                    rotate_q_ready = freed(F_Q1)
                    dve.wait_ge(*rotate_q_ready)
                    rotate_q(0)
                split_lo(t + (1 + LOOK))
                if c == 0:
                    step.link(dve.memset(xb[:, :, 0:CONV1 - 1], 0.0))
                if c == 1:
                    dve.wait_ge(*freed(F_KV))
                    k_ = kv_tok[:, :, 0:KV_HEADS * HEAD].rearrange("p t (h n) -> p t h n", h=KV_HEADS)
                    c_, s_ = (rope1[:, j, :, :].unsqueeze(2).broadcast_to([P, TOK, KV_HEADS, HALF]) for j in range(2))
                    rotate(k_[:, :, :, 0:HALF], k_[:, :, :, HALF:], c_, s_, [x_[:, 0:256] for x_ in temps])
                if c == 4:
                    rotate_q(1)
                    dve.sem_inc(rope_ready, 1)
                if c == 5:
                    conv1(0)
                if c == 6:
                    conv1(1)
                split_lo(t + (2 + LOOK))
                if c == 7:
                    dve.wait_ge(*freed(F_GATE1))
                    step.link(dve.tensor_tensor(lru_e, gelu, gelu, ALU.mult))
                    step.link(dve.tensor_scalar(flat(lru_e), flat(lru_e), GELU_C * 0.044715, GELU_C,
                                                ALU.mult, ALU.add))
                    dve.tensor_tensor(lru_e, lru_e, gelu, ALU.mult).then_inc(gelu_arg, 1)
                if c == 9:
                    dve.wait_ge(gelu_tanh, 1)
                    step.link(dve.scalar_tensor_tensor(gelu, lru_e, 1.0, gelu, ALU.add, ALU.mult))
                    dve.wait_ge(decay_ready, 1)
                    step.link(dve.tensor_tensor(flat(lru_e), flat(lru_a), flat(lru_a), ALU.mult))
                    step.link(dve.scalar_tensor_tensor(flat(lru_e), flat(lru_e), 1.0, flat(lru_tl), ALU.add, ALU.mult))
                    dve.tensor_scalar(flat(lru_e), flat(lru_e), -1.0, 0.0, ALU.mult, ALU.max).then_inc(sqrt_arg, 1)
                split_lo(t + (3 + LOOK))
                if c == 9:
                    dve.wait_ge(values_ready, 2)
                    recip_part(0)
                    divide_rows(heads1[:, 0, :], wide(6, 1024), Q_HEADS, 0).then_inc(values_read, 1)
                    dve.wait_ge(*freed(F_I1))
                    step.link(dve.scalar_tensor_tensor(flat(lru_i), flat(lru_i), 1.0, flat(xc), ALU.add, ALU.mult))
                if c == 10:
                    dve.wait_ge(sqrt_done, 1)
                    step.link(dve.tensor_tensor(flat(lru_i), flat(lru_i), flat(lru_e), ALU.mult))
                    for f in range(KD):
                        step.mark(dve.tensor_tensor_scan(xc[:, f, :], lru_a[:, f, :], lru_i[:, f, :], 0.0,
                                                         ALU.mult, ALU.add))
                    step.sync()
                    dve.tensor_tensor(gelu, gelu, xc, ALU.mult).then_inc(lru_ready, 1)
                    dve.wait_ge(lru_hi, 1)
                    dve.wait_ge(lru_ready, 1)
                    rest(y1_lo[:, :, :], gelu, 0.5, y1_hi[:, :, :]).then_inc(lru_lo, 1)
                if c in (12, 13):
                    h = c - 12
                    dve.wait_ge(weights_used, t.value)
                    gated(merged1[:, :, h * 512:(h + 1) * 512], gate_t[:, 0, :, h * 512:(h + 1) * 512], F_PL0 + h
                          ).then_inc(dve_freed, 1)
                if c == 12:
                    dve.wait_ge(values_ready, 6)
                    recip_part(1)
                    divide_rows(heads1[:, 1, :], wide(6, 1024), Q_HEADS, Q_HEADS).then_inc(values_read, 1)
                    dve.wait_ge(heads_hi, 1)
                    dve.tensor_tensor(flat(y2_lo[:, :, :]), wide(4, 2048), flat(y2_hi[:, :, :]).bitcast(F32),
                                      ALU.subtract).then_inc(heads_lo, 1)
                if c == 14:
                    for h in range(2):
                        dve.wait_ge(weights_used, (t + 4 * h).value)
                        part = slice(h * 512, (h + 1) * 512)
                        gated(merge_tmp1, gate_t[:, 1, :, part], F_PA0 + h).then_inc(dve_freed, 1)
                        dve.wait_ge(*freed(F_PA0 + h))
                        ins = dve.tensor_tensor(merged1[:, :, part], merged1[:, :, part], merge_tmp1, ALU.add)
                        if h:
                            ins.then_inc(merged_ready, 1)
                        else:
                            step.link(ins)
                    dve.wait_ge(merged_hi, 1)
                    rest(flat(x_lo[:, :, :]), wide(4, 2048), 0.5, flat(x_hi[:, :, :])).then_inc(merged_lo, 1)
            post_norm(1, 1.0)

            pre_norm(At(2), par[:, B_FFN2:B_FFN2 + KD])
            ffn(1, FFN2_AT)

            step.restart()
            with dve.Fori(0, LAYERS) as l:
                base = At(LAYER_AT, l, LAYER_TILES)
                dve.wait_ge(layer_loaded, At(32, l, 32).value)
                step.mark(dve.tensor_scalar(lp[:, L_DQ:L_DQ + 3], lp[:, L_DQ:L_DQ + 3], HEAD ** -0.5, None, ALU.mult))
                step.mark(dve.tensor_scalar(lp[:, L_GQ:L_GQ + QK], lp[:, L_GQ:L_GQ + QK], QK ** -0.5, None, ALU.mult))
                pre_norm(At(3, l, 1), lp[:, L_NORM:L_NORM + KD])
                dve.wait_ge(bias_split, At(1, l, 1).value)
                dve.tensor_tensor(bias_lo[:, :], bias_stage, bias_hi[:, :].bitcast(F32), ALU.subtract
                                  ).then_inc(bias_rest, 1)

                def z_of(n):
                    return norm[:, n, :].rearrange("p (t n) -> p t n", t=TOK)

                def dil_sum(j):
                    dve.wait_ge(dil_squares, At(j + 1, l, 6).value)
                    at = 8 + 16 * (j % 2)
                    dve.tensor_reduce(squares[:, at:at + 16], probs[:, :].rearrange("p (h n) -> p h n", n=HEAD), AX.X,
                                      ALU.add).then_inc(dil_sums, 1)

                def dil_norm(j):
                    at = 8 + 16 * (j % 2)
                    dve.wait_ge(dil_rstd, At(j + 1, l, 6).value)
                    dve.wait_ge(*freed(fill_of(1 + j), l))
                    z = norm[:, (j + 1) % 2, :].rearrange("p (h n) -> p h n", n=HEAD)
                    dve.tensor_tensor(z, z, rstd[:, at:at + 16].unsqueeze(2).broadcast_to([P, 16, HEAD]), ALU.mult
                                      ).then_inc(dil_normed, 1)

                def slow(v):
                    return v.rearrange("p f s -> p (f s)")

                def add_product(m, h):
                    part = slice(h * 512, (h + 1) * 512)
                    fill = fill_of(LAYER_CHUNKS) + 2 * m + h
                    if m == 0:
                        gated(merged2[:, :, part], ga_t[:, 0, :, part], fill).then_inc(dve_freed, 1)
                        return
                    gated(merge_tmp2, ga_t[:, m, :, part], fill).then_inc(dve_freed, 1)
                    dve.wait_ge(*freed(fill, l))
                    ins = dve.tensor_tensor(merged2[:, :, part], merged2[:, :, part], merge_tmp2, ALU.add)
                    if m == 2 and h == 1:
                        ins.then_inc(merged_ready, 1)
                    else:
                        step.link(ins)

                UB = len(UNITS1)
                for c in range(LAYER_CHUNKS + 2):
                    t = chunk_at(base, c)
                    u = c - 9
                    if 1 <= u:
                        probs_copy(At(UB + u, l, UNITS_LAYER), 8 if u <= len(UNITS_MLA) else 6)
                    split_lo(t + LOOK)
                    if 0 <= u:
                        un = At(UB + u + 1, l, UNITS_LAYER)
                        if u < len(UNITS_MLA):
                            qt, heads = UNITS_MLA[u]
                            mask_scores(un, qt, len(heads), mask_causal)
                            negated_max(len(heads), P * (qt + 1)).then_inc(max_ready, 1)
                        else:
                            qt, heads = DIL_UNITS[u - len(UNITS_MLA)]
                            width = P * (qt + 1)
                            dve.wait_ge(scores_ready, un.value)
                            for n, (h, g) in enumerate((h, g) for h in heads for g in range(DIL_GROUPS)):
                                step.mark(dve.scalar_tensor_tensor(
                                    probs[:, n * width:(n + 1) * width], dil_dist[:, g, SEQ - width:], -slope(g, h),
                                    wide(4, 1024)[:, n * width:(n + 1) * width], ALU.mult, ALU.add))
                            step.sync()
                            negated_max(len(heads), DIL_GROUPS * width).then_inc(max_ready, 1)
                    if c == 11 or c == 12:
                        dve.wait_ge(silu_tanh, At(c - 10, l, 3).value)
                        gated(z_of(c - 11), z_of(c - 11), fill_of(c - 1)).then_inc(dve_freed, 1)
                    if c == 14:
                        dve.wait_ge(weights_used, t.value)
                        dve.wait_ge(*freed(fill_of(12), l))
                        step.link(dve.tensor_tensor(conv_in[:, :, CONV2 - 1:], a_c,
                                                    pair(fill_of(13)).rearrange("p b (f s) -> p (b f) s", s=SEQ),
                                                    ALU.mult))
                        dve.sem_inc(dve_freed, 1)
                    if c == 15:
                        dve.wait_ge(weights_used, t.value)
                        step.link(dve.tensor_tensor(a_y, a_y,
                                                    pair(fill_of(14)).rearrange("p b (f s) -> p (b f) s", s=SEQ),
                                                    ALU.mult))
                        dve.sem_inc(dve_freed, 1)
                    if c == 16:
                        dve.wait_ge(silu_tanh, At(3, l, 3).value)
                        step.link(dve.scalar_tensor_tensor(
                            slow(a_z), slow(a_z), 1.0, pair(fill_of(15)).rearrange("p b n -> p (b n)"),
                            ALU.add, ALU.mult))
                        dve.sem_inc(dve_freed, 1)
                        dve.tensor_tensor(a_z, a_z, a_y, ALU.mult).then_inc(ya_ready, 1)
                    if c in (22, 23):
                        m = c - 22
                        dve.wait_ge(weights_used, (t + 2).value)
                        add_product(m, 0)
                    split_lo(t + (1 + LOOK))
                    if c == 1:
                        dve.wait_ge(lora_rstd, At(2, l, 2).value)
                        dve.wait_ge(*freed(0, l))
                        z = z_of(0)
                        step.mark(dve.tensor_copy(qk[:, :, MLA_HEADS:, NOPE:],
                                                  z[:, :, 384:416].unsqueeze(2).broadcast_to([P, TOK, MLA_HEADS, ROPE2])))
                        for n, (lo, hi) in enumerate(((0, 256), (256, 384))):
                            for tok in range(TOK):
                                step.mark(dve.tensor_scalar(z[:, tok, lo:hi], z[:, tok, lo:hi],
                                                            rstd[:, 4 + 2 * n + tok:5 + 2 * n + tok], None, ALU.mult))
                        step.sync()
                        dve.sem_inc(lora_ready, 1)
                    if c == 2:
                        dil_sum(0)
                        for k in range(3):
                            dve.wait_ge(lora_hi, At((2, 2, 3)[k], l, 3).value)
                            rest(y2_lo[:, 4 + k, :], wide(4, 1024)[:, k * SEQ:(k + 1) * SEQ],
                                 lp[:, L_QA + k:L_QA + k + 1], y2_hi[:, 4 + k, :]).then_inc(lora_lo, 1)
                    if 4 <= c <= 7:
                        dil_sum(c - 2)
                    if c == 13:
                        dve.wait_ge(values_ready, At(UB + 3, l, UNITS_LAYER).value)
                        recip_sums(MLA_HEADS, 2 * MLA_HEADS)
                        divide_rows(y_tok[:, 1, :], psum[:, 7, :], MLA_HEADS, MLA_HEADS).then_inc(values_read, 1)
                        step.mark(dve.memset(conv_in[:, :, 0:CONV2 - 1], 0.0))
                        dve.wait_ge(values_read, At(4, l, 4).value)
                        dve.tensor_tensor(y_tok, y_tok, z_of(0), ALU.mult).then_inc(heads_ready, 1)
                    split_lo(t + (2 + LOOK))
                    if c == 2:
                        dil_norm(0)
                    if 4 <= c <= 7:
                        dil_norm(c - 2)
                    if c == 4:
                        dve.wait_ge(mla_squares, At(1, l, 1).value)
                        dve.tensor_reduce(squares[:, 40:72], qk_sq.rearrange("p t h n -> p (t h) n"), AX.X, ALU.add
                                          ).then_inc(mla_sums, 1)
                    split_lo(t + (3 + LOOK))
                    if c == 2:
                        dil_sum(1)
                        split_lo(t + (4 + LOOK))
                        split_lo(t + (5 + LOOK))
                        split_lo(t + (6 + LOOK))
                        dil_norm(1)
                    if c == 5:
                        dve.wait_ge(mla_rstd, At(1, l, 1).value)
                        v = qk.rearrange("p t h n -> p (t h) n")
                        step.link(dve.tensor_tensor(v, v, rstd[:, 40:72].unsqueeze(2).broadcast_to([P, 32, QK]),
                                                    ALU.mult))
                    if c == 6:
                        for n, at in enumerate((L_GQ, L_GK)):
                            part = qk[:, :, n * MLA_HEADS:(n + 1) * MLA_HEADS, :]
                            gain = lp[:, at:at + QK].unsqueeze(1).unsqueeze(1)
                            step.mark(dve.tensor_tensor(part, part, gain.broadcast_to([P, TOK, MLA_HEADS, QK]),
                                                        ALU.mult))
                        step.sync()
                    if c == 7:
                        half = ROPE2 // 2
                        c_, s_ = (rope2[:, j, :, :].unsqueeze(2).broadcast_to([P, TOK, 2 * MLA_HEADS, half])
                                  for j in range(2))
                        sq = qk_sq.rearrange("p t h n -> p (t h n)")
                        rotate(qk[:, :, :, NOPE:NOPE + half], qk[:, :, :, NOPE + half:], c_, s_,
                               [sq[:, 512 * j:512 * (j + 1)] for j in range(4)])
                        dve.sem_inc(mla_ready, 1)
                    if c == 11:
                        dve.wait_ge(values_ready, At(UB + 1, l, UNITS_LAYER).value)
                        recip_sums(0, MLA_HEADS)
                        divide_rows(y_tok[:, 0, :], psum[:, 6, :], MLA_HEADS, 0).then_inc(values_read, 1)
                    if c == 14:
                        dve.wait_ge(heads_hi, At(2, l, 2).value)
                        rest(slow(y1_lo[:, 4:8, :]), wide(4, 1024), 0.5, slow(y1_hi[:, 4:8, :])).then_inc(heads_lo, 1)
                        for f in range(4):
                            step.mark(dve.tensor_scalar(a_y[:, f, :], conv_in[:, f, 0:SEQ], lp[:, L_CONVW + f:L_CONVW + f + 1],
                                                        lp[:, L_CONVB + f:L_CONVB + f + 1], ALU.mult, ALU.add))
                        for tap in range(1, CONV2):
                            step.sync()
                            for f in range(4):
                                w = L_CONVW + 4 * tap + f
                                step.mark(dve.scalar_tensor_tensor(a_y[:, f, :], conv_in[:, f, tap:tap + SEQ],
                                                                   lp[:, w:w + 1], a_y[:, f, :], ALU.mult, ALU.add))
                        step.sync()
                    if c == 17:
                        dve.wait_ge(values_ready, At(UB + 7, l, UNITS_LAYER).value)
                        recip_sums(0, DIL_HEADS)
                        divide_rows(y_tok[:, 0, :], psum[:, 6, :], DIL_HEADS, 0).then_inc(values_read, 1)
                        dve.wait_ge(ya_hi, At(1, l, 1).value)
                        rest(y1_lo[:, 0:4, :], a_z, 0.5, y1_hi[:, 0:4, :]).then_inc(ya_lo, 1)
                    if c in (22, 23):
                        dve.wait_ge(weights_used, (t + 4).value)
                        add_product(c - 22, 1)
                t = chunk_at(base, LAYER_CHUNKS + 2)
                probs_copy(At(UB + UNITS_LAYER, l, UNITS_LAYER), 6)
                dve.wait_ge(values_ready, At(UB + UNITS_LAYER, l, UNITS_LAYER).value)
                recip_sums(DIL_HEADS, 2 * DIL_HEADS)
                divide_rows(y_tok[:, 1, :], psum[:, 7, :], DIL_HEADS, DIL_HEADS).then_inc(values_read, 1)
                dve.wait_ge(values_read, At(6, l, 4).value)
                dve.tensor_tensor(y_tok, y_tok, z_of(1), ALU.mult).then_inc(heads_ready, 1)
                dve.wait_ge(heads_hi, At(3, l, 2).value)
                rest(slow(y2_lo[:, 0:4, :]), wide(4, 1024), 0.5, slow(y2_hi[:, 0:4, :])).then_inc(heads_lo, 1)
                for j in range(4):
                    split_lo(t + (j + LOOK))
                for h in range(2):
                    dve.wait_ge(weights_used, (t + 2 * (h + 1)).value)
                    add_product(2, h)
                dve.wait_ge(merged_hi, At(2, l, 1).value)
                rest(slow(x_lo[:, :, :]), wide(4, 2048), 0.5, slow(x_hi[:, :, :])).then_inc(merged_lo, 1)
                for j in range(4, 12):
                    split_lo(t + (j + LOOK))
                    if j in (7, 11):
                        h = (j - 7) // 4
                        dve.wait_ge(weights_used, (t + (8 + 4 * h)).value)
                        half = slice(512 * h, 512 * (h + 1))
                        dve.tensor_tensor(res[:, :, half], res[:, :, half],
                                          psum[:, 4 + 2 * h:6 + 2 * h, :], ALU.add).then_inc(x_ready, 1)
                step.restart()

        @block.tensor
        def _(pe):
            def three(out_, lh, rh, start, stop, skip=False):
                (l_hi, l_lo), (r_hi, r_lo) = lh, rh
                for n, (a, b) in enumerate(((l_hi, r_hi), (l_hi, r_lo), (l_lo, r_hi))):
                    ins = pe.matmul(out_, a, b, start=start and n == 0, stop=stop and n == 2, skip_group_check=skip)
                return ins

            def dense(t, xs, ks, width, out_of, first, last):
                pe.wait_ge(lo_ready, (t + 1).value)
                for tok in range(TOK):
                    for n0 in range(0, width, 512):
                        n1 = min(n0 + 512, width)
                        for j, k in enumerate(ks):
                            lh = [v[:, k, tok * P:(tok + 1) * P] for v in xs]
                            rh = [w[:, t.slot, j * width + n0:j * width + n1] for w in (w_hi, w_lo)]
                            ins = three(out_of(tok, n0, n1), lh, rh, first and j == 0, last and j == len(ks) - 1)
                ins.then_inc(weights_used, 1)

            def dense_features(t, q, out_):
                pe.wait_ge(lo_ready, (t + 1).value)
                for f in range(4):
                    for j in range(2):
                        k = 2 * q + j
                        lh = [w[:, t.slot, j * 512 + f * P:j * 512 + (f + 1) * P] for w in (w_hi, w_lo)]
                        rh = [v[:, k, :] for v in (x_hi, x_lo)]
                        ins = three(out_[:, f // 2, (f % 2) * SEQ:(f % 2 + 1) * SEQ], lh, rh,
                                    k == 0 and f % 2 == 0, k == KD - 1, skip=True)
                ins.then_inc(weights_used, 1)

            def turn(out_, in_):
                return pe.transpose(out_, in_, ident)

            def pre_norm(n):
                for tok in range(TOK):
                    pe.wait_ge(normed, (n * TOK + (1 + tok)).value)
                    for k in range(KD):
                        ins = turn(wide(4, 2048)[:, k * SEQ + tok * P:k * SEQ + (tok + 1) * P],
                                   norm[:, tok, k * P:(k + 1) * P])
                    ins.then_inc(norm_turned, 1)

            def norm_part(n, k):
                pe.wait_ge(norm_lo, (n * KD + (k + 1)).value)

            def gate_up(t, n=None):
                for q in range(4):
                    if n is not None:
                        norm_part(n, 2 * q + 1)
                    dense(t + q, (x_hi, x_lo), (2 * q, 2 * q + 1), 512, lambda tok, n0, n1: psum[:, tok, :],
                          q == 0, q == 3)

            def down(t, n, first, last):
                pe.wait_ge(hidden_lo, n.value)
                for j in range(2):
                    dense(t + j, (y1_hi, y1_lo), (j,), D, lambda tok, n0, n1: wide(4 + 2 * tok, D)[:, n0:n1],
                          first and j == 0, last and j == 1)

            def turn_hidden(n):
                for tok in range(TOK):
                    pe.wait_ge(hidden_ready, (n * TOK + (1 + tok)).value)
                    for j in range(2):
                        ins = turn(psum[:, 2, j * SEQ + tok * P:j * SEQ + (tok + 1) * P],
                                   ff_a[:, tok, j * P:(j + 1) * P])
                ins.then_inc(hidden_turned, 1)

            def ffn(f, base):
                h = At(f * FF_STEPS)
                gate_up(At(base), At(2 * f))
                turn_hidden(h)
                gate_up(At(base + 4))
                down(At(base + 8), h + 1, True, False)
                turn_hidden(h + 1)
                with pe.Fori(2, FF_STEPS) as i:
                    t = At(base - 2, i, 6)
                    gate_up(t)
                    down(t + 4, At(f * FF_STEPS, i, 1), False, False)
                    turn_hidden(At(f * FF_STEPS, i, 1))
                down(At(base + FFN_TILES - 2), h + FF_STEPS, False, True)

            def fill_ready(fill, l=None):
                if fill >= 2:
                    pe.wait_ge(*freed(fill - 2, l))

            def scores(u, items, width):
                for n, (q_, k_) in enumerate(items):
                    ins = pe.matmul(wide(4, 1024)[:, n * width:(n + 1) * width], q_, k_, start=True, stop=True)
                ins.then_inc(scores_ready, 1)

            def probs_read(u):
                pe.wait_ge(probs_act, u.value)
                pe.wait_ge(probs_dve, u.value)

            def turn_probs(u, blocks):
                pe.wait_ge(exp_done, u.value)
                for b in range(blocks):
                    ins = turn(wide(4, 1024)[:, b * P:(b + 1) * P], probs[:, b * P:(b + 1) * P])
                ins.then_inc(probs_turned, 1)

            def values(outs):
                for out_, blocks, vs in outs:
                    for n, (b, v) in enumerate(zip(blocks, vs)):
                        ins = pe.matmul(out_, probs_t[:, b * P:(b + 1) * P], v, start=n == 0,
                                        stop=n == len(blocks) - 1)
                ins.then_inc(values_ready, 1)

            pe.wait_ge(small_loaded, 48)

            pre_norm(At(0))
            ffn(0, FFN1_AT)

            pre_norm(At(1))

            def q_rows(h, qt):
                return q_t[HEAD * (h % 2):HEAD * (h % 2 + 1), h // 2, qt * P:(qt + 1) * P]

            def k_rows(h, width):
                return k_t[HEAD * (h % 2):HEAD * (h % 2 + 1), h // 8, 0:width]

            def v_cols(h, s):
                kv = 2 * (h // 8) + h % 2
                return kv_tok[:, s, (KV_HEADS + kv) * HEAD:(KV_HEADS + kv + 1) * HEAD]

            def values1(u):
                qt, heads = UNITS1[u]
                probs_read(At(u + 1))
                if u == 2:
                    pe.wait_ge(values_read, 1)
                values([(wide(6, 1024)[:, h * HEAD:(h + 1) * HEAD], [n * (qt + 1) + s for s in range(qt + 1)],
                         [v_cols(h, s) for s in range(qt + 1)]) for n, h in enumerate(heads)])

            def gates_ri(half):
                pe.wait_ge(conv_done, half + 1)
                pe.wait_ge(lru_loaded, 16)
                for which in range(2):
                    fill = (F_R0, F_I0, F_R1, F_I1)[2 * half + which]
                    fill_ready(fill)
                    for j in range(4):
                        f = 4 * half + j
                        ins = pe.matmul(pair(fill)[:, j // 2, (j % 2) * SEQ:(j % 2 + 1) * SEQ],
                                        lru_blocks[:, which, f, :], xc[:, f, :], start=True, stop=True)
                    ins.then_inc(ri_ready, 1)

            chunk_fill = [F_KV, F_Q0, F_Q1, F_XB0, F_XB1, F_GATE0, F_GATE1, F_GL0, F_GL1, F_GA0, F_GA1,
                          F_PL0, F_PL1, F_PA0, F_PA1]
            for c in range(MIX_CHUNKS):
                t = At(MIX_AT + 4 * c)
                u = c - 6
                if c < len(chunk_fill):
                    fill_ready(chunk_fill[c])

                def unit_scores():
                    qt, heads = UNITS1[u]
                    width = P * (qt + 1)
                    if u:
                        probs_read(At(u))
                    else:
                        pe.wait_ge(q_copied, 1)
                        pe.wait_ge(q_copied_b, 1)
                        pe.wait_ge(k_copied, 1)
                    scores(u, [(q_rows(h, qt), k_rows(h, width)) for h in heads], width)

                if c == 11:
                    unit_scores()
                    pe.wait_ge(lru_lo, 1)
                if c == 13:
                    pe.wait_ge(heads_lo, 1)
                if c == 15:
                    pe.wait_ge(merged_lo, 1)
                for q in range(4):
                    if c == 0:
                        norm_part(At(1), 2 * q + 1)
                    if 3 <= c <= 6:
                        dense_features(t + q, q, pair(chunk_fill[c]))
                    elif c < 15:
                        xs = (x_hi, x_lo) if c < 11 else (y1_hi, y1_lo) if c < 13 else (y2_hi, y2_lo)
                        dense(t + q, xs, (2 * q, 2 * q + 1), 512,
                              lambda tok, n0, n1: pair(chunk_fill[c])[:, tok, :], q == 0, q == 3)
                    else:
                        dense(t + q, (x_hi, x_lo), (2 * q, 2 * q + 1), 512,
                              lambda tok, n0, n1: psum[:, 4 + 2 * tok + (c - 15), :], q == 0, q == 3)
                    if c == 4 and q == 3:
                        pe.wait_ge(rope_ready, 1)
                        for pr in range(KD):
                            for tok in range(TOK):
                                ins = turn(wide(4, 2048)[:, pr * SEQ + tok * P:pr * SEQ + (tok + 1) * P],
                                           q_tok[:, tok, pr * P:(pr + 1) * P])
                        ins.then_inc(qk_turned, 1)
                    if c == 5 and q == 1:
                        pe.wait_ge(q_copied, 1)
                        for j in range(2):
                            for tok in range(TOK):
                                ins = turn(psum[:, 4, j * SEQ + tok * P:j * SEQ + (tok + 1) * P],
                                           kv_tok[:, tok, j * P:(j + 1) * P])
                        ins.then_inc(qk_turned, 1)
                    if q == 0 and 0 <= u < len(UNITS1) and c != 11:
                        unit_scores()
                    if q == (3 if u == 3 else 1) and 1 <= u <= len(UNITS1):
                        values1(u - 1)
                if 0 <= u < len(UNITS1):
                    turn_probs(At(u + 1), 8)
                if c == 6:
                    gates_ri(0)
                if c == 7:
                    gates_ri(1)
                if c == 12:
                    pe.wait_ge(values_read, 2)
                    for f in range(KD):
                        for tok in range(TOK):
                            ins = turn(wide(4, 2048)[:, f * SEQ + tok * P:f * SEQ + (tok + 1) * P],
                                       heads1[:, tok, f * P:(f + 1) * P])
                    ins.then_inc(heads_turned, 1)
                if c == 14:
                    pe.wait_ge(merged_ready, 1)
                    for f in range(KD):
                        for tok in range(TOK):
                            ins = turn(wide(4, 2048)[:, f * SEQ + tok * P:f * SEQ + (tok + 1) * P],
                                       merged1[:, tok, f * P:(f + 1) * P])
                    ins.then_inc(merged_turned, 1)

            pre_norm(At(2))
            ffn(1, FFN2_AT)

            with pe.Fori(0, LAYERS) as l:
                base = At(LAYER_AT, l, LAYER_TILES)
                UB = len(UNITS1)
                pre_norm(At(3, l, 1))

                def unit_items(u):
                    if u < len(UNITS_MLA):
                        qt, heads = UNITS_MLA[u]
                        width = P * (qt + 1)
                        return [(mla_t[0:QK, h, qt * P:(qt + 1) * P], mla_t[0:QK, MLA_HEADS + h, 0:width])
                                for h in heads], width
                    qt, heads = DIL_UNITS[u - len(UNITS_MLA)]
                    width = P * (qt + 1)
                    items = []
                    for h in heads:
                        r = slice(HEAD * (h % 2), HEAD * (h % 2 + 1))
                        items += [(dil_q[r, 4 * g + h // 2, qt * P:(qt + 1) * P], dil_k[r, 4 * g + h // 2, 0:width])
                                  for g in range(DIL_GROUPS)]
                    return items, width

                def unit_values(u):
                    probs_read(At(UB + u + 1, l, UNITS_LAYER))
                    if u == 3:
                        pe.wait_ge(values_read, At(3, l, 4).value)
                    if u == 7:
                        pe.wait_ge(values_read, At(4, l, 4).value)
                    if u < len(UNITS_MLA):
                        qt, heads = UNITS_MLA[u]
                        values([(psum[:, 6 + qt, h * HEAD:(h + 1) * HEAD], [n * (qt + 1) + s for s in range(qt + 1)],
                                 [mla_v[:, s, h * HEAD:(h + 1) * HEAD] for s in range(qt + 1)])
                                for n, h in enumerate(heads)])
                    else:
                        qt, heads = DIL_UNITS[u - len(UNITS_MLA)]
                        values([(psum[:, 6 + qt, h * HEAD:(h + 1) * HEAD],
                                 [(n * DIL_GROUPS + g) * (qt + 1) + s for g in range(DIL_GROUPS) for s in range(qt + 1)],
                                 [dil_v[:, g, s, h * HEAD:(h + 1) * HEAD] for g in range(DIL_GROUPS)
                                  for s in range(qt + 1)]) for n, h in enumerate(heads)])

                def turn_heads(count):
                    pe.wait_ge(heads_ready, (count + -1).value)
                    for f in range(4):
                        for tok in range(TOK):
                            ins = turn(wide(4, 1024)[:, f * SEQ + tok * P:f * SEQ + (tok + 1) * P],
                                       y_tok[:, tok, f * P:(f + 1) * P])
                    ins.then_inc(heads_turned, 1)

                def turn_mla(r):
                    b = (6, 4)[r % 2]
                    if r >= 2:
                        pe.wait_ge(mla_copied, At(r - 1, l, 4).value)
                    for j in range(4):
                        for tok in range(TOK):
                            ins = turn(wide(b, 1024)[0:QK, j * SEQ + tok * P:j * SEQ + (tok + 1) * P],
                                       qk[:, tok, 4 * r + j, :])
                    ins.then_inc(mla_turned, 1)

                for c in range(LAYER_CHUNKS):
                    t = chunk_at(base, c)
                    u = c - 9
                    fill = fill_of(c)
                    fill_ready(fill, l)
                    if 16 <= c:
                        g = c - 16
                        if g == 0:
                            pe.wait_ge(bias_rest, At(1, l, 1).value)
                        for tok in range(TOK):
                            for n, b in enumerate((bias_hi, bias_lo)):
                                pe.matmul(pair(fill)[:, tok, :], sel_r[:, g * P:(g + 1) * P], b[:, :],
                                          start=n == 0, stop=False)
                    for q in range(4):
                        if c == 0:
                            norm_part(At(3, l, 1), 2 * q + 1)
                        if 12 <= c <= 15:
                            dense_features(t + q, q, pair(fill))
                        else:
                            dense(t + q, (x_hi, x_lo), (2 * q, 2 * q + 1), 512,
                                  lambda tok, n0, n1: pair(fill)[:, tok, :], q == 0 and c < 16, q == 3)
                        if c == 2 and q == 1:
                            pe.wait_ge(lora_ready, At(1, l, 1).value)
                            z = norm[:, 0, :].rearrange("p (t n) -> p t n", t=TOK)
                            for f in range(3):
                                for tok in range(TOK):
                                    ins = turn(wide(4, 1024)[:, f * SEQ + tok * P:f * SEQ + (tok + 1) * P],
                                               z[:, tok, f * P:(f + 1) * P])
                            ins.then_inc(lora_turned, 1)
                        if c == 8 and q == 0:
                            pe.wait_ge(mla_ready, At(1, l, 1).value)
                            turn_mla(0)
                            pe.wait_ge(dil_copied, At(6, l, 6).value)
                            turn_mla(1)
                        if c == 8 and q == 1:
                            turn_mla(2)
                            turn_mla(3)
                        if q == 0 and 0 <= u:
                            if u:
                                probs_read(At(UB + u, l, UNITS_LAYER))
                            else:
                                pe.wait_ge(mla_copied, At(4, l, 4).value)
                            scores(u, *unit_items(u))
                        if q == 1 and 1 <= u:
                            unit_values(u - 1)
                        if c == 14 and q == 2:
                            pe.wait_ge(max_ready, At(UB + u + 1, l, UNITS_LAYER).value)
                            turn_heads(At(2, l, 2))
                    if c == 14:
                        pe.wait_ge(heads_lo, At(2, l, 2).value)
                    if 0 <= u:
                        turn_probs(At(UB + u + 1, l, UNITS_LAYER), 8 if u < len(UNITS_MLA) else 6)
                    if c in (2, 3, 4, 5, 6, 7):
                        j = 0 if c == 2 else c - 2
                        pe.wait_ge(dil_normed, At(j + 1, l, 6).value)
                        if j == 0:
                            pe.wait_ge(lora_lo, At(3, l, 3).value)
                        else:
                            pe.wait_ge(dil_copied, At(j, l, 6).value)
                        if c == 3:
                            pe.wait_ge(up_copied, At(2, l, 2).value)
                        z = norm[:, (j + 1) % 2, :].rearrange("p (t n) -> p t n", t=TOK)
                        for f in range(4):
                            for tok in range(TOK):
                                ins = turn(wide(4, 1024)[:, f * SEQ + tok * P:f * SEQ + (tok + 1) * P],
                                           z[:, tok, f * P:(f + 1) * P])
                        ins.then_inc(dil_turned, 1)
                    if c == 2:
                        pe.wait_ge(*freed(1, l))
                        pe.wait_ge(*freed(2, l))
                        for k in range(2):
                            dense(t + (4 + k), (y2_hi[:, 4:, :], y2_lo[:, 4:, :]), (k,), MLA_HEADS * QK,
                                  lambda tok, n0, n1: wide(2 * ((3 + tok) % 2), 1024)[:, n0:n1], k == 0, k == 1)
                        pe.wait_ge(dil_copied, At(1, l, 6).value)
                        dense(t + 6, (y2_hi[:, 6:, :], y2_lo[:, 6:, :]), (0,), 1024,
                              lambda tok, n0, n1: wide(4 + 2 * tok, 1024)[:, n0:n1], True, True)

                for m in range(3):
                    t = chunk_at(base, LAYER_CHUNKS + m)
                    u = LAYER_CHUNKS + m - 9
                    if u < UNITS_LAYER:
                        probs_read(At(UB + u, l, UNITS_LAYER))
                        scores(u, *unit_items(u))
                        unit_values(u - 1)
                    xs = ((y1_hi, y1_lo), (y1_hi[:, 4:, :], y1_lo[:, 4:, :]), (y2_hi, y2_lo))[m]
                    if m == 0:
                        pe.wait_ge(ya_lo, At(1, l, 1).value)
                    if m == 2:
                        unit_values(u - 1)
                        turn_heads(At(3, l, 2))
                        pe.wait_ge(heads_lo, At(3, l, 2).value)
                    for h in range(2):
                        fill = fill_of(LAYER_CHUNKS) + 2 * m + h
                        fill_ready(fill, l)
                        for q in range(2):
                            dense(t + (2 * h + q), xs, (2 * q, 2 * q + 1), 512,
                                  lambda tok, n0, n1: pair(fill)[:, tok, :], q == 0, q == 1)
                    if u < UNITS_LAYER:
                        turn_probs(At(UB + u + 1, l, UNITS_LAYER), 6)
                pe.wait_ge(merged_ready, At(2, l, 1).value)
                for f in range(KD):
                    for tok in range(TOK):
                        ins = turn(wide(4, 2048)[:, f * SEQ + tok * P:f * SEQ + (tok + 1) * P],
                                   merged2[:, tok, f * P:(f + 1) * P])
                ins.then_inc(merged_turned, 1)
                pe.wait_ge(merged_lo, At(2, l, 1).value)
                t = chunk_at(base, LAYER_CHUNKS + 3)
                for h in range(2):
                    for q in range(4):
                        dense(t + (4 * h + q), (x_hi, x_lo), (2 * q, 2 * q + 1), 512,
                              lambda tok, n0, n1: psum[:, 4 + 2 * h + tok, :], q == 0, q == 3)


def weight_tiles(named):
    tiles = []

    def chunk(w, c0, width=512, ks=2):
        part = w[:, c0:c0 + width]
        if part.shape[1] < width:
            part = np.concatenate([part, np.zeros((part.shape[0], width - part.shape[1]), np.float32)], 1)
        for k in range(0, w.shape[0], ks * P):
            tile = part[k:k + ks * P].reshape(ks, P, width).transpose(1, 0, 2).reshape(P, ks * width)
            if ks * width < TILE:
                tile = np.concatenate([tile, np.zeros((P, TILE - ks * width), np.float32)], 1)
            tiles.append(tile)

    def ffn(w_gu, w_down):
        def gate_up(i):
            a = i * FF_STEP
            chunk(np.concatenate([w_gu[:, a:a + FF_STEP], w_gu[:, D_FF + a:D_FF + a + FF_STEP]], 1), 0)

        def down(i):
            chunk(w_down[i * FF_STEP:(i + 1) * FF_STEP], 0, D, 1)

        gate_up(0)
        for i in range(1, FF_STEPS):
            gate_up(i)
            down(i - 1)
        down(FF_STEPS - 1)

    ffn(named["ffn1_w_gu"][0], named["ffn1_w_down"][0])
    w = named["w_in"][0]
    gate, xbr, q, kv, g_lru, g_attn = 0, 1024, 2048, 3072, 3584, 4608
    w_q = w[:, q:q + 1024].reshape(D, Q_HEADS, HEAD)[:, head_order()].reshape(D, 1024)
    chunk(w, kv)
    chunk(w_q, 0)
    chunk(w_q, 512)
    for at in (xbr, gate, g_lru, g_attn):
        chunk(w, at)
        chunk(w, at + 512)
    w_attn = named["w_proj_attn"][0].reshape(Q_HEADS, HEAD, D)[head_order()].reshape(1024, D)
    for w in (named["w_proj_lru"][0], w_attn, named["w_out"][0]):
        chunk(w, 0)
        chunk(w, 512)
    ffn(named["ffn2_w_gu"][0], named["ffn2_w_down"][0])
    for l in range(LAYERS):
        w = named["w_in_2"][l]
        a_b, a_c, a_x, a_z, low, b_z = 0, 512, 1024, 1536, 2048, 2464
        dq = 2976
        dk, dv, c_z, gates = dq + 1536, dq + 3072, dq + 4608, dq + 5120
        chunk(w[:, low:low + 416], 0)
        chunk(w, dq)
        chunk(w, dq + 512)
        chunk(named["w_uq_2"][l], 0, MLA_HEADS * QK, 1)
        chunk(named["w_ukv_2"][l], 0, 1024, 1)
        for at in [dq + 1024] + [dk + 512 * g for g in range(3)] + [dv + 512 * g for g in range(3)] + [
                b_z, c_z, a_c, a_x, a_b, a_z] + [gates + 512 * g for g in range(GATE_CHUNKS)]:
            chunk(w, at)
        for name in ("w_out_a_2", "w_out_b_2", "w_out_c_2", "w_o_2"):
            chunk(named[name][l], 0)
            chunk(named[name][l], 512)
    tiles += [np.zeros((P, TILE), np.float32)] * LOOK
    assert len(tiles) == ALL_TILES, (len(tiles), ALL_TILES)
    return np.stack(tiles)


def head_order():
    return np.array([(2 * j + i) * (Q_HEADS // KV_HEADS) + g for j in range(2) for g in range(4) for i in range(2)])


def constants():
    c = np.zeros((P, N_CONST), np.float32)
    c[:, C_IDENT:C_IDENT + P] = np.eye(P)
    q, s = np.arange(P)[:, None], np.arange(SEQ)[None, :]
    back = P + q - s
    c[:, C_MASK1:C_MASK1 + SEQ] = np.where((back >= 0) & (back < P), 0.0, NEG)
    c[:, C_MASK2:C_MASK2 + SEQ] = np.where(back >= 0, 0.0, NEG)
    for g, dil in enumerate(DILATIONS):
        ok = (back >= 0) & (back % dil == 0) & (back <= dil * DIL_BACK)
        c[:, C_DIL + g * SEQ:C_DIL + (g + 1) * SEQ] = np.where(ok, back, BIG)
    for at, half in ((C_ROPE1, HALF), (C_ROPE2, ROPE2 // 2)):
        inv = np.float32(10000.0) ** (-np.arange(half, dtype=np.float32) / np.float32(half))
        ang = np.arange(SEQ, dtype=np.float32)[:, None] * inv[None, :]
        table = np.stack([np.cos(ang), np.sin(ang)]).astype(np.float32).reshape(2, TOK, P, half)
        c[:, at:at + 2 * TOK * half] = table.transpose(2, 0, 1, 3).reshape(P, -1)
    return c


def columns(v):
    return v.reshape(-1, P).T


def kernel(**inputs):
    import concourse.bacc as bacc
    from concourse.bass_utils import run_bass_kernel_spmd

    named = {k: np.asarray(v) for k, v in inputs.items()}
    params1 = np.concatenate(
        [columns(named[n][0]) for n in ("ffn1_pre_g", "mix_pre_g", "ffn2_pre_g")]
        + [columns(named["conv_w"][0, k]) for k in range(CONV1)]
        + [columns(named[n][0]) for n in ("conv_b", "lru_b_a", "lru_b_x", "lru_lambda")]
        + [np.broadcast_to(named["attn_sinks"][0][head_order()], (P, Q_HEADS))], 1)
    gains = np.stack([np.broadcast_to(named[n][0], (P, D)) for n in ("ffn1_post_g", "mix_post_g", "ffn2_post_g")])
    lru_w = np.zeros((P, 2, KD, P), np.float32)
    for a, name in enumerate(("lru_w_a", "lru_w_x")):
        w = named[name][0]
        for f in range(KD):
            for i in range(2):
                part = slice(HEAD * i, HEAD * (i + 1))
                lru_w[part, a, f, part] = w[2 * f + i]
    lru_w = lru_w.reshape(P, -1)
    layer_params = np.stack([np.concatenate(
        [columns(named["norm_g_2"][l])]
        + [columns(named["conv_w_2"][l, k]) for k in range(CONV2)]
        + [columns(named["conv_b_2"][l]), columns(named["q_a_norm_g_2"][l]), columns(named["kv_a_norm_g_2"][l])]
        + [columns(np.concatenate([named[n][l, g]] * 2)) for n in ("dil_q_norm_g_2", "dil_k_norm_g_2")
           for g in range(DIL_GROUPS)]
        + [np.broadcast_to(named[n][l], (P, QK)) for n in ("mla_q_norm_g_2", "mla_k_norm_g_2")], 1)
        for l in range(LAYERS)])
    gate_bias = named["b_gate_2"].reshape(LAYERS, GATE_CHUNKS, 512)
    selectors = np.zeros((GATE_CHUNKS, GATE_CHUNKS, P), np.float32)
    for g in range(GATE_CHUNKS):
        selectors[g, g] = 1.0
    arrays = {
        "x": named["x"].reshape(SEQ, D), "weights": weight_tiles(named), "consts": constants(),
        "params1": params1, "gains": gains, "lru_w": lru_w, "layer_params": layer_params,
        "gate_bias": gate_bias, "selectors": selectors.reshape(GATE_CHUNKS, -1),
    }
    arrays = {k: np.ascontiguousarray(v) for k, v in arrays.items()}
    nc = bacc.Bacc("TRN2", target_bir_lowering=False, num_devices=1)
    args = [nc.dram_tensor(k, v.shape, F32, kind="ExternalInput").ap() for k, v in arrays.items()]
    out = nc.dram_tensor("out", (SEQ, D), F32, kind="ExternalOutput").ap()
    block_program(nc, *args, out)
    result = run_bass_kernel_spmd(nc, [arrays], core_ids=[0])
    return result.results[0]["out"].reshape(1, SEQ, D)
```

```python
import math
from contextlib import ExitStack

import concourse.bass as bass
import numpy as np
from concourse import mybir

F32 = mybir.dt.float32
F32R = mybir.dt.float32r
ALU = mybir.AluOpType
ACT = mybir.ActivationFunctionType
AX = mybir.AxisListType

P = 128
SEQ = 256
TOK = SEQ // P
D = 1024
KD = D // P
D_FF = 2816
FF_STEP = 256
FF_STEPS = D_FF // FF_STEP
LAYERS = 2
TILE = 1024
RING = 3
BIG = 1e33
NEG = -1e30

HEAD = 64
HALF = HEAD // 2
Q_HEADS = 16
KV_HEADS = 4
LRU_C = 8.0
CONV1 = 4
MLA_HEADS = 8
NOPE = 64
ROPE2 = 32
QK = NOPE + ROPE2
DIL_HEADS = 8
DIL_GROUPS = 3
DILATIONS = (1, 4, 16)
DIL_BACK = 128
CONV2 = 3
W2 = 512
K2 = W2 // P
EPS = 1e-6
GELU_C = math.sqrt(2.0 / math.pi)

FFN_TILES = 6 * FF_STEPS
MIX_CHUNKS = 17
MIX_TILES = 4 * MIX_CHUNKS
FFN1_AT = 0
MIX_AT = FFN1_AT + FFN_TILES
FFN2_AT = MIX_AT + MIX_TILES
LAYER_AT = FFN2_AT + FFN_TILES
LAYER_CHUNKS = 22
LAYER_TILES = 4 * LAYER_CHUNKS + 3 + 12 + 8
LOOK = 2
ALL_TILES = LAYER_AT + LAYERS * LAYER_TILES
assert LAYER_TILES % RING == 0

PAIRED = [(0, 0), (0, 1), (1, 0), (1, 1), (0, 2), (0, 3), (1, 2), (1, 3)]
C_IDENT = 0
C_MASK1 = C_IDENT + P
C_MASK2 = C_MASK1 + SEQ
C_DIL = C_MASK2 + SEQ
C_ROPE1 = C_DIL + DIL_GROUPS * SEQ
C_ROPE2 = C_ROPE1 + 2 * TOK * HALF
N_CONST = C_ROPE2 + 2 * TOK * (ROPE2 // 2)
B_FFN1, B_MIX, B_FFN2, B_CONVW = 0, 8, 16, 24
B_CONVB, B_BA, B_BX, B_LAM, B_SINK = 56, 64, 72, 80, 88
N_B1 = B_SINK + Q_HEADS
L_NORM, L_CONVW, L_CONVB, L_QA, L_KVA, L_DQ, L_DK, L_GQ = 0, 8, 20, 24, 26, 27, 30, 33
L_GK = L_GQ + QK
N_LP = L_GK + QK
GATE_CHUNKS = 6


class At:

    def __init__(self, base, var=None, per=0):
        self.base, self.var, self.per = base, var, per

    def __add__(self, n):
        return At(self.base + n, self.var, self.per)

    def __mul__(self, n):
        return At(self.base * n, self.var, self.per * n)

    @property
    def slot(self):
        assert self.per % RING == 0
        return self.base % RING

    @property
    def value(self):
        return self.base if self.var is None else self.var * self.per + self.base

    @property
    def loaded(self):
        rounds = 16 * (self.base // RING + 1)
        return rounds if self.var is None else self.var * (16 * self.per // RING) + rounds

    @property
    def first(self):
        return self.var is None and self.base < RING


class Steps:

    def __init__(self, eng, sem):
        self.eng, self.sem, self.n = eng, sem, 0

    def mark(self, ins):
        ins.then_inc(self.sem, 1)
        self.n += 1

    def sync(self):
        self.eng.wait_ge(self.sem, self.n)

    def link(self, ins):
        self.mark(ins)
        self.sync()

    def restart(self):
        self.sync()
        self.eng.sem_clear(self.sem)
        self.n = 0


def slope(g, h):
    return 2.0 ** (-8.0 * (g * DIL_HEADS + h + 1) / (DIL_GROUPS * DIL_HEADS))


def units_two_tiles(heads):
    return [(0, list(range(h, h + 8))) for h in range(0, heads, 8)] + [
        (1, list(range(h, h + 4))) for h in range(0, heads, 4)]


def even_odd(heads):
    return heads[0::2] + heads[1::2]


DIL_UNITS = [(0, [h, h + 2]) for h in (0, 1, 4, 5)] + [(1, [h]) for h in range(DIL_HEADS)]
UNITS1 = [(qt, even_odd(heads)) for qt, heads in units_two_tiles(Q_HEADS)]
UNITS_MLA = units_two_tiles(MLA_HEADS)
UNITS_LAYER = len(UNITS_MLA) + len(DIL_UNITS)


def block_program(nc, x, weights, consts, params1, gains, lru_w, layer_params, gate_bias, selectors, out):
    ctx = ExitStack()
    with ctx:
        def sb(name, shape, dt=F32):
            return ctx.enter_context(nc.sbuf_tensor(name, shape, dt))

        def sem(name):
            return ctx.enter_context(nc.semaphore(name))

        raw = sb("raw", [P, RING, TILE])
        w_hi = sb("w_hi", [P, RING, TILE], F32R)
        w_lo = sb("w_lo", [P, RING, TILE], F32R)
        x_hi = sb("x_hi", [P, KD, SEQ], F32R)
        x_lo = sb("x_lo", [P, KD, SEQ], F32R)
        y1_hi = sb("y1_hi", [P, KD, SEQ], F32R)
        y1_lo = sb("y1_lo", [P, KD, SEQ], F32R)
        y2_hi = sb("y2_hi", [P, KD, SEQ], F32R)
        y2_lo = sb("y2_lo", [P, KD, SEQ], F32R)
        res = sb("res", [P, TOK, D])
        norm = sb("norm", [P, TOK, D])
        cst = sb("cst", [P, N_CONST])
        squares = sb("squares", [P, 80])
        rstd = sb("rstd", [P, 80])
        mean = sb("mean", [P, 32])
        power = sb("power", [P, 32])
        scores_max = sb("scores_max", [P, Q_HEADS])
        scores_sum = sb("scores_sum", [P, TOK * Q_HEADS])
        sum_recip = sb("sum_recip", [P, TOK * Q_HEADS])
        probs = sb("probs", [P, 1024])
        probs_t = sb("probs_t", [P, 1024])
        ident = cst[:, C_IDENT:C_IDENT + P]
        mask_window = cst[:, C_MASK1:C_MASK1 + SEQ]
        mask_causal = cst[:, C_MASK2:C_MASK2 + SEQ]
        dil_dist = cst[:, C_DIL:C_DIL + DIL_GROUPS * SEQ].rearrange("p (g s) -> p g s", g=DIL_GROUPS)
        rope1 = cst[:, C_ROPE1:C_ROPE1 + 2 * TOK * HALF].rearrange("p (c t i) -> p c t i", c=2, t=TOK)
        rope2 = cst[:, C_ROPE2:N_CONST].rearrange("p (c t i) -> p c t i", c=2, t=TOK)

        ARENA = 21760
        arena = sb("arena", [P, ARENA])
        sel_r = sb("sel_r", [GATE_CHUNKS, GATE_CHUNKS * P], F32R)
        bias_hi = sb("bias_hi", [GATE_CHUNKS, 512], F32R)
        bias_lo = sb("bias_lo", [GATE_CHUNKS, 512], F32R)

        def view(at, *shape):
            n = int(np.prod(shape))
            assert at + n <= ARENA, (at, shape)
            flat = arena[:, at:at + n]
            if len(shape) == 1:
                return flat
            names = "abcd"[:len(shape)]
            return flat.rearrange(f"p ({' '.join(names)}) -> p {' '.join(names)}",
                                  **{n_: s for n_, s in zip(names[:-1], shape[:-1])})

        XB_W = SEQ + CONV1 - 1
        gain_row = view(1024, D)
        lru_blocks = view(0, 2, KD, P)
        par = view(2048, N_B1)
        half_bias = view(2152, 2 * KD)
        c4 = view(2168, KD)
        soft = view(2176, 6, KD)
        sink_exp = view(2224, TOK * Q_HEADS)
        kv_tok = view(2304, TOK, 512)
        q_t = view(3328, KD, SEQ)
        k_t = view(5376, KV_HEADS // 2, SEQ)
        gate_t = view(5888, 2, TOK, D)
        xb = view(9984, KD, XB_W)
        xc = view(12064, KD, SEQ)
        lru_a = view(14112, KD, SEQ)
        lru_i = view(16160, KD, SEQ)
        lru_e = view(18208, KD, SEQ)
        q_tok = view(14112, TOK, D)
        lru_tl = view(9984, KD, SEQ)
        heads1 = (view(20256, D), view(9984, D))
        gelu = norm[:, :, :].rearrange("p t (f s) -> p (t f) s", s=SEQ)
        merged1 = view(18208, TOK, D)
        merge_tmp1 = view(14112, TOK, 512)
        ff_t = view(9984, TOK, FF_STEP)
        ff_a = view(9984 + 512, TOK, FF_STEP)
        sel_stage = view(12064, GATE_CHUNKS * P)[0:GATE_CHUNKS, :]
        lp = view(0, N_LP)
        bias_stage = view(10496, 512)[0:GATE_CHUNKS, :]
        dil_v = view(256, DIL_GROUPS, TOK, 512)
        dil_q = view(3328, 4 * DIL_GROUPS, SEQ)
        dil_k = view(6400, 4 * DIL_GROUPS, SEQ)
        mla_v = view(9472, TOK, 512)
        y_tok = view(10496, TOK, 512)
        ga_t = view(11520, 3, TOK, D)
        qk = view(11520, TOK, 2 * MLA_HEADS, QK)
        qk_sq = view(14592, TOK, 2 * MLA_HEADS, QK)
        mla_t = view(17664, 2 * MLA_HEADS, SEQ)
        conv_in = view(17664 + 1024, 4, SEQ + CONV2 - 1)
        a_c = view(17664, 4, SEQ)
        a_y = view(17664 + 2056, 4, SEQ)
        a_z = view(17664, 4, SEQ)
        merged2 = view(17664, TOK, D)
        merge_tmp2 = view(17664 + 2048, TOK, 512)

        psum = ctx.enter_context(nc.psum_tensor("psum", [P, 8, 512], F32))

        def diag(tok):
            return probs[:, tok * P:(tok + 1) * P]

        def turned_norm(tok, k):
            return psum[:, 4 * tok + k // 2, (k % 2) * P:(k % 2 + 1) * P]

        def pair(fill):
            return psum[:, 2 * (fill % 2):2 * (fill % 2) + 2, :]

        def second_half(fill):
            return pair(fill).rearrange("p b n -> p (b n)")

        def wide(b, n):
            return psum[:, b:8, :].rearrange("p b n -> p (b n)")[:, 0:n]

        raw_loaded = [sem(f"raw_loaded{i}") for i in range(RING)]
        hi_ready = sem("hi_ready")
        lo_ready = sem("lo_ready")
        weights_used = sem("weights_used")
        x_loaded = [sem(f"x_loaded{i}") for i in range(TOK)]
        ident_loaded = sem("ident_loaded")
        params_loaded = sem("params_loaded")
        small_loaded = sem("small_loaded")
        gain_loaded = sem("gain_loaded")
        layer_loaded = sem("layer_loaded")
        bias_loaded = sem("bias_loaded")
        x_ready = sem("x_ready")
        x_stored = sem("x_stored")
        power_set = sem("power_set")
        mean_ready = sem("mean_ready")
        root_started = sem("root_started")
        act_step = sem("act_step")
        dve_step = sem("dve_step")
        squares_ready = sem("squares_ready")
        rstd_ready = sem("rstd_ready")
        diag_ready = sem("diag_ready")
        idle_operand = sem("idle_operand")
        first_rows_done = sem("first_rows_done")
        norm_turned = sem("norm_turned")
        norm_hi = sem("norm_hi")
        norm_lo = sem("norm_lo")
        post_squares = sem("post_squares")
        post_rstd = sem("post_rstd")
        swish_tanh = sem("swish_tanh")
        hidden_ready = sem("hidden_ready")
        hidden_turned = sem("hidden_turned")
        hidden_hi = sem("hidden_hi")
        hidden_lo = sem("hidden_lo")
        act_freed = sem("act_freed")
        dve_freed = sem("dve_freed")
        scores_ready = sem("scores_ready")
        max_ready = sem("max_ready")
        exp_done = sem("exp_done")
        probs_turned = sem("probs_turned")
        probs_act = sem("probs_act")
        probs_dve = sem("probs_dve")
        values_ready = sem("values_ready")
        values_read = sem("values_read")
        fold_ready = sem("fold_ready")
        abs_exp = sem("abs_exp")
        rope_ready = sem("rope_ready")
        qk_turned = sem("qk_turned")
        q_copied = sem("q_copied")
        k_copied = sem("k_copied")
        conv_done = sem("conv_done")
        lru_loaded = sem("lru_loaded")
        bias_rest = sem("bias_rest")
        q_copied_b = sem("q_copied_b")
        sink_done = sem("sink_done")
        half_swish = sem("half_swish")
        ri_ready = sem("ri_ready")
        tl_ready = sem("tl_ready")
        decay_ready = sem("decay_ready")
        decay_squared = sem("decay_squared")
        gelu_arg = sem("gelu_arg")
        gelu_tanh = sem("gelu_tanh")
        gelu_ready = sem("gelu_ready")
        input_ready = sem("input_ready")
        pool_step = sem("pool_step")
        sqrt_arg = sem("sqrt_arg")
        sqrt_done = sem("sqrt_done")
        lru_ready = sem("lru_ready")
        lru_hi = sem("lru_hi")
        lru_lo = sem("lru_lo")
        heads_ready = sem("heads_ready")
        heads_turned = sem("heads_turned")
        heads_hi = sem("heads_hi")
        heads_lo = sem("heads_lo")
        merged_ready = sem("merged_ready")
        merged_turned = sem("merged_turned")
        merged_hi = sem("merged_hi")
        merged_lo = sem("merged_lo")
        bias_split = sem("bias_split")
        lora_squares = sem("lora_squares")
        lora_rstd = sem("lora_rstd")
        lora_ready = sem("lora_ready")
        lora_turned = sem("lora_turned")
        lora_hi = sem("lora_hi")
        lora_lo = sem("lora_lo")
        dil_squares = sem("dil_squares")
        dil_sums = sem("dil_sums")
        dil_rstd = sem("dil_rstd")
        dil_normed = sem("dil_normed")
        dil_turned = sem("dil_turned")
        dil_copied = sem("dil_copied")
        up_copied = sem("up_copied")
        mla_squares = sem("mla_squares")
        mla_sums = sem("mla_sums")
        mla_rstd = sem("mla_rstd")
        mla_ready = sem("mla_ready")
        mla_turned = sem("mla_turned")
        mla_copied = sem("mla_copied")
        silu_tanh = sem("silu_tanh")
        ya_ready = sem("ya_ready")
        ya_hi = sem("ya_hi")
        ya_lo = sem("ya_lo")

        FILLS1 = "AAAAA" + "AA" + "AA" + "A" + "AA" + "AAA" + "VVVV"
        (F_KV, F_Q0, F_Q1, F_XB0, F_XB1, F_GATE0, F_GATE1, F_R0, F_I0, F_GL0, F_R1, F_I1, F_GL1, F_GA0,
         F_GA1, F_PL0, F_PL1, F_PA0, F_PA1) = range(19)
        FILLS2 = "AAA" + "AA" + "AAAAAAA" + "VV" + "AVVV" + "AAAAAA" + "VVVVVV"
        FREED = {"A": act_freed, "V": dve_freed}

        def freed(fill, layer=None):
            fills = FILLS1 if layer is None else FILLS2
            who = fills[fill]
            n = fills[:fill + 1].count(who)
            if layer is None:
                return FREED[who], n
            return FREED[who], At(FILLS1.count(who) + n, layer, FILLS2.count(who)).value

        def fill_of(chunk):
            return chunk if chunk < 3 else chunk + 2

        def chunk_at(base, chunk):
            return base + (4 * chunk if chunk < 3 else 4 * chunk + 3)

        block = ctx.enter_context(nc.Block())

        @block.sync
        def _(sp):
            for tok in range(TOK):
                sp.dma_start(res[:, tok, :], x[tok * P:(tok + 1) * P, :]).then_inc(x_loaded[tok], 16)
            for t in range(RING):
                sp.dma_start(raw[:, t, :], weights[t, :, :]).then_inc(raw_loaded[t], 16)
            rounds = ALL_TILES // RING
            with sp.Fori(1, rounds) as r:
                for s in range(RING):
                    sp.wait_ge(lo_ready, At(s - RING + 1, r, RING).value)
                    sp.dma_start(raw[:, s, :], weights[bass.ds(r * RING + s, 1), :, :].rearrange("a p n -> (a p) n")
                                 ).then_inc(raw_loaded[s], 16)
            for t in range(rounds * RING, ALL_TILES):
                sp.wait_ge(lo_ready, t - RING + 1)
                sp.dma_start(raw[:, t % RING, :], weights[t, :, :]).then_inc(raw_loaded[t % RING], 16)
            for tok in range(TOK):
                sp.wait_ge(x_ready, TOK * (2 + LAYERS) + tok + 1)
                sp.dma_start(out[tok * P:(tok + 1) * P, :], res[:, tok, :]).then_inc(x_stored, 16)
            sp.wait_ge(x_stored, 16 * TOK)

        @block.gpsimd
        def _(pool):
            pool.memset(power[:, :], -0.5).then_inc(power_set, 1)
            pool.wait_ge(power_set, 1)

            jobs = At(0)

            def inverse_root(at, n, width, done, factor=1.0):
                nonlocal jobs
                jobs = jobs + 1
                pool.sem_inc(root_started, 1)
                pool.tensor_scalar(mean[:, 0:n], squares[:, at:at + n],
                                   1.0 / (width * factor ** 2), EPS / factor ** 2,
                                   ALU.mult, ALU.add).then_inc(mean_ready, 1)
                pool.wait_ge(mean_ready, jobs.value)
                pool.tensor_tensor(rstd[:, at:at + n], mean[:, 0:n], power[:, 0:n], ALU.pow).then_inc(done, 1)

            def pre_norm(n):
                for tok in range(TOK):
                    pool.wait_ge(squares_ready, (n + (1 + tok)).value)
                    inverse_root(tok, 1, D, rstd_ready)
                    pool.wait_ge(rstd_ready, (n + (1 + tok)).value)

            def rg_lru():
                def flat(v):
                    return v.rearrange("p f s -> p (f s)")

                def link(ins):
                    nonlocal steps
                    steps += 1
                    ins.then_inc(pool_step, 1)
                    pool.wait_ge(pool_step, steps)

                steps = 0
                pool.wait_ge(*freed(F_GATE1))
                link(pool.tensor_tensor(flat(lru_e), flat(gelu), flat(gelu), ALU.mult))
                link(pool.tensor_scalar(flat(lru_e), flat(lru_e), GELU_C * 0.044715, GELU_C, ALU.mult, ALU.add))
                pool.tensor_tensor(flat(lru_e), flat(lru_e), flat(gelu), ALU.mult).then_inc(gelu_arg, 1)
                pool.wait_ge(*freed(F_I1))
                link(pool.tensor_scalar(flat(lru_i), flat(lru_i), 1.0, None, ALU.add))
                pool.tensor_tensor(flat(lru_i), flat(lru_i), flat(xc), ALU.mult).then_inc(input_ready, 1)
                pool.wait_ge(gelu_tanh, 1)
                link(pool.tensor_scalar(flat(lru_e), flat(lru_e), 1.0, None, ALU.add))
                pool.tensor_tensor(flat(gelu), flat(gelu), flat(lru_e), ALU.mult).then_inc(gelu_ready, 1)

            for n in range(3):
                pre_norm(At(TOK * n))
                if n == 1:
                    rg_lru()
                for tok in range(TOK):
                    pool.wait_ge(post_squares, TOK * n + tok + 1)
                    inverse_root(2 + tok, 1, D, post_rstd, (0.5, 1.0, 0.5)[n])
                    pool.wait_ge(post_rstd, TOK * n + tok + 1)
            roots1, roots_layer = jobs.base, 2 + 2 + 6 + 1
            with pool.Fori(0, LAYERS) as l:
                jobs = At(roots1, l, roots_layer)
                pre_norm(At(3 * TOK, l, TOK))

                def dil(j):
                    pool.wait_ge(dil_sums, At(j + 1, l, 6).value)
                    inverse_root(8 + 16 * (j % 2), 16, HEAD, dil_rstd)
                    pool.wait_ge(dil_rstd, At(j + 1, l, 6).value)

                pool.wait_ge(lora_squares, At(1, l, 1).value)
                inverse_root(4, 2, 256, lora_rstd)
                pool.wait_ge(lora_rstd, At(1, l, 2).value)
                inverse_root(6, 2, 128, lora_rstd)
                pool.wait_ge(lora_rstd, At(2, l, 2).value)
                for j in range(3):
                    dil(j)
                pool.wait_ge(mla_sums, At(1, l, 1).value)
                inverse_root(40, 32, QK, mla_rstd)
                pool.wait_ge(mla_rstd, At(1, l, 1).value)
                for j in range(3, 6):
                    dil(j)
                assert jobs.base == roots1 + roots_layer

        @block.scalar
        def _(act):
            step = Steps(act, act_step)

            def split_hi(t):
                if not t.first:
                    act.wait_ge(weights_used, (t + (1 - RING)).value)
                act.wait_ge(raw_loaded[t.slot], t.loaded)
                act.activation(w_hi[:, t.slot, :], raw[:, t.slot, :], ACT.Copy).then_inc(hi_ready, 1)

            def pre_norm(n, gain, base, begun):
                def row_squares(tok):
                    if n.var is None and n.base == 0:
                        act.wait_ge(x_loaded[tok], 16)
                    else:
                        act.wait_ge(x_ready, (n * TOK + (tok + 1 - TOK)).value)
                    act.activation(norm[:, tok, :], res[:, tok, :], ACT.Square,
                                   accum_out=squares[:, tok:tok + 1]).then_inc(squares_ready, 1)

                def transposed(tok, ks):
                    for k in ks:
                        if k % 2 == 0:
                            act.wait_ge(norm_turned, (n * (TOK * KD // 2) + (tok * KD // 2 + k // 2 + 1)).value)
                        act.activation(x_hi[:, k, tok * P:(tok + 1) * P], turned_norm(tok, k), ACT.Copy,
                                       scale=gain[:, k:k + 1]).then_inc(norm_hi, 1)

                def diagonal(tok):
                    act.wait_ge(rstd_ready, (n * TOK + (1 + tok)).value)
                    act.activation(diag(tok), ident, ACT.Copy, scale=rstd[:, tok:tok + 1]).then_inc(diag_ready, 1)

                row_squares(0)
                split_hi(base + 1 if begun else base)
                diagonal(0)
                transposed(0, range(6))
                if not begun:
                    split_hi(base + 1)
                split_hi(base + 2)
                transposed(0, range(6, KD))
                row_squares(1)
                diagonal(1)
                transposed(1, range(KD))

            def post_norm(n, last, begin=True):
                for tok in range(TOK):
                    if tok == 0:
                        act.wait_ge(first_rows_done, n + 1)
                    else:
                        act.wait_ge(weights_used, last)
                    act.activation(norm[:, tok, :], wide(4 + 2 * tok, D), ACT.Square,
                                   accum_out=squares[:, 2 + tok:3 + tok]).then_inc(post_squares, 1)
                    if tok == 0 and begin:
                        split_hi(At(last))

            def bank_copies(dst, f0, src, scale, done):
                for b in range(2):
                    act.activation(dst[:, f0 + 2 * b:f0 + 2 * b + 2, :].rearrange("p f s -> p (f s)"),
                                   src[:, 512 * b:512 * (b + 1)], ACT.Copy, scale=scale).then_inc(done, 1)

            def load_gain(n):
                act.dma_start(gain_row, gains[n, :, :]).then_inc(gain_loaded, 16)

            def load_layer(l):
                act.dma_start(lp, layer_params[bass.ds(l.value, 1), :, :].rearrange("a p n -> (a p) n")
                              ).then_inc(layer_loaded, 16)

            def swish(at, i):
                act.wait_ge(weights_used, at.value)
                for tok in range(TOK):
                    act.activation(ff_t[:, tok, :], psum[:, tok, 0:FF_STEP], ACT.Tanh, scale=0.5
                                   ).then_inc(swish_tanh, 1)

            def hidden_copy(n):
                act.wait_ge(hidden_turned, n.value)
                act.activation(y1_hi[:, 0:2, :].rearrange("p a s -> p (a s)"), psum[:, 2, :], ACT.Copy
                               ).then_inc(hidden_hi, 1)

            def ffn(f, base):
                split_hi(At(base + 3))
                swish(At(base + 4), 0)
                split_hi(At(base + 4))
                if f == 0:
                    act.wait_ge(small_loaded, 32)
                    act.activation(sel_r[:, :], sel_stage, ACT.Copy)
                    step.link(act.activation(soft[:, 0, :], par[:, B_LAM:B_LAM + KD], ACT.Abs))
                    act.activation(soft[:, 1, :], soft[:, 0, :], ACT.Exp, scale=-1.0).then_inc(abs_exp, 1)
                split_hi(At(base + 5))
                with act.Fori(1, FF_STEPS) as i:
                    t = At(base - 2, i, 6)
                    hidden_copy(At(f * FF_STEPS, i, 1))
                    for j in range(4):
                        split_hi(t + (j + LOOK))
                    swish(t + 4, i)
                    split_hi(t + (4 + LOOK))
                    split_hi(t + (5 + LOOK))
                hidden_copy(At((f + 1) * FF_STEPS))
                post_norm(2 * f, base + FFN_TILES, f == 0)

            def exps(u, rows):
                act.wait_ge(max_ready, u.value)
                for n, (lo, hi, col) in enumerate(rows):
                    ins = act.activation(probs[:, lo:hi], probs[:, lo:hi], ACT.Exp,
                                         bias=scores_max[:, n:n + 1], accum_out=scores_sum[:, col:col + 1])
                ins.then_inc(exp_done, 1)

            def probs_copy(u):
                act.wait_ge(probs_turned, u.value)
                act.activation(probs_t[:, 0:512], psum[:, 4, :], ACT.Copy).then_inc(probs_act, 1)

            def chunk_done(at):
                act.wait_ge(weights_used, at.value)

            act.dma_start(ident, consts[:, C_IDENT:C_IDENT + P]).then_inc(ident_loaded, 16)
            act.dma_start(par, params1).then_inc(params_loaded, 16)
            act.wait_ge(power_set, 1)
            act.activation(scores_max[:, 0:1], power[:, 0:1], ACT.Tanh)
            act.dma_start(cst[:, P:], consts[:, P:]).then_inc(small_loaded, 16)
            act.dma_start(sel_stage, selectors).then_inc(small_loaded, 16)
            load_gain(0)
            act.wait_ge(ident_loaded, 16)
            act.wait_ge(params_loaded, 16)

            pre_norm(At(0), par[:, B_FFN1:B_FFN1 + KD], At(FFN1_AT), False)
            ffn(0, FFN1_AT)

            pre_norm(At(1), par[:, B_MIX:B_MIX + KD], At(MIX_AT), True)
            act.dma_start(lru_blocks.rearrange("p a f d -> p (a f d)"), lru_w).then_inc(lru_loaded, 16)
            rows1 = [[(j * P * (qt + 1), (j + 1) * P * (qt + 1), qt * Q_HEADS + h)
                      for j, h in enumerate(heads)] for qt, heads in UNITS1]

            def sink_part(u):
                qt, heads = UNITS1[u]
                cols = slice(qt * Q_HEADS + min(heads), qt * Q_HEADS + min(heads) + len(heads))
                act.activation(sink_exp[:, cols], sum_recip[:, cols], ACT.Exp).then_inc(sink_done, 1)

            act.wait_ge(fold_ready, 2)

            def lru_half(half):
                fs = slice(4 * half, 4 * half + 4)
                act.wait_ge(lru_ready, half + 1)
                act.activation(y1_hi[:, fs, :], gelu[:, fs, :], ACT.Copy, scale=0.5).then_inc(lru_hi, 1)

            def tanh_part(half, which):
                act.wait_ge(ri_ready, 2 * half + which + 1)
                fill = (F_R0, F_I0, F_R1, F_I1)[2 * half + which]
                dst = lru_i if which else lru_a
                for j in range(4):
                    f = 4 * half + j
                    ins = act.activation(dst[:, f, :], pair(fill)[:, j // 2, (j % 2) * SEQ:(j % 2 + 1) * SEQ],
                                         ACT.Tanh, scale=0.5, bias=half_bias[:, which * KD + f:which * KD + f + 1])
                ins.then_inc(act_freed, 1)

            for c in range(MIX_CHUNKS):
                t = At(MIX_AT + 4 * c)
                u = c - 6
                if c == 5:
                    act.wait_ge(qk_turned, 1)
                    act.activation(q_t[:, 0:4, :].rearrange("p a s -> p (a s)"), wide(4, 1024), ACT.Copy,
                                   scale=HEAD ** -0.5).then_inc(q_copied, 1)
                if 0 <= u - 1 < len(UNITS1):
                    probs_copy(At(u))
                if c:
                    split_hi(t + LOOK)
                if c == 10:
                    act.wait_ge(sqrt_arg, 1)
                    flat = lru_e.rearrange("p f s -> p (f s)")
                    act.activation(flat, flat, ACT.Sqrt, scale=0.25).then_inc(sqrt_done, 1)
                if c == 9:
                    act.wait_ge(tl_ready, 1)
                    for f in range(KD):
                        ins = act.activation(lru_a[:, f, :], lru_a[:, f, :], ACT.Exp, scale=c4[:, f:f + 1],
                                             bias=c4[:, f:f + 1])
                    ins.then_inc(decay_ready, 1)
                if 1 <= c <= 11:
                    chunk_done(t)
                if c == 1:
                    act.activation(kv_tok, pair(F_KV), ACT.Copy).then_inc(act_freed, 1)
                if c in (2, 3):
                    h = c - 2
                    act.activation(q_tok[:, :, h * 512:(h + 1) * 512], pair(F_Q0 + h), ACT.Copy).then_inc(act_freed, 1)
                if c in (4, 5):
                    h = c - 4
                    act.activation(xb[:, 4 * h:4 * h + 4, CONV1 - 1:XB_W],
                                   pair(F_XB0 + h).rearrange("p b (f s) -> p (b f) s", s=SEQ), ACT.Copy
                                   ).then_inc(act_freed, 1)
                if c in (6, 7):
                    h = c - 6
                    act.activation(gelu[:, 4 * h:4 * h + 4, :],
                                   pair(F_GATE0 + h).rearrange("p b (f s) -> p (b f) s", s=SEQ), ACT.Copy
                                   ).then_inc(act_freed, 1)
                if c == 7:
                    tanh_part(0, 0)
                    tanh_part(0, 1)
                if 8 <= c <= 11:
                    j = c - 8
                    act.activation(gate_t[:, j // 2, :, (j % 2) * 512:(j % 2 + 1) * 512],
                                   pair((F_GL0, F_GL1, F_GA0, F_GA1)[j]), ACT.Tanh, scale=0.5).then_inc(act_freed, 1)
                if c == 5:
                    act.wait_ge(qk_turned, 2)
                    act.activation(k_t.rearrange("p a s -> p (a s)"), psum[:, 4, :], ACT.Copy).then_inc(k_copied, 1)
                if c == 8:
                    tanh_part(1, 0)
                    tanh_part(1, 1)
                if c == 11:
                    lru_half(1)
                split_hi(t + (1 + LOOK))
                if c in (14, 15):
                    h = c - 14
                    act.wait_ge(merged_turned, h + 1)
                    bank_copies(x_hi, 4 * h, second_half(F_PA0) if h else wide(4, 1024), 0.5, merged_hi)
                if 0 <= u < len(UNITS1):
                    exps(At(u + 1), rows1[u])
                    sink_part(u)
                if c == 9:
                    act.wait_ge(decay_ready, 1)
                    act.wait_ge(gelu_ready, 1)
                    act.activation(lru_e.rearrange("p f s -> p (f s)"), lru_a.rearrange("p f s -> p (f s)"),
                                   ACT.Square).then_inc(decay_squared, 1)
                if c < MIX_CHUNKS - 1:
                    split_hi(t + (2 + LOOK))
                if c == 8:
                    act.wait_ge(gelu_arg, 1)
                    act.activation(lru_e.rearrange("p f s -> p (f s)"), lru_e.rearrange("p f s -> p (f s)"),
                                   ACT.Tanh).then_inc(gelu_tanh, 1)
                if c == 10:
                    lru_half(0)
                if c < MIX_CHUNKS - 1:
                    split_hi(t + (3 + LOOK))
                if c == 8:
                    for f in range(KD):
                        ins = act.activation(lru_tl[:, f, :], lru_a[:, f, :], ACT.Tanh, scale=c4[:, f:f + 1],
                                             bias=c4[:, f:f + 1])
                    ins.then_inc(tl_ready, 1)
                if c == 9:
                    load_gain(1)
                if c == 12:
                    for half in range(2):
                        act.wait_ge(heads_turned, half + 1)
                        bank_copies(y2_hi, 4 * half, wide(4 + 2 * half, 1024), 1.0, heads_hi)
            post_norm(1, MIX_AT + MIX_TILES)

            pre_norm(At(2), par[:, B_FFN2:B_FFN2 + KD], At(FFN2_AT), True)
            load_gain(2)
            load_layer(At(0))
            ffn(1, FFN2_AT)

            step.restart()
            with act.Fori(0, LAYERS) as l:
                base = At(LAYER_AT, l, LAYER_TILES)
                act.wait_ge(layer_loaded, At(16, l, 16).value)
                pre_norm(At(3, l, 1), lp[:, L_NORM:L_NORM + KD], base, False)
                act.dma_start(bias_stage,
                              gate_bias[bass.ds(l, 1), :, :].rearrange("a p n -> (a p) n")
                              ).then_inc(bias_loaded, 16)
                rows_mla = [[(j * P * (qt + 1), (j + 1) * P * (qt + 1), qt * MLA_HEADS + h)
                             for j, h in enumerate(heads)] for qt, heads in UNITS_MLA]
                rows_dil = [[(j * 3 * P * (qt + 1), (j + 1) * 3 * P * (qt + 1), qt * DIL_HEADS + h)
                             for j, h in enumerate(heads)] for qt, heads in DIL_UNITS]
                rows2 = rows_mla + rows_dil
                UB = len(UNITS1)

                def dil_chunk(j):
                    z = norm[:, (j + 1) % 2, :].rearrange("p (t n) -> p t n", t=TOK)
                    if j >= 2:
                        act.wait_ge(dil_turned, At(j - 1, l, 6).value)
                    if j == 1:
                        act.wait_ge(lora_turned, At(1, l, 1).value)
                    act.activation(z, pair(fill_of(1 + j)), ACT.Copy).then_inc(act_freed, 1)
                    if j:
                        act.wait_ge(dil_sums, At(j, l, 6).value)
                    act.wait_ge(*freed(fill_of(1 + j), l))
                    act.activation(probs[:, :].rearrange("p (t n) -> p t n", t=TOK), z, ACT.Square
                                   ).then_inc(dil_squares, 1)

                def dil_copy(j):
                    act.wait_ge(dil_turned, At(j + 1, l, 6).value)
                    dst, g = (dil_q, j) if j < 3 else (dil_k, j - 3)
                    gain = lp[:, (L_DQ, L_DK)[j // 3] + g:(L_DQ, L_DK)[j // 3] + g + 1]
                    act.activation(dst[:, 4 * g:4 * g + 4, :].rearrange("p f s -> p (f s)"), wide(4, 1024), ACT.Copy,
                                   scale=gain).then_inc(dil_copied, 1)

                for c in range(LAYER_CHUNKS + 2):
                    t = chunk_at(base, c)
                    u = c - 9
                    if 1 <= u:
                        probs_copy(At(UB + u, l, UNITS_LAYER))
                    if c == 4:
                        dil_copy(1)
                    if c:
                        split_hi(t + LOOK)
                    if c == 1:
                        act.wait_ge(bias_loaded, At(16, l, 16).value)
                        act.activation(bias_hi[:, :], bias_stage, ACT.Copy).then_inc(bias_split, 1)
                    if c == 3:
                        chunk_done(t)
                        up = psum[:, 4:8, :].rearrange("p b (h n) -> p (b h) n", n=P)
                        act.activation(qk[:, :, MLA_HEADS:, 0:NOPE],
                                       up[:, :, 0:NOPE].rearrange("p (t h) n -> p t h n", t=TOK), ACT.Copy
                                       ).then_inc(up_copied, 1)
                        act.activation(mla_v.rearrange("p t (h n) -> p (t h) n", n=HEAD), up[:, :, NOPE:P],
                                       ACT.Copy).then_inc(up_copied, 1)
                    if c and c != 3 and c < LAYER_CHUNKS + 1:
                        chunk_done(t)
                    if c == 1:
                        z = norm[:, 0, :].rearrange("p (t n) -> p t n", t=TOK)
                        for n, (lo, hi) in enumerate(((0, 256), (256, 384))):
                            for tok in range(TOK):
                                ins = act.activation(z[:, tok, lo:hi], pair(0)[:, tok, lo:hi], ACT.Square,
                                                     accum_out=squares[:, 4 + 2 * n + tok:5 + 2 * n + tok])
                                step.mark(ins)
                        step.sync()
                        act.activation(z[:, :, 0:416], pair(0)[:, :, 0:416], ACT.Copy).then_inc(act_freed, 1)
                        act.sem_inc(lora_squares, 1)
                    if c == 2:
                        dil_chunk(0)
                    if 4 <= c <= 7:
                        dil_chunk(c - 2)
                    if 8 <= c <= 10:
                        act.activation(dil_v[:, c - 8, :, :], pair(fill_of(c - 1)), ACT.Copy).then_inc(act_freed, 1)
                    if c in (11, 12):
                        z = norm[:, c - 11, :].rearrange("p (t n) -> p t n", t=TOK)
                        act.activation(z, pair(fill_of(c - 1)), ACT.Tanh, scale=0.5).then_inc(silu_tanh, 1)
                    if c == 13:
                        act.wait_ge(values_ready, At(UB + 3, l, UNITS_LAYER).value)
                        act.activation(a_c, pair(fill_of(c - 1)).rearrange("p b (f s) -> p (b f) s", s=SEQ), ACT.Copy
                                       ).then_inc(act_freed, 1)
                    if c == 16:
                        act.activation(a_z, pair(fill_of(c - 1)).rearrange("p b (f s) -> p (b f) s", s=SEQ), ACT.Tanh,
                                       scale=0.5).then_inc(silu_tanh, 1)
                    if 17 <= c <= 22:
                        i = c - 17
                        act.activation(ga_t[:, i // 2, :, (i % 2) * 512:(i % 2 + 1) * 512], pair(fill_of(c - 1)),
                                       ACT.Tanh, scale=0.5).then_inc(act_freed, 1)
                    split_hi(t + (1 + LOOK))
                    if 5 <= c <= 8:
                        dil_copy(c - 3)
                    if c == 2:
                        act.wait_ge(lora_turned, At(1, l, 1).value)
                        for k in range(3):
                            gain = lp[:, L_QA + k:L_QA + k + 1]
                            act.activation(y2_hi[:, 4 + k, :], wide(4, 1024)[:, k * SEQ:(k + 1) * SEQ], ACT.Copy,
                                           scale=gain).then_inc(lora_hi, 1)
                    if c == 4:
                        act.activation(qk_sq, qk, ACT.Square).then_inc(mla_squares, 1)
                    if 0 <= u:
                        exps(At(UB + u + 1, l, UNITS_LAYER), rows2[u])
                    split_hi(t + (2 + LOOK))
                    if c == 8:
                        for r in range(2):
                            act.wait_ge(mla_turned, At(r + 1, l, 4).value)
                            act.activation(mla_t[0:QK, 4 * r:4 * r + 4, :].rearrange("p h s -> p (h s)"),
                                           wide((6, 4)[r % 2], 1024)[0:QK, :], ACT.Copy).then_inc(mla_copied, 1)
                    if c == 23:
                        probs_copy(At(UB + UNITS_LAYER, l, UNITS_LAYER))
                    split_hi(t + (3 + LOOK))
                    if c == 8:
                        for r in range(2, 4):
                            act.wait_ge(mla_turned, At(r + 1, l, 4).value)
                            act.activation(mla_t[0:QK, 4 * r:4 * r + 4, :].rearrange("p h s -> p (h s)"),
                                           wide((6, 4)[r % 2], 1024)[0:QK, :], ACT.Copy).then_inc(mla_copied, 1)
                    if c == 2:
                        dil_copy(0)
                        chunk_done(t + 4)
                        dil_chunk(1)
                        split_hi(t + (4 + LOOK))
                        split_hi(t + (5 + LOOK))
                        chunk_done(t + 6)
                        for tok in range(TOK):
                            act.activation(qk[:, tok, 0:MLA_HEADS, :].rearrange("p h n -> p (h n)"),
                                           wide(2 * ((3 + tok) % 2), MLA_HEADS * QK), ACT.Copy).then_inc(act_freed, 1)
                        split_hi(t + (6 + LOOK))
                    if c == 14:
                        act.wait_ge(heads_turned, At(3, l, 2).value)
                        bank_copies(y1_hi, 4, wide(4, 1024), 0.5, heads_hi)
                    if c == 17:
                        act.wait_ge(ya_ready, At(1, l, 1).value)
                        act.activation(y1_hi[:, 0:4, :], a_z, ACT.Copy, scale=0.5).then_inc(ya_hi, 1)
                        load_layer(At(1, l, 1))
                t = chunk_at(base, LAYER_CHUNKS + 2)
                act.wait_ge(heads_turned, At(4, l, 2).value)
                bank_copies(y2_hi, 0, wide(4, 1024), 0.5, heads_hi)
                split_hi(t + LOOK)
                for j in range(1, 6):
                    split_hi(t + (j + LOOK))
                    if j == 2:
                        act.wait_ge(merged_turned, At(3, l, 2).value)
                        bank_copies(x_hi, 0, wide(4, 1024), 0.5, merged_hi)
                act.wait_ge(merged_turned, At(4, l, 2).value)
                bank_copies(x_hi, 4, second_half(fill_of(LAYER_CHUNKS) + 4), 0.5, merged_hi)
                for j in range(6, 10):
                    split_hi(t + (j + LOOK))
                step.restart()

            act.wait_ge(layer_loaded, 16 * (LAYERS + 1))

        @block.vector
        def _(dve):
            step = Steps(dve, dve_step)

            def split_lo(t):
                dve.wait_ge(hi_ready, (t + 1).value)
                dve.tensor_tensor(w_lo[:, t.slot, :], raw[:, t.slot, :], w_hi[:, t.slot, :].bitcast(F32),
                                  ALU.subtract).then_inc(lo_ready, 1)

            def rest(out_, in_, scale, hi):
                return dve.scalar_tensor_tensor(out_, in_, scale, hi.bitcast(F32), ALU.mult, ALU.subtract)

            def bank_rests(lo, hi, f0, src, scale, copied, n, done):
                for b in range(2):
                    fs = slice(f0 + 2 * b, f0 + 2 * b + 2)
                    dve.wait_ge(copied, (n + (b + 1)).value)
                    rest(lo[:, fs, :].rearrange("p f s -> p (f s)"), src[:, 512 * b:512 * (b + 1)], scale,
                         hi[:, fs, :].rearrange("p f s -> p (f s)")).then_inc(done, 1)

            def pre_norm(n, gain, base, begun):
                def transposed(tok, ks):
                    for k in ks:
                        dve.wait_ge(norm_hi, (n * (TOK * KD) + (KD * tok + 2 * (1 + k // 2))).value)
                        rest(x_lo[:, k, tok * P:(tok + 1) * P], turned_norm(tok, k), gain[:, k:k + 1],
                             x_hi[:, k, tok * P:(tok + 1) * P]).then_inc(norm_lo, 1)

                if not begun:
                    split_lo(base)
                transposed(0, range(2))
                split_lo(base + 1)
                transposed(0, range(2, 6))
                split_lo(base + 2)
                transposed(0, range(6, KD))
                transposed(1, range(KD))

            def post_norm(n, next_tile):
                dve.wait_ge(gain_loaded, 16 * (n + 1))
                for tok in range(TOK):
                    dve.wait_ge(post_squares, TOK * n + tok + 1)
                    step.link(dve.tensor_tensor(norm[:, tok, :], wide(4 + 2 * tok, D), gain_row, ALU.mult))
                    dve.wait_ge(post_rstd, TOK * n + tok + 1)
                    dve.scalar_tensor_tensor(res[:, tok, :], norm[:, tok, :], rstd[:, 2 + tok:3 + tok],
                                             res[:, tok, :], ALU.mult, ALU.add).then_inc(x_ready, 1)
                    if tok == 0 and next_tile is not None:
                        split_lo(At(next_tile))

            def swiglu(n):
                for tok in range(TOK):
                    dve.wait_ge(swish_tanh, (n * TOK + (1 + tok)).value)
                    dve.scalar_tensor_tensor(ff_a[:, tok, :], ff_t[:, tok, :], 1.0, psum[:, tok, 0:FF_STEP],
                                             ALU.add, ALU.mult).then_inc(half_swish, 1)
                for tok in range(TOK):
                    dve.wait_ge(half_swish, (n * TOK + (1 + tok)).value)
                    dve.scalar_tensor_tensor(ff_a[:, tok, :], ff_a[:, tok, :], 0.5,
                                             psum[:, tok, FF_STEP:2 * FF_STEP], ALU.mult, ALU.mult
                                             ).then_inc(hidden_ready, 1)

            def hidden_rest(n):
                dve.wait_ge(hidden_hi, n.value)
                dve.tensor_tensor(y1_lo[:, 0:2, :].rearrange("p a s -> p (a s)"), psum[:, 2, :],
                                  y1_hi[:, 0:2, :].rearrange("p a s -> p (a s)").bitcast(F32),
                                  ALU.subtract).then_inc(hidden_lo, 1)

            def ffn(f, base):
                split_lo(At(base + 3))
                swiglu(At(f * FF_STEPS))
                split_lo(At(base + 4))
                if f == 0:
                    block1_constants(0)
                split_lo(At(base + 5))
                if f == 0:
                    block1_constants(1)
                with dve.Fori(1, FF_STEPS) as i:
                    t = At(base - 2, i, 6)
                    hidden_rest(At(f * FF_STEPS, i, 1))
                    for j in range(4):
                        split_lo(t + (j + LOOK))
                    swiglu(At(f * FF_STEPS, i, 1))
                    split_lo(t + (4 + LOOK))
                    split_lo(t + (5 + LOOK))
                hidden_rest(At((f + 1) * FF_STEPS))
                post_norm(2 * f, base + FFN_TILES if f == 0 else None)

            def rows(n, width):
                return probs[:, 0:n * width].rearrange("p (h s) -> p h s", h=n)

            def mask_scores(u, qt, n, mask):
                width = P * (qt + 1)
                dve.wait_ge(scores_ready, u.value)
                step.link(dve.tensor_tensor(rows(n, width), wide(4, n * width).rearrange("p (h s) -> p h s", h=n),
                                            mask[:, SEQ - width:].unsqueeze(1).broadcast_to([P, n, width]), ALU.add))

            def negated_max(n, width):
                return dve.tensor_reduce(scores_max[:, 0:n], rows(n, width), AX.X, ALU.max, negate=True)

            def probs_copy(u, blocks):
                dve.wait_ge(probs_turned, u.value)
                n = (blocks - 4) * P
                dve.tensor_copy(probs_t[:, 512:512 + n], psum[:, 5, 0:n]).then_inc(probs_dve, 1)

            def recip_sums(lo, hi):
                step.link(dve.reciprocal(sum_recip[:, lo:hi], scores_sum[:, lo:hi]))

            def divide_rows(out_, in_, heads, lo):
                return dve.tensor_tensor(out_.rearrange("p (h n) -> p h n", h=heads),
                                         in_.rearrange("p (h n) -> p h n", h=heads),
                                         sum_recip[:, lo:lo + heads].unsqueeze(2).broadcast_to([P, heads, HEAD]),
                                         ALU.mult)

            def rotate(first, second, cos, sin, temps):
                shape = list(first.shape)
                tmp = [t_.rearrange("p (a b) -> p a b", b=shape[-1]) if len(shape) == 3 else
                       t_.rearrange("p (a b c) -> p a b c", a=shape[1], b=shape[2]) for t_ in temps]
                for dst, a, b in ((0, first, cos), (1, second, sin), (2, second, cos), (3, first, sin)):
                    step.mark(dve.tensor_tensor(tmp[dst], a, b, ALU.mult))
                step.sync()
                step.mark(dve.tensor_tensor(first, tmp[0], tmp[1], ALU.subtract))
                step.mark(dve.tensor_tensor(second, tmp[2], tmp[3], ALU.add))
                step.sync()

            e, two_e, t_, t2, poly = (soft[:, j, :] for j in range(1, 6))

            def block1_constants(part):
                if part == 0:
                    dve.tensor_scalar(half_bias, par[:, B_BA:B_BA + 2 * KD], 0.5, None, ALU.mult
                                      ).then_inc(fold_ready, 1)
                    dve.wait_ge(abs_exp, 1)
                    step.link(dve.tensor_scalar(two_e, e, 2.0, None, ALU.add))
                    step.link(dve.reciprocal(two_e, two_e))
                    step.link(dve.tensor_tensor(t_, e, two_e, ALU.mult))
                    step.link(dve.tensor_tensor(t2, t_, t_, ALU.mult))
                    step.link(dve.tensor_scalar(poly, t2, 1.0 / 17.0, 1.0 / 15.0, ALU.mult, ALU.add))
                for odd in (13, 11, 9, 7) if part == 0 else (5, 3, 1):
                    step.link(dve.tensor_tensor(poly, poly, t2, ALU.mult))
                    step.link(dve.tensor_scalar(poly, poly, 1.0 / odd, None, ALU.add))
                if part == 1:
                    step.link(dve.tensor_tensor(poly, poly, t_, ALU.mult))
                    step.link(dve.tensor_scalar(t_, par[:, B_LAM:B_LAM + KD], -1.0, 0.0, ALU.mult, ALU.max))
                    step.link(dve.scalar_tensor_tensor(t_, poly, 2.0, t_, ALU.mult, ALU.add))
                    dve.tensor_scalar(c4, t_, -0.5 * LRU_C, None, ALU.mult).then_inc(fold_ready, 1)

            dve.memset(gate_t[:, 0, 0, 0:512], 0.0).then_inc(idle_operand, 1)
            dve.wait_ge(params_loaded, 16)
            pre_norm(At(0), par[:, B_FFN1:B_FFN1 + KD], At(FFN1_AT), False)
            ffn(0, FFN1_AT)

            dve.wait_ge(small_loaded, 32)
            pre_norm(At(1), par[:, B_MIX:B_MIX + KD], At(MIX_AT), True)
            temps = [probs[:, 0:512], probs[:, 512:], probs_t[:, 0:512], probs_t[:, 512:]]

            def rotate_q(tok):
                q = q_tok[:, tok, :].rearrange("p (h n) -> p h n", h=Q_HEADS)
                c_, s_ = (rope1[:, j, tok, :].unsqueeze(1).broadcast_to([P, Q_HEADS, HALF]) for j in range(2))
                rotate(q[:, :, 0:HALF], q[:, :, HALF:], c_, s_, temps)

            def conv1(half, taps):
                dve.wait_ge(*freed(F_XB0 + half))
                fs = range(4 * half, 4 * half + 4)
                w = par[:, B_CONVW:B_CONVW + CONV1 * KD]
                for tap in taps:
                    if tap:
                        step.sync()
                    for f in fs:
                        if tap == 0:
                            ins = dve.tensor_scalar(xc[:, f, :], xb[:, f, 0:SEQ], w[:, f:f + 1],
                                                    par[:, B_CONVB + f:B_CONVB + f + 1], ALU.mult, ALU.add)
                        else:
                            ins = dve.scalar_tensor_tensor(xc[:, f, :], xb[:, f, tap:tap + SEQ],
                                                           w[:, tap * KD + f:tap * KD + f + 1], xc[:, f, :],
                                                           ALU.mult, ALU.add)
                        if tap < CONV1 - 1:
                            step.mark(ins)
                if tap == CONV1 - 1:
                    ins.then_inc(conv_done, 1)

            def recip_part(qt):
                part = slice(qt * Q_HEADS, (qt + 1) * Q_HEADS)
                dve.wait_ge(sink_done, (2, 6)[qt])
                step.link(dve.tensor_tensor(scores_sum[:, part], scores_sum[:, part], sink_exp[:, part], ALU.add))
                recip_sums(qt * Q_HEADS, (qt + 1) * Q_HEADS)

            def flat(v):
                return v.rearrange("p f s -> p (f s)")

            def lru(half):
                fs = slice(4 * half, 4 * half + 4)
                step.link(dve.tensor_tensor(flat(lru_i[:, fs, :]), flat(lru_i[:, fs, :]), flat(lru_e[:, fs, :]),
                                            ALU.mult))
                for f in range(4 * half, 4 * half + 4):
                    step.mark(dve.tensor_tensor_scan(xc[:, f, :], lru_a[:, f, :], lru_i[:, f, :], 0.0,
                                                     ALU.mult, ALU.add))
                step.sync()
                dve.tensor_tensor(gelu[:, fs, :], gelu[:, fs, :], xc[:, fs, :], ALU.mult).then_inc(lru_ready, 1)

            def lru_rest(half):
                fs = slice(4 * half, 4 * half + 4)
                dve.wait_ge(lru_hi, half + 1)
                dve.wait_ge(lru_ready, half + 1)
                rest(y1_lo[:, fs, :], gelu[:, fs, :], 0.5, y1_hi[:, fs, :]).then_inc(lru_lo, 1)

            def gated(dst, gate, fill):
                return dve.scalar_tensor_tensor(dst, gate, 1.0, pair(fill), ALU.add, ALU.mult)

            for c in range(MIX_CHUNKS):
                t = At(MIX_AT + 4 * c)
                u = c - 6
                if 0 <= u - 1 < len(UNITS1):
                    probs_copy(At(u), 8)
                if c == 10:
                    dve.tensor_scalar(flat(lru_e), flat(lru_e), -1.0, 0.0, ALU.mult, ALU.max).then_inc(sqrt_arg, 1)
                if c == 5:
                    dve.wait_ge(qk_turned, 1)
                    dve.tensor_scalar(flat(q_t[:, 4:8, :]), wide(6, 1024), HEAD ** -0.5, None, ALU.mult
                                      ).then_inc(q_copied_b, 1)
                if c:
                    split_lo(t + LOOK)
                if c == 11:
                    lru(1)
                if 0 <= u < len(UNITS1):
                    qt, heads = UNITS1[u]
                    n = len(heads)
                    mask_scores(At(u + 1), qt, n, mask_window)
                    step.link(negated_max(n, P * (qt + 1)))
                    h0, col = B_SINK + min(heads), qt * Q_HEADS + min(heads)
                    sink = par[:, h0:h0 + n].rearrange("p (a b) -> p b a", b=2)
                    top = scores_max[:, 0:n].rearrange("p (b a) -> p b a", b=2)
                    over = sum_recip[:, col:col + n].rearrange("p (a b) -> p b a", b=2)
                    step.link(dve.scalar_tensor_tensor(top, sink, -1.0, top, ALU.mult, ALU.min))
                    dve.tensor_tensor(over, sink, top, ALU.add).then_inc(max_ready, 1)
                if c in (14, 15):
                    h = c - 14
                    dve.wait_ge(weights_used, t.value)
                    part = slice(h * 512, (h + 1) * 512)
                    gated(merge_tmp1, gate_t[:, 1, :, part], F_PA0 + h).then_inc(dve_freed, 1)
                    dve.wait_ge(*freed(F_PA0 + h))
                    dve.tensor_tensor(merged1[:, :, part], merged1[:, :, part], merge_tmp1, ALU.add
                                      ).then_inc(merged_ready, 1)
                if c == 3:
                    dve.wait_ge(*freed(F_Q1))
                    rotate_q(0)
                split_lo(t + (1 + LOOK))
                if c in (14, 15):
                    bank_rests(x_lo, x_hi, 4 * h, second_half(F_PA0) if h else wide(4, 1024), 0.5, merged_hi,
                               At(2 * h), merged_lo)
                if c == 0:
                    step.link(dve.memset(xb[:, :, 0:CONV1 - 1], 0.0))
                if c == 1:
                    dve.wait_ge(*freed(F_KV))
                    k_ = kv_tok[:, :, 0:KV_HEADS * HEAD].rearrange("p t (h n) -> p t h n", h=KV_HEADS)
                    c_, s_ = (rope1[:, j, :, :].unsqueeze(2).broadcast_to([P, TOK, KV_HEADS, HALF]) for j in range(2))
                    rotate(k_[:, :, :, 0:HALF], k_[:, :, :, HALF:], c_, s_, [x_[:, 0:256] for x_ in temps])
                if c == 4:
                    rotate_q(1)
                    dve.sem_inc(rope_ready, 1)
                if c in (5, 6):
                    conv1(c - 5, range(2))
                if c == 11:
                    lru_rest(1)
                if c == 10:
                    dve.wait_ge(sqrt_done, 1)
                    dve.wait_ge(input_ready, 1)
                    lru(0)
                if c < MIX_CHUNKS - 1:
                    split_lo(t + (2 + LOOK))
                if c == 12:
                    dve.wait_ge(values_ready, 6)
                    recip_part(1)
                    divide_rows(heads1[1], wide(6, 1024), Q_HEADS, Q_HEADS).then_inc(values_read, 1)
                if c in (5, 6):
                    conv1(c - 5, range(2, CONV1))
                if c == 9:
                    dve.wait_ge(decay_squared, 1)
                    step.link(dve.scalar_tensor_tensor(flat(lru_e), flat(lru_e), 1.0, flat(lru_tl), ALU.add, ALU.mult))
                if c == 10:
                    lru_rest(0)
                if c < MIX_CHUNKS - 1:
                    split_lo(t + (3 + LOOK))
                if c == 8:
                    dve.wait_ge(values_ready, 2)
                    recip_part(0)
                    divide_rows(heads1[0], wide(6, 1024), Q_HEADS, 0).then_inc(values_read, 1)
                if c in (12, 13):
                    h = c - 12
                    dve.wait_ge(weights_used, (t + (2 - 2 * h)).value)
                    gated(merged1[:, :, h * 512:(h + 1) * 512], gate_t[:, 0, :, h * 512:(h + 1) * 512], F_PL0 + h
                          ).then_inc(dve_freed, 1)
                if c == 12:
                    for half in range(2):
                        bank_rests(y2_lo, y2_hi, 4 * half, wide(4 + 2 * half, 1024), 1.0, heads_hi, At(2 * half),
                                   heads_lo)
            post_norm(1, MIX_AT + MIX_TILES)

            pre_norm(At(2), par[:, B_FFN2:B_FFN2 + KD], At(FFN2_AT), True)
            ffn(1, FFN2_AT)

            step.restart()
            with dve.Fori(0, LAYERS) as l:
                base = At(LAYER_AT, l, LAYER_TILES)
                dve.wait_ge(layer_loaded, At(16, l, 16).value)
                step.mark(dve.tensor_scalar(lp[:, L_DQ:L_DQ + 3], lp[:, L_DQ:L_DQ + 3], HEAD ** -0.5, None, ALU.mult))
                step.mark(dve.tensor_scalar(lp[:, L_GQ:L_GQ + QK], lp[:, L_GQ:L_GQ + QK], QK ** -0.5, None, ALU.mult))
                pre_norm(At(3, l, 1), lp[:, L_NORM:L_NORM + KD], base, False)

                def z_of(n):
                    return norm[:, n, :].rearrange("p (t n) -> p t n", t=TOK)

                def dil_sum(j):
                    dve.wait_ge(dil_squares, At(j + 1, l, 6).value)
                    at = 8 + 16 * (j % 2)
                    dve.tensor_reduce(squares[:, at:at + 16], probs[:, :].rearrange("p (h n) -> p h n", n=HEAD), AX.X,
                                      ALU.add).then_inc(dil_sums, 1)

                def dil_norm(j):
                    at = 8 + 16 * (j % 2)
                    dve.wait_ge(dil_rstd, At(j + 1, l, 6).value)
                    dve.wait_ge(*freed(fill_of(1 + j), l))
                    z = norm[:, (j + 1) % 2, :].rearrange("p (h n) -> p h n", n=HEAD)
                    dve.tensor_tensor(z, z, rstd[:, at:at + 16].unsqueeze(2).broadcast_to([P, 16, HEAD]), ALU.mult
                                      ).then_inc(dil_normed, 1)

                def flat_rows(v):
                    return v.rearrange("p f s -> p (f s)")

                def conv2(taps):
                    for tap in taps:
                        for f in range(4):
                            w = L_CONVW + 4 * tap + f
                            if tap == 0:
                                ins = dve.tensor_scalar(a_y[:, f, :], conv_in[:, f, 0:SEQ], lp[:, w:w + 1],
                                                        lp[:, L_CONVB + f:L_CONVB + f + 1], ALU.mult, ALU.add)
                            else:
                                ins = dve.scalar_tensor_tensor(a_y[:, f, :], conv_in[:, f, tap:tap + SEQ],
                                                               lp[:, w:w + 1], a_y[:, f, :], ALU.mult, ALU.add)
                            step.mark(ins)
                        step.sync()

                def last_values():
                    dve.wait_ge(values_ready, At(UB + UNITS_LAYER, l, UNITS_LAYER).value)
                    recip_sums(DIL_HEADS, 2 * DIL_HEADS)
                    divide_rows(y_tok[:, 1, :], psum[:, 7, :], DIL_HEADS, DIL_HEADS).then_inc(values_read, 1)
                    dve.wait_ge(values_read, At(6, l, 4).value)
                    dve.tensor_tensor(y_tok, y_tok, z_of(1), ALU.mult).then_inc(heads_ready, 1)

                def add_product(m, h):
                    part = slice(h * 512, (h + 1) * 512)
                    fill = fill_of(LAYER_CHUNKS) + 2 * m + h
                    if m == 0:
                        gated(merged2[:, :, part], ga_t[:, 0, :, part], fill).then_inc(dve_freed, 1)
                        return
                    gated(merge_tmp2, ga_t[:, m, :, part], fill).then_inc(dve_freed, 1)
                    dve.wait_ge(*freed(fill, l))
                    ins = dve.tensor_tensor(merged2[:, :, part], merged2[:, :, part], merge_tmp2, ALU.add)
                    if m == 2:
                        ins.then_inc(merged_ready, 1)
                    else:
                        step.link(ins)

                UB = len(UNITS1)
                for c in range(LAYER_CHUNKS + 2):
                    t = chunk_at(base, c)
                    u = c - 9
                    if 1 <= u:
                        probs_copy(At(UB + u, l, UNITS_LAYER), 8 if u <= len(UNITS_MLA) else 6)
                    if c:
                        split_lo(t + LOOK)
                    if 0 <= u:
                        un = At(UB + u + 1, l, UNITS_LAYER)
                        if u < len(UNITS_MLA):
                            qt, heads = UNITS_MLA[u]
                            mask_scores(un, qt, len(heads), mask_causal)
                            negated_max(len(heads), P * (qt + 1)).then_inc(max_ready, 1)
                        else:
                            qt, heads = DIL_UNITS[u - len(UNITS_MLA)]
                            width = P * (qt + 1)
                            dve.wait_ge(scores_ready, un.value)
                            for n, (h, g) in enumerate((h, g) for h in heads for g in range(DIL_GROUPS)):
                                step.mark(dve.scalar_tensor_tensor(
                                    probs[:, n * width:(n + 1) * width], dil_dist[:, g, SEQ - width:], -slope(g, h),
                                    wide(4, 1024)[:, n * width:(n + 1) * width], ALU.mult, ALU.add))
                            step.sync()
                            negated_max(len(heads), DIL_GROUPS * width).then_inc(max_ready, 1)
                    if c == 11 or c == 12:
                        dve.wait_ge(silu_tanh, At(c - 10, l, 3).value)
                        gated(z_of(c - 11), z_of(c - 11), fill_of(c - 1)).then_inc(dve_freed, 1)
                    if c == 14:
                        dve.wait_ge(weights_used, t.value)
                        dve.wait_ge(*freed(fill_of(12), l))
                        step.link(dve.tensor_tensor(conv_in[:, :, CONV2 - 1:], a_c,
                                                    pair(fill_of(13)).rearrange("p b (f s) -> p (b f) s", s=SEQ),
                                                    ALU.mult))
                        dve.sem_inc(dve_freed, 1)
                    if c == 15:
                        conv2((2,))
                        dve.wait_ge(weights_used, t.value)
                        step.link(dve.tensor_tensor(a_y, a_y,
                                                    pair(fill_of(14)).rearrange("p b (f s) -> p (b f) s", s=SEQ),
                                                    ALU.mult))
                        dve.sem_inc(dve_freed, 1)
                    if c == 16:
                        dve.wait_ge(silu_tanh, At(3, l, 3).value)
                        step.link(dve.scalar_tensor_tensor(
                            flat_rows(a_z), flat_rows(a_z), 1.0, pair(fill_of(15)).rearrange("p b n -> p (b n)"),
                            ALU.add, ALU.mult))
                        dve.sem_inc(dve_freed, 1)
                        dve.tensor_tensor(a_z, a_z, a_y, ALU.mult).then_inc(ya_ready, 1)
                    if c == 23:
                        add_product(0, 1)
                    split_lo(t + (1 + LOOK))
                    if c == 1:
                        dve.wait_ge(bias_split, At(1, l, 1).value)
                        dve.tensor_tensor(bias_lo[:, :], bias_stage, bias_hi[:, :].bitcast(F32), ALU.subtract
                                          ).then_inc(bias_rest, 1)
                        dve.wait_ge(lora_rstd, At(2, l, 2).value)
                        dve.wait_ge(*freed(0, l))
                        z = z_of(0)
                        step.mark(dve.tensor_copy(qk[:, :, MLA_HEADS:, NOPE:],
                                                  z[:, :, 384:416].unsqueeze(2).broadcast_to([P, TOK, MLA_HEADS, ROPE2])))
                        for n, (lo, hi) in enumerate(((0, 256), (256, 384))):
                            for tok in range(TOK):
                                step.mark(dve.tensor_scalar(z[:, tok, lo:hi], z[:, tok, lo:hi],
                                                            rstd[:, 4 + 2 * n + tok:5 + 2 * n + tok], None, ALU.mult))
                        step.sync()
                        dve.sem_inc(lora_ready, 1)
                    if c == 2:
                        dil_sum(0)
                        for k in range(3):
                            dve.wait_ge(lora_hi, At((2, 2, 3)[k], l, 3).value)
                            rest(y2_lo[:, 4 + k, :], wide(4, 1024)[:, k * SEQ:(k + 1) * SEQ],
                                 lp[:, L_QA + k:L_QA + k + 1], y2_hi[:, 4 + k, :]).then_inc(lora_lo, 1)
                    if 4 <= c <= 7:
                        dil_sum(c - 2)
                    if c == 13:
                        dve.wait_ge(values_ready, At(UB + 3, l, UNITS_LAYER).value)
                        recip_sums(MLA_HEADS, 2 * MLA_HEADS)
                        divide_rows(y_tok[:, 1, :], psum[:, 7, :], MLA_HEADS, MLA_HEADS).then_inc(values_read, 1)
                        step.mark(dve.memset(conv_in[:, :, 0:CONV2 - 1], 0.0))
                        dve.wait_ge(values_read, At(4, l, 4).value)
                        dve.tensor_tensor(y_tok, y_tok, z_of(0), ALU.mult).then_inc(heads_ready, 1)
                    split_lo(t + (2 + LOOK))
                    if c == 2:
                        dil_norm(0)
                    if c == 4:
                        dve.wait_ge(mla_squares, At(1, l, 1).value)
                        dve.tensor_reduce(squares[:, 40:56], qk_sq[:, 0, :, :], AX.X, ALU.add)
                    if c == 23:
                        probs_copy(At(UB + UNITS_LAYER, l, UNITS_LAYER), 6)
                    if c in (22, 23):
                        dve.wait_ge(weights_used, (t + 2).value)
                        add_product(c - 22, 0)
                    if c == 23:
                        last_values()
                    split_lo(t + (3 + LOOK))
                    if c == 2:
                        dil_sum(1)
                        split_lo(t + (4 + LOOK))
                        split_lo(t + (5 + LOOK))
                        split_lo(t + (6 + LOOK))
                        dil_norm(1)
                    if 4 <= c <= 7:
                        dil_norm(c - 2)
                    if c == 4:
                        dve.tensor_reduce(squares[:, 56:72], qk_sq[:, 1, :, :], AX.X, ALU.add).then_inc(mla_sums, 1)
                    if c == 5:
                        dve.wait_ge(mla_rstd, At(1, l, 1).value)
                        v = qk.rearrange("p t h n -> p (t h) n")
                        step.link(dve.tensor_tensor(v, v, rstd[:, 40:72].unsqueeze(2).broadcast_to([P, 32, QK]),
                                                    ALU.mult))
                    if c == 6:
                        for n, at in enumerate((L_GQ, L_GK)):
                            part = qk[:, :, n * MLA_HEADS:(n + 1) * MLA_HEADS, :]
                            gain = lp[:, at:at + QK].unsqueeze(1).unsqueeze(1)
                            step.mark(dve.tensor_tensor(part, part, gain.broadcast_to([P, TOK, MLA_HEADS, QK]),
                                                        ALU.mult))
                        step.sync()
                    if c == 7:
                        half = ROPE2 // 2
                        c_, s_ = (rope2[:, j, :, :].unsqueeze(2).broadcast_to([P, TOK, 2 * MLA_HEADS, half])
                                  for j in range(2))
                        sq = qk_sq.rearrange("p t h n -> p (t h n)")
                        rotate(qk[:, :, :, NOPE:NOPE + half], qk[:, :, :, NOPE + half:], c_, s_,
                               [sq[:, 512 * j:512 * (j + 1)] for j in range(4)])
                        dve.sem_inc(mla_ready, 1)
                    if c == 11:
                        dve.wait_ge(values_ready, At(UB + 1, l, UNITS_LAYER).value)
                        recip_sums(0, MLA_HEADS)
                        divide_rows(y_tok[:, 0, :], psum[:, 6, :], MLA_HEADS, 0).then_inc(values_read, 1)
                    if c == 14:
                        bank_rests(y1_lo, y1_hi, 4, wide(4, 1024), 0.5, heads_hi, At(4, l, 4), heads_lo)
                        conv2((0, 1))
                    if c == 17:
                        dve.wait_ge(values_ready, At(UB + 7, l, UNITS_LAYER).value)
                        recip_sums(0, DIL_HEADS)
                        divide_rows(y_tok[:, 0, :], psum[:, 6, :], DIL_HEADS, 0).then_inc(values_read, 1)
                        dve.wait_ge(ya_hi, At(1, l, 1).value)
                        rest(y1_lo[:, 0:4, :], a_z, 0.5, y1_hi[:, 0:4, :]).then_inc(ya_lo, 1)
                t = chunk_at(base, LAYER_CHUNKS + 2)
                bank_rests(y2_lo, y2_hi, 0, wide(4, 1024), 0.5, heads_hi, At(6, l, 4), heads_lo)
                split_lo(t + LOOK)
                add_product(1, 1)
                split_lo(t + (1 + LOOK))
                dve.wait_ge(weights_used, (t + 2).value)
                add_product(2, 0)
                split_lo(t + (2 + LOOK))
                bank_rests(x_lo, x_hi, 0, wide(4, 1024), 0.5, merged_hi, At(4, l, 4), merged_lo)
                split_lo(t + (3 + LOOK))
                dve.wait_ge(weights_used, (t + 4).value)
                add_product(2, 1)
                split_lo(t + (4 + LOOK))
                split_lo(t + (5 + LOOK))
                bank_rests(x_lo, x_hi, 4, second_half(fill_of(LAYER_CHUNKS) + 4), 0.5, merged_hi, At(6, l, 4),
                           merged_lo)
                for j in range(6, 10):
                    split_lo(t + (j + LOOK))
                for tok in range(TOK):
                    if tok == 0:
                        dve.wait_ge(first_rows_done, At(4, l, 1).value)
                    else:
                        dve.wait_ge(weights_used, (t + 12).value)
                    dve.tensor_tensor(res[:, tok, :], res[:, tok, :], wide(4 + 2 * tok, D), ALU.add
                                      ).then_inc(x_ready, 1)
                step.restart()

        @block.tensor
        def _(pe):
            def three(out_, lh, rh, start, stop, skip=False):
                (l_hi, l_lo), (r_hi, r_lo) = lh, rh
                for n, (a, b) in enumerate(((l_hi, r_hi), (l_hi, r_lo), (l_lo, r_hi))):
                    ins = pe.matmul(out_, a, b, start=start and n == 0, stop=stop and n == 2, skip_group_check=skip)
                return ins

            def rows_product(t, tok, xs, ks, width, out_of, first, last):
                for n0 in range(0, width, 512):
                    n1 = min(n0 + 512, width)
                    for j, k in enumerate(ks):
                        lh = [v[:, k, tok * P:(tok + 1) * P] for v in xs]
                        rh = [w[:, t.slot, j * width + n0:j * width + n1] for w in (w_hi, w_lo)]
                        ins = three(out_of(tok, n0, n1), lh, rh, first and j == 0, last and j == len(ks) - 1)
                return ins

            def dense(t, xs, ks, width, out_of, first, last):
                pe.wait_ge(lo_ready, (t + 1).value)
                for tok in range(TOK):
                    ins = rows_product(t, tok, xs, ks, width, out_of, first, last)
                ins.then_inc(weights_used, 1)

            def dense_last(t, count, xs, ks_of, width, out_of, first):
                for tok in range(TOK):
                    for j in range(count):
                        if tok == 0:
                            pe.wait_ge(lo_ready, (t + (j + 1)).value)
                        ins = rows_product(t + j, tok, xs, ks_of(j), width, out_of, first and j == 0, j == count - 1)
                        if tok:
                            ins.then_inc(weights_used, 1)
                    if tok == 0:
                        ins.then_inc(first_rows_done, 1)

            def dense_features(t, q, out_):
                pe.wait_ge(lo_ready, (t + 1).value)
                for f in range(4):
                    for j in range(2):
                        k = 2 * q + j
                        lh = [w[:, t.slot, j * 512 + f * P:j * 512 + (f + 1) * P] for w in (w_hi, w_lo)]
                        rh = [v[:, k, :] for v in (x_hi, x_lo)]
                        ins = three(out_[:, f // 2, (f % 2) * SEQ:(f % 2 + 1) * SEQ], lh, rh,
                                    k == 0 and f % 2 == 0, k == KD - 1, skip=True)
                ins.then_inc(weights_used, 1)

            def turn(out_, in_):
                return pe.transpose(out_, in_, ident)

            def keep_warm(count):
                for _ in range(count):
                    pe.matmul(psum[:, 0, 0:P], ident, ident, start=True, stop=True)

            def first_chunk(n, base):
                def tile(q, tok):
                    pe.wait_ge(norm_lo, (n * (TOK * KD) + (KD * tok + 2 * (q + 1))).value)
                    return rows_product(base + q, tok, (x_hi, x_lo), (2 * q, 2 * q + 1), 512,
                                        lambda tok_, n0, n1: psum[:, tok_, :], q == 0, q == 3)

                if not (n.var is None and n.base == 0):
                    keep_warm(12)
                for tok in range(TOK):
                    pe.wait_ge(diag_ready, (n * TOK + (1 + tok)).value)
                    for k in range(KD):
                        ins = pe.matmul(turned_norm(tok, k), res[:, tok, k * P:(k + 1) * P], diag(tok),
                                        start=True, stop=True)
                        if k % 2:
                            ins.then_inc(norm_turned, 1)
                    for q in range(3):
                        if tok == 0:
                            pe.wait_ge(lo_ready, (base + (q + 1)).value)
                        ins = tile(q, tok)
                        if tok:
                            ins.then_inc(weights_used, 1)
                pe.wait_ge(lo_ready, (base + 4).value)
                for tok in range(TOK):
                    ins = tile(3, tok)
                ins.then_inc(weights_used, 1)

            def gate_up(t):
                for q in range(4):
                    dense(t + q, (x_hi, x_lo), (2 * q, 2 * q + 1), 512, lambda tok, n0, n1: psum[:, tok, :],
                          q == 0, q == 3)

            def down(t, n, first, last):
                pe.wait_ge(hidden_lo, n.value)

                def out_of(tok, n0, n1):
                    return wide(4 + 2 * tok, D)[:, n0:n1]

                if last:
                    dense_last(t, 2, (y1_hi, y1_lo), lambda j: (j,), D, out_of, False)
                    return
                for j in range(2):
                    dense(t + j, (y1_hi, y1_lo), (j,), D, out_of, first and j == 0, False)

            def turn_hidden(n):
                for tok in range(TOK):
                    pe.wait_ge(hidden_ready, (n * TOK + (1 + tok)).value)
                    for j in range(2):
                        ins = turn(psum[:, 2, j * SEQ + tok * P:j * SEQ + (tok + 1) * P],
                                   ff_a[:, tok, j * P:(j + 1) * P])
                ins.then_inc(hidden_turned, 1)

            def ffn(f, base):
                h = At(f * FF_STEPS)
                first_chunk(At(2 * f), At(base))
                turn_hidden(h)
                gate_up(At(base + 4))
                down(At(base + 8), h + 1, True, False)
                turn_hidden(h + 1)
                with pe.Fori(2, FF_STEPS) as i:
                    t = At(base - 2, i, 6)
                    gate_up(t)
                    down(t + 4, At(f * FF_STEPS, i, 1), False, False)
                    turn_hidden(At(f * FF_STEPS, i, 1))
                down(At(base + FFN_TILES - 2), h + FF_STEPS, False, True)

            def fill_ready(fill, l=None):
                if fill >= 2:
                    pe.wait_ge(*freed(fill - 2, l))

            def scores(u, items, width):
                for n, (q_, k_) in enumerate(items):
                    ins = pe.matmul(wide(4, 1024)[:, n * width:(n + 1) * width], q_, k_, start=True, stop=True)
                ins.then_inc(scores_ready, 1)

            def probs_read(u):
                pe.wait_ge(probs_act, u.value)
                pe.wait_ge(probs_dve, u.value)

            def turn_probs(u, blocks):
                pe.wait_ge(exp_done, u.value)
                for b in range(blocks):
                    ins = turn(wide(4, 1024)[:, b * P:(b + 1) * P], probs[:, b * P:(b + 1) * P])
                ins.then_inc(probs_turned, 1)

            def values(outs):
                for out_, blocks, vs in outs:
                    for n, (b, v) in enumerate(zip(blocks, vs)):
                        ins = pe.matmul(out_, probs_t[:, b * P:(b + 1) * P], v, start=n == 0,
                                        stop=n == len(blocks) - 1)
                ins.then_inc(values_ready, 1)

            pe.wait_ge(idle_operand, 1)
            for _ in range(4):
                pe.matmul(psum[:, 0, :], gate_t[:, 0, 0, 0:P], gate_t[:, 0, 0, 0:512], start=True, stop=True)
            ffn(0, FFN1_AT)

            def q_rows(h, qt):
                return q_t[HEAD * (h % 2):HEAD * (h % 2 + 1), h // 2, qt * P:(qt + 1) * P]

            def k_rows(h, width):
                return k_t[HEAD * (h % 2):HEAD * (h % 2 + 1), h // 8, 0:width]

            def v_cols(h, s):
                kv = 2 * (h // 8) + h % 2
                return kv_tok[:, s, (KV_HEADS + kv) * HEAD:(KV_HEADS + kv + 1) * HEAD]

            def values1(u):
                qt, heads = UNITS1[u]
                probs_read(At(u + 1))
                if u == 2:
                    pe.wait_ge(values_read, 1)
                values([(wide(6, 1024)[:, h * HEAD:(h + 1) * HEAD], [n * (qt + 1) + s for s in range(qt + 1)],
                         [v_cols(h, s) for s in range(qt + 1)]) for n, h in enumerate(heads)])

            def out_products(t, turn_second, n):
                def out_of(h):
                    return lambda tok, n0, n1: psum[:, 4 + 2 * tok + h, :]

                for j, (h, k) in enumerate(PAIRED[:5]):
                    if j == 2:
                        turn_second()
                    pe.wait_ge(merged_lo, (n + (k + 1)).value)
                    dense(t + j, (x_hi, x_lo), (2 * k, 2 * k + 1), 512, out_of(h), k == 0, k == 3)
                pe.wait_ge(merged_lo, (n + 4).value)
                for tok in range(TOK):
                    for j, (h, k) in enumerate(PAIRED[5:]):
                        if tok == 0:
                            pe.wait_ge(lo_ready, (t + (j + 6)).value)
                        ins = rows_product(t + (j + 5), tok, (x_hi, x_lo), (2 * k, 2 * k + 1), 512, out_of(h), False,
                                           k == 3)
                        if tok:
                            ins.then_inc(weights_used, 1)
                    if tok == 0:
                        ins.then_inc(first_rows_done, 1)

            def turn_merged1(half):
                pe.wait_ge(merged_ready, half + 1)
                out_ = second_half(F_PA0) if half else wide(4, 1024)
                for f in range(4):
                    for tok in range(TOK):
                        ins = turn(out_[:, f * SEQ + tok * P:f * SEQ + (tok + 1) * P],
                                   merged1[:, tok, (4 * half + f) * P:(4 * half + f + 1) * P])
                ins.then_inc(merged_turned, 1)

            def gates_ri(half):
                pe.wait_ge(conv_done, half + 1)
                pe.wait_ge(lru_loaded, 16)
                for which in range(2):
                    fill = (F_R0, F_I0, F_R1, F_I1)[2 * half + which]
                    fill_ready(fill)
                    for j in range(4):
                        f = 4 * half + j
                        ins = pe.matmul(pair(fill)[:, j // 2, (j % 2) * SEQ:(j % 2 + 1) * SEQ],
                                        lru_blocks[:, which, f, :], xc[:, f, :], start=True, stop=True)
                    ins.then_inc(ri_ready, 1)

            chunk_fill = [F_KV, F_Q0, F_Q1, F_XB0, F_XB1, F_GATE0, F_GATE1, F_GL0, F_GL1, F_GA0, F_GA1,
                          F_PL0, F_PL1, F_PA0, F_PA1]
            for c in range(MIX_CHUNKS):
                t = At(MIX_AT + 4 * c)
                u = c - 6
                if c < len(chunk_fill) and c != 12:
                    fill_ready(chunk_fill[c])
                if c == 0:
                    first_chunk(At(1), t)
                    continue

                def unit_scores():
                    qt, heads = UNITS1[u]
                    width = P * (qt + 1)
                    if u:
                        probs_read(At(u))
                    else:
                        pe.wait_ge(q_copied, 1)
                        pe.wait_ge(q_copied_b, 1)
                        pe.wait_ge(k_copied, 1)
                    scores(u, [(q_rows(h, qt), k_rows(h, width)) for h in heads], width)

                for q in range(4):
                    if c == 13:
                        pe.wait_ge(heads_lo, q + 1)
                    if c == 11 and q == 2:
                        fill_ready(F_PL1)
                    if c in (11, 12):
                        h, k = PAIRED[4 * (c - 11) + q]
                        pe.wait_ge(lru_lo, k // 2 + 1)
                        dense(t + q, (y1_hi, y1_lo), (2 * k, 2 * k + 1), 512,
                              lambda tok, n0, n1: pair(F_PL0 + h)[:, tok, :], k == 0, k == 3)
                    elif 3 <= c <= 6:
                        dense_features(t + q, q, pair(chunk_fill[c]))
                    elif c < 15:
                        xs = (x_hi, x_lo) if c < 11 else (y2_hi, y2_lo)
                        dense(t + q, xs, (2 * q, 2 * q + 1), 512,
                              lambda tok, n0, n1: pair(chunk_fill[c])[:, tok, :], q == 0, q == 3)
                    elif c == 15 and q == 0:
                        out_products(t, lambda: turn_merged1(1), At(0))
                    if c == 14 and q == 1:
                        turn_merged1(0)
                    if c == 4 and q == 3:
                        pe.wait_ge(rope_ready, 1)
                        for pr in range(KD):
                            for tok in range(TOK):
                                ins = turn(wide(4, 2048)[:, pr * SEQ + tok * P:pr * SEQ + (tok + 1) * P],
                                           q_tok[:, tok, pr * P:(pr + 1) * P])
                        ins.then_inc(qk_turned, 1)
                    if c == 5 and q == 1:
                        pe.wait_ge(q_copied, 1)
                        for j in range(2):
                            for tok in range(TOK):
                                ins = turn(psum[:, 4, j * SEQ + tok * P:j * SEQ + (tok + 1) * P],
                                           kv_tok[:, tok, j * P:(j + 1) * P])
                        ins.then_inc(qk_turned, 1)
                    if q == 0 and 0 <= u < len(UNITS1):
                        unit_scores()
                    if q == 1 and 1 <= u <= len(UNITS1):
                        values1(u - 1)
                if 0 <= u < len(UNITS1):
                    turn_probs(At(u + 1), 8)
                if c == 6:
                    gates_ri(0)
                if c == 7:
                    gates_ri(1)
                if c == 12:
                    pe.wait_ge(values_read, 2)
                    for f in range(KD):
                        for tok in range(TOK):
                            ins = turn(wide(4, 2048)[:, f * SEQ + tok * P:f * SEQ + (tok + 1) * P],
                                       heads1[tok][:, f * P:(f + 1) * P])
                        if f % 4 == 3:
                            ins.then_inc(heads_turned, 1)
            ffn(1, FFN2_AT)

            with pe.Fori(0, LAYERS) as l:
                base = At(LAYER_AT, l, LAYER_TILES)
                UB = len(UNITS1)

                def unit_items(u):
                    if u < len(UNITS_MLA):
                        qt, heads = UNITS_MLA[u]
                        width = P * (qt + 1)
                        return [(mla_t[0:QK, h, qt * P:(qt + 1) * P], mla_t[0:QK, MLA_HEADS + h, 0:width])
                                for h in heads], width
                    qt, heads = DIL_UNITS[u - len(UNITS_MLA)]
                    width = P * (qt + 1)
                    items = []
                    for h in heads:
                        r = slice(HEAD * (h % 2), HEAD * (h % 2 + 1))
                        items += [(dil_q[r, 4 * g + h // 2, qt * P:(qt + 1) * P], dil_k[r, 4 * g + h // 2, 0:width])
                                  for g in range(DIL_GROUPS)]
                    return items, width

                def unit_values(u):
                    probs_read(At(UB + u + 1, l, UNITS_LAYER))
                    if u == 3:
                        pe.wait_ge(values_read, At(3, l, 4).value)
                    if u == 7:
                        pe.wait_ge(values_read, At(4, l, 4).value)
                    if u < len(UNITS_MLA):
                        qt, heads = UNITS_MLA[u]
                        values([(psum[:, 6 + qt, h * HEAD:(h + 1) * HEAD], [n * (qt + 1) + s for s in range(qt + 1)],
                                 [mla_v[:, s, h * HEAD:(h + 1) * HEAD] for s in range(qt + 1)])
                                for n, h in enumerate(heads)])
                    else:
                        qt, heads = DIL_UNITS[u - len(UNITS_MLA)]
                        values([(psum[:, 6 + qt, h * HEAD:(h + 1) * HEAD],
                                 [(n * DIL_GROUPS + g) * (qt + 1) + s for g in range(DIL_GROUPS) for s in range(qt + 1)],
                                 [dil_v[:, g, s, h * HEAD:(h + 1) * HEAD] for g in range(DIL_GROUPS)
                                  for s in range(qt + 1)]) for n, h in enumerate(heads)])

                def turn_heads(count):
                    pe.wait_ge(heads_ready, (count + -2).value)
                    for f in range(4):
                        for tok in range(TOK):
                            ins = turn(wide(4, 1024)[:, f * SEQ + tok * P:f * SEQ + (tok + 1) * P],
                                       y_tok[:, tok, f * P:(f + 1) * P])
                    ins.then_inc(heads_turned, 1)

                def turn_dil(j):
                    pe.wait_ge(dil_normed, At(j + 1, l, 6).value)
                    if j == 0:
                        pe.wait_ge(lora_lo, At(3, l, 3).value)
                    else:
                        pe.wait_ge(dil_copied, At(j, l, 6).value)
                    if j == 1:
                        pe.wait_ge(up_copied, At(2, l, 2).value)
                    z = norm[:, (j + 1) % 2, :].rearrange("p (t n) -> p t n", t=TOK)
                    for f in range(4):
                        for tok in range(TOK):
                            ins = turn(wide(4, 1024)[:, f * SEQ + tok * P:f * SEQ + (tok + 1) * P],
                                       z[:, tok, f * P:(f + 1) * P])
                    ins.then_inc(dil_turned, 1)

                def turn_mla(r):
                    b = (6, 4)[r % 2]
                    if r >= 2:
                        pe.wait_ge(mla_copied, At(r - 1, l, 4).value)
                    for j in range(4):
                        for tok in range(TOK):
                            ins = turn(wide(b, 1024)[0:QK, j * SEQ + tok * P:j * SEQ + (tok + 1) * P],
                                       qk[:, tok, 4 * r + j, :])
                    ins.then_inc(mla_turned, 1)

                for c in range(LAYER_CHUNKS):
                    t = chunk_at(base, c)
                    u = c - 9
                    fill = fill_of(c)
                    fill_ready(fill, l)
                    if c == 0:
                        first_chunk(At(3, l, 1), base)
                        continue
                    if 16 <= c:
                        g = c - 16
                        if g == 0:
                            pe.wait_ge(bias_rest, At(1, l, 1).value)
                        for tok in range(TOK):
                            for n, b in enumerate((bias_hi, bias_lo)):
                                pe.matmul(pair(fill)[:, tok, :], sel_r[:, g * P:(g + 1) * P], b[:, :],
                                          start=n == 0, stop=False)
                    for q in range(4):
                        if 12 <= c <= 15:
                            dense_features(t + q, q, pair(fill))
                        else:
                            dense(t + q, (x_hi, x_lo), (2 * q, 2 * q + 1), 512,
                                  lambda tok, n0, n1: pair(fill)[:, tok, :], q == 0 and c < 16, q == 3)
                        if c == 2 and q == 1:
                            pe.wait_ge(lora_ready, At(1, l, 1).value)
                            z = norm[:, 0, :].rearrange("p (t n) -> p t n", t=TOK)
                            for f in range(3):
                                for tok in range(TOK):
                                    ins = turn(wide(4, 1024)[:, f * SEQ + tok * P:f * SEQ + (tok + 1) * P],
                                               z[:, tok, f * P:(f + 1) * P])
                            ins.then_inc(lora_turned, 1)
                        if 5 <= c <= 8 and q == 0:
                            turn_dil(c - 3)
                        if c == 8 and q == 1:
                            pe.wait_ge(mla_ready, At(1, l, 1).value)
                            turn_mla(0)
                            pe.wait_ge(dil_copied, At(6, l, 6).value)
                            turn_mla(1)
                        if c == 8 and q == 2:
                            turn_mla(2)
                            turn_mla(3)
                        if q == 0 and 0 <= u:
                            if u:
                                probs_read(At(UB + u, l, UNITS_LAYER))
                            else:
                                pe.wait_ge(mla_copied, At(4, l, 4).value)
                            scores(u, *unit_items(u))
                        if q == 1 and 1 <= u:
                            unit_values(u - 1)
                        if c == 14 and q == 2:
                            pe.wait_ge(max_ready, At(UB + u + 1, l, UNITS_LAYER).value)
                            turn_heads(At(3, l, 2))
                    if c == 14:
                        pe.wait_ge(heads_lo, At(6, l, 4).value)
                    if 0 <= u:
                        turn_probs(At(UB + u + 1, l, UNITS_LAYER), 8 if u < len(UNITS_MLA) else 6)
                    if c in (2, 3):
                        turn_dil(c - 2)
                    if c == 2:
                        pe.wait_ge(*freed(1, l))
                        for tok in range(TOK):
                            if tok:
                                pe.wait_ge(*freed(2, l))
                            for k in range(2):
                                if tok == 0:
                                    pe.wait_ge(lo_ready, (t + (5 + k)).value)
                                ins = rows_product(t + (4 + k), tok, (y2_hi[:, 4:, :], y2_lo[:, 4:, :]), (k,),
                                                   MLA_HEADS * QK,
                                                   lambda tok_, n0, n1: wide(2 * ((3 + tok_) % 2), 1024)[:, n0:n1],
                                                   k == 0, k == 1)
                                if tok:
                                    ins.then_inc(weights_used, 1)
                        pe.wait_ge(dil_copied, At(1, l, 6).value)
                        dense(t + 6, (y2_hi[:, 6:, :], y2_lo[:, 6:, :]), (0,), 1024,
                              lambda tok, n0, n1: wide(4 + 2 * tok, 1024)[:, n0:n1], True, True)

                def turn_merged(half):
                    pe.wait_ge(merged_ready, At(3 + half, l, 2).value)
                    out_ = second_half(fill_of(LAYER_CHUNKS) + 4) if half else wide(4, 1024)
                    for f in range(4):
                        for tok in range(TOK):
                            ins = turn(out_[:, f * SEQ + tok * P:f * SEQ + (tok + 1) * P],
                                       merged2[:, tok, (4 * half + f) * P:(4 * half + f + 1) * P])
                    ins.then_inc(merged_turned, 1)

                for m in range(3):
                    t = chunk_at(base, LAYER_CHUNKS + m)
                    u = LAYER_CHUNKS + m - 9
                    if u < UNITS_LAYER:
                        probs_read(At(UB + u, l, UNITS_LAYER))
                        scores(u, *unit_items(u))
                        unit_values(u - 1)
                    xs = ((y1_hi, y1_lo), (y1_hi[:, 4:, :], y1_lo[:, 4:, :]), (y2_hi, y2_lo))[m]
                    if m == 0:
                        pe.wait_ge(ya_lo, At(1, l, 1).value)
                    if m == 2:
                        turn_heads(At(4, l, 2))
                    for h in range(2):
                        fill = fill_of(LAYER_CHUNKS) + 2 * m + h
                        fill_ready(fill, l)
                        for q in range(2):
                            if m == 2 and h == 0:
                                pe.wait_ge(heads_lo, At(7 + q, l, 4).value)
                            dense(t + (2 * h + q), xs, (2 * q, 2 * q + 1), 512,
                                  lambda tok, n0, n1: pair(fill)[:, tok, :], q == 0, q == 1)
                            if m == 1 and h == 1 and q == 0:
                                unit_values(u)
                            if m == 2 and h == 1 and q == 0:
                                turn_merged(0)
                        if u < UNITS_LAYER and (m, h) in ((0, 1), (1, 0)):
                            turn_probs(At(UB + u + 1, l, UNITS_LAYER), 6)
                out_products(chunk_at(base, LAYER_CHUNKS + 3), lambda: turn_merged(1), At(4, l, 4))


def weight_tiles(named):
    tiles = []

    def chunk(w, c0, width=512, ks=2):
        part = w[:, c0:c0 + width]
        if part.shape[1] < width:
            part = np.concatenate([part, np.zeros((part.shape[0], width - part.shape[1]), np.float32)], 1)
        for k in range(0, w.shape[0], ks * P):
            tile = part[k:k + ks * P].reshape(ks, P, width).transpose(1, 0, 2).reshape(P, ks * width)
            if ks * width < TILE:
                tile = np.concatenate([tile, np.zeros((P, TILE - ks * width), np.float32)], 1)
            tiles.append(tile)

    def paired(w):
        for c, q in PAIRED:
            chunk(w[2 * q * P:2 * (q + 1) * P], 512 * c)

    def ffn(w_gu, w_down):
        def gate_up(i):
            a = i * FF_STEP
            chunk(np.concatenate([w_gu[:, a:a + FF_STEP], w_gu[:, D_FF + a:D_FF + a + FF_STEP]], 1), 0)

        def down(i):
            chunk(w_down[i * FF_STEP:(i + 1) * FF_STEP], 0, D, 1)

        gate_up(0)
        for i in range(1, FF_STEPS):
            gate_up(i)
            down(i - 1)
        down(FF_STEPS - 1)

    ffn(named["ffn1_w_gu"][0], named["ffn1_w_down"][0])
    w = named["w_in"][0]
    gate, xbr, q, kv, g_lru, g_attn = 0, 1024, 2048, 3072, 3584, 4608
    w_q = w[:, q:q + 1024].reshape(D, Q_HEADS, HEAD)[:, head_order()].reshape(D, 1024)
    chunk(w, kv)
    chunk(w_q, 0)
    chunk(w_q, 512)
    for at in (xbr, gate, g_lru, g_attn):
        chunk(w, at)
        chunk(w, at + 512)
    w_attn = named["w_proj_attn"][0].reshape(Q_HEADS, HEAD, D)[head_order()].reshape(1024, D)
    paired(named["w_proj_lru"][0])
    chunk(w_attn, 0)
    chunk(w_attn, 512)
    paired(named["w_out"][0])
    ffn(named["ffn2_w_gu"][0], named["ffn2_w_down"][0])
    for l in range(LAYERS):
        w = named["w_in_2"][l]
        a_b, a_c, a_x, a_z, low, b_z = 0, 512, 1024, 1536, 2048, 2464
        dq = 2976
        dk, dv, c_z, gates = dq + 1536, dq + 3072, dq + 4608, dq + 5120
        chunk(w[:, low:low + 416], 0)
        chunk(w, dq)
        chunk(w, dq + 512)
        chunk(named["w_uq_2"][l], 0, MLA_HEADS * QK, 1)
        chunk(named["w_ukv_2"][l], 0, 1024, 1)
        for at in [dq + 1024] + [dk + 512 * g for g in range(3)] + [dv + 512 * g for g in range(3)] + [
                b_z, c_z, a_c, a_x, a_b, a_z] + [gates + 512 * g for g in range(GATE_CHUNKS)]:
            chunk(w, at)
        for name in ("w_out_a_2", "w_out_b_2", "w_out_c_2"):
            chunk(named[name][l], 0)
            chunk(named[name][l], 512)
        paired(named["w_o_2"][l])
    assert len(tiles) == ALL_TILES, (len(tiles), ALL_TILES)
    return np.stack(tiles)


def head_order():
    return np.array([(2 * j + i) * (Q_HEADS // KV_HEADS) + g for j in range(2) for g in range(4) for i in range(2)])


def constants():
    c = np.zeros((P, N_CONST), np.float32)
    c[:, C_IDENT:C_IDENT + P] = np.eye(P)
    q, s = np.arange(P)[:, None], np.arange(SEQ)[None, :]
    back = P + q - s
    c[:, C_MASK1:C_MASK1 + SEQ] = np.where((back >= 0) & (back < P), 0.0, NEG)
    c[:, C_MASK2:C_MASK2 + SEQ] = np.where(back >= 0, 0.0, NEG)
    for g, dil in enumerate(DILATIONS):
        ok = (back >= 0) & (back % dil == 0) & (back <= dil * DIL_BACK)
        c[:, C_DIL + g * SEQ:C_DIL + (g + 1) * SEQ] = np.where(ok, back, BIG)
    for at, half in ((C_ROPE1, HALF), (C_ROPE2, ROPE2 // 2)):
        inv = np.float32(10000.0) ** (-np.arange(half, dtype=np.float32) / np.float32(half))
        ang = np.arange(SEQ, dtype=np.float32)[:, None] * inv[None, :]
        table = np.stack([np.cos(ang), np.sin(ang)]).astype(np.float32).reshape(2, TOK, P, half)
        c[:, at:at + 2 * TOK * half] = table.transpose(2, 0, 1, 3).reshape(P, -1)
    return c


def columns(v):
    return v.reshape(-1, P).T


def kernel(**inputs):
    import concourse.bacc as bacc
    from concourse.bass_utils import run_bass_kernel_spmd

    named = {k: np.asarray(v) for k, v in inputs.items()}
    params1 = np.concatenate(
        [columns(named[n][0]) for n in ("ffn1_pre_g", "mix_pre_g", "ffn2_pre_g")]
        + [columns(named["conv_w"][0, k]) for k in range(CONV1)]
        + [columns(named[n][0]) for n in ("conv_b", "lru_b_a", "lru_b_x", "lru_lambda")]
        + [np.broadcast_to(named["attn_sinks"][0][head_order()], (P, Q_HEADS))], 1)
    gains = np.stack([np.broadcast_to(named[n][0], (P, D)) for n in ("ffn1_post_g", "mix_post_g", "ffn2_post_g")])
    lru_w = np.zeros((P, 2, KD, P), np.float32)
    for a, name in enumerate(("lru_w_a", "lru_w_x")):
        w = named[name][0]
        for f in range(KD):
            for i in range(2):
                part = slice(HEAD * i, HEAD * (i + 1))
                lru_w[part, a, f, part] = w[2 * f + i]
    lru_w = lru_w.reshape(P, -1)
    layer_params = np.stack([np.concatenate(
        [columns(named["norm_g_2"][l])]
        + [columns(named["conv_w_2"][l, k]) for k in range(CONV2)]
        + [columns(named["conv_b_2"][l]), columns(named["q_a_norm_g_2"][l]), columns(named["kv_a_norm_g_2"][l])]
        + [columns(np.concatenate([named[n][l, g]] * 2)) for n in ("dil_q_norm_g_2", "dil_k_norm_g_2")
           for g in range(DIL_GROUPS)]
        + [np.broadcast_to(named[n][l], (P, QK)) for n in ("mla_q_norm_g_2", "mla_k_norm_g_2")], 1)
        for l in range(LAYERS)])
    layer_params = np.concatenate([layer_params, np.zeros_like(layer_params[:1])])
    gate_bias = named["b_gate_2"].reshape(LAYERS, GATE_CHUNKS, 512)
    selectors = np.zeros((GATE_CHUNKS, GATE_CHUNKS, P), np.float32)
    for g in range(GATE_CHUNKS):
        selectors[g, g] = 1.0
    arrays = {
        "x": named["x"].reshape(SEQ, D), "weights": weight_tiles(named), "consts": constants(),
        "params1": params1, "gains": gains, "lru_w": lru_w, "layer_params": layer_params,
        "gate_bias": gate_bias, "selectors": selectors.reshape(GATE_CHUNKS, -1),
    }
    arrays = {k: np.ascontiguousarray(v) for k, v in arrays.items()}
    nc = bacc.Bacc("TRN2", target_bir_lowering=False, num_devices=1)
    args = [nc.dram_tensor(k, v.shape, F32, kind="ExternalInput").ap() for k, v in arrays.items()]
    out = nc.dram_tensor("out", (SEQ, D), F32, kind="ExternalOutput").ap()
    block_program(nc, *args, out)
    result = run_bass_kernel_spmd(nc, [arrays], core_ids=[0])
    return result.results[0]["out"].reshape(1, SEQ, D)
```
